# Optimizing a Trainium2 kernel written in Bass

```python
import math
import jax, jax.numpy as jnp
from jax import lax
import numpy as np

D_MODEL = 1024
BATCH = 1
SEQ = 256
DEPTH = 2

HEAD_DIM = 64
N_HEADS = D_MODEL // HEAD_DIM
N_HEADS_A = N_HEADS // 4
N_HEADS_B = N_HEADS // 4
N_HEADS_C = N_HEADS - N_HEADS_A - N_HEADS_B
WIDTH_A = N_HEADS_A * HEAD_DIM
WIDTH_B = N_HEADS_B * HEAD_DIM
WIDTH_C = N_HEADS_C * HEAD_DIM
DIFF_DIM = HEAD_DIM // 2
ROPE_THETA = 500000.0
ROPE_FRACTION = 4
Q_BLOCK = 128
MOBA_BLOCK = 256
MOBA_TOPK = 3
MOBA_Q_CHUNK = 32
DILATED_PATTERNS = ((128, 1), (512, 4), (2048, 16))
SW_BLOCK = 128
D_FF = ((8 * D_MODEL // 3 + 255) // 256) * 256
CONV_WIDTH = 3
EPS = 1e-6
NEG_INF = -1e30


def rms_norm(x, g):
    xf = x.astype(jnp.float32)
    y = xf * lax.rsqrt(jnp.mean(xf * xf, axis=-1, keepdims=True) + EPS)
    return (y * g.astype(jnp.float32)).astype(x.dtype)

def partial_rope(x, positions):
    d = x.shape[-1]
    rot = d // ROPE_FRACTION
    half = rot // 2
    inv = jnp.power(jnp.float32(ROPE_THETA), -jnp.arange(half, dtype=jnp.float32) * 2.0 / rot)
    ang = positions.astype(jnp.float32)[..., None] * inv
    ang = ang.reshape((x.shape[0],) + (1,) * (x.ndim - 3) + ang.shape[1:])
    cos = jnp.cos(ang).astype(x.dtype)
    sin = jnp.sin(ang).astype(x.dtype)
    x1 = x[..., :half]
    x2 = x[..., half:rot]
    return jnp.concatenate([x1 * cos - x2 * sin, x2 * cos + x1 * sin, x[..., rot:]], axis=-1)

def to_heads(t, h):
    b, s, _ = t.shape
    return t.reshape(b, s, h, -1).transpose(0, 2, 1, 3)

def from_heads(t):
    b, h, s, d = t.shape
    return t.transpose(0, 2, 1, 3).reshape(b, s, h * d)

def differential_attention(q, k, v, positions, lam, g_head, lam_init):
    b, s, _ = q.shape
    h = N_HEADS_A
    q = partial_rope(q.reshape(b, s, h, 2, DIFF_DIM).transpose(0, 2, 3, 1, 4), positions)
    k = partial_rope(k.reshape(b, s, h, 2, DIFF_DIM).transpose(0, 2, 3, 1, 4), positions)
    vf = to_heads(v, h).astype(jnp.float32)
    nq = s // Q_BLOCK
    qb = q.reshape(b, h, 2, nq, Q_BLOCK, DIFF_DIM).transpose(3, 0, 1, 2, 4, 5)
    key_pos = jnp.arange(s)
    scale = DIFF_DIM ** -0.5

    def block(args):
        qi, i = args
        sc = jnp.einsum('bhcqd,bhckd->bhcqk', qi, k).astype(jnp.float32) * scale
        q_pos = i * Q_BLOCK + jnp.arange(Q_BLOCK)
        sc = jnp.where(key_pos[None, :] <= q_pos[:, None], sc, NEG_INF)
        p = jax.nn.softmax(sc, axis=-1)
        a = p[:, :, 0] - lam * p[:, :, 1]
        return jnp.einsum('bhqk,bhkd->bhqd', a, vf)

    o = lax.map(block, (qb, jnp.arange(nq)))
    o = o.transpose(1, 2, 0, 3, 4).reshape(b, h, s, HEAD_DIM)
    o = rms_norm(o, g_head) * (1.0 - lam_init)
    return from_heads(o)

def moba_attention(q, k, v, positions):
    b, s, _ = q.shape
    h = N_HEADS_B
    q = partial_rope(to_heads(q, h), positions)
    k = partial_rope(to_heads(k, h), positions)
    v = to_heads(v, h)
    nb = -(-s // MOBA_BLOCK)
    sp = nb * MOBA_BLOCK
    pad = ((0, 0), (0, 0), (0, sp - s), (0, 0))
    q, k, v = jnp.pad(q, pad), jnp.pad(k, pad), jnp.pad(v, pad)
    n_sel = max(1, min(MOBA_TOPK, nb - 1))
    kb = k.reshape(b, h, nb, MOBA_BLOCK, HEAD_DIM)
    vb = v.reshape(b, h, nb, MOBA_BLOCK, HEAD_DIM)
    k_mean = jnp.mean(kb.astype(jnp.float32), axis=3)
    gate = jnp.einsum('bhsd,bhnd->bhsn', q.astype(jnp.float32), k_mean)
    q_blk = jnp.arange(sp) // MOBA_BLOCK
    gate = jnp.where(jnp.arange(nb)[None, :] < q_blk[:, None], gate, NEG_INF)
    _, sel = lax.top_k(gate, n_sel)
    valid = jnp.arange(n_sel)[None, :] < q_blk[:, None]
    c = MOBA_Q_CHUNK
    nc = sp // c
    qc = q.reshape(b, h, nc, c, HEAD_DIM).transpose(2, 0, 1, 3, 4)
    selc = sel.reshape(b, h, nc, c, n_sel).transpose(2, 0, 1, 3, 4)
    validc = valid.reshape(nc, c, n_sel)
    b_idx = jnp.arange(b)[:, None, None, None]
    h_idx = jnp.arange(h)[None, :, None, None]
    scale = HEAD_DIM ** -0.5

    def chunk(args):
        qi, si, vi, ci = args
        kg = kb[b_idx, h_idx, si]
        vg = vb[b_idx, h_idx, si].astype(jnp.float32)
        q_pos = ci * c + jnp.arange(c)
        start = (ci * c) // MOBA_BLOCK * MOBA_BLOCK
        k_own = lax.dynamic_slice_in_dim(k, start, MOBA_BLOCK, axis=2)
        v_own = lax.dynamic_slice_in_dim(v, start, MOBA_BLOCK, axis=2).astype(jnp.float32)
        s_sel = jnp.einsum('bhqd,bhqnkd->bhqnk', qi, kg).astype(jnp.float32) * scale
        s_sel = jnp.where(vi[None, None, :, :, None], s_sel, NEG_INF).reshape(b, h, c, n_sel * MOBA_BLOCK)
        s_own = jnp.einsum('bhqd,bhkd->bhqk', qi, k_own).astype(jnp.float32) * scale
        k_pos = start + jnp.arange(MOBA_BLOCK)
        s_own = jnp.where(k_pos[None, :] <= q_pos[:, None], s_own, NEG_INF)
        p = jax.nn.softmax(jnp.concatenate([s_sel, s_own], axis=-1), axis=-1)
        p_sel = p[..., :n_sel * MOBA_BLOCK].reshape(b, h, c, n_sel, MOBA_BLOCK)
        p_own = p[..., n_sel * MOBA_BLOCK:]
        return (jnp.einsum('bhqnk,bhqnkd->bhqd', p_sel, vg)
                + jnp.einsum('bhqk,bhkd->bhqd', p_own, v_own))

    o = lax.map(chunk, (qc, selc, validc, jnp.arange(nc)))
    o = o.transpose(1, 2, 0, 3, 4).reshape(b, h, sp, HEAD_DIM)[:, :, :s]
    return from_heads(o)

def dilated_branch(q, k, v, window, dil):
    b, h, s, d = q.shape
    span = dil * SW_BLOCK
    sp = -(-s // span) * span
    m_len = sp // dil
    nb = m_len // SW_BLOCK
    w_sub = window // dil

    def sub(t):
        t = jnp.pad(t, ((0, 0), (0, 0), (0, sp - s), (0, 0)))
        return t.reshape(b, h, m_len, dil, d).transpose(0, 1, 3, 2, 4).reshape(b, h, dil, nb, SW_BLOCK, d)

    def band(t):
        prev = jnp.pad(t, ((0, 0), (0, 0), (0, 0), (1, 0), (0, 0), (0, 0)))[:, :, :, :-1]
        return jnp.concatenate([prev, t], axis=4)

    qs = sub(q)
    kw = band(sub(k))
    vw = band(sub(v)).astype(jnp.float32)
    sc = jnp.einsum('bhrnqd,bhrnkd->bhrnqk', qs, kw).astype(jnp.float32) * (d ** -0.5)
    qi = jnp.arange(SW_BLOCK)[:, None]
    kj = jnp.arange(2 * SW_BLOCK)[None, :] - SW_BLOCK
    dist = qi - kj
    blk = jnp.arange(nb)[:, None, None]
    mask = (dist >= 0) & (dist <= w_sub) & (blk * SW_BLOCK + kj >= 0)
    sc = jnp.where(mask, sc, NEG_INF)
    mx = jnp.max(sc, axis=-1, keepdims=True)
    e = jnp.exp(sc - mx)
    den = jnp.sum(e, axis=-1)
    o = jnp.einsum('bhrnqk,bhrnkd->bhrnqd', e, vw) / den[..., None]
    lse = mx[..., 0] + jnp.log(den)
    o = o.reshape(b, h, dil, m_len, d).transpose(0, 1, 3, 2, 4).reshape(b, h, sp, d)[:, :, :s]
    lse = lse.reshape(b, h, dil, m_len).transpose(0, 1, 3, 2).reshape(b, h, sp)[:, :, :s]
    return o, lse

def dilated_attention(q, k, v, positions):
    h = N_HEADS_C
    q = partial_rope(to_heads(q, h), positions)
    k = partial_rope(to_heads(k, h), positions)
    v = to_heads(v, h)
    outs, lses = [], []
    for window, dil in DILATED_PATTERNS:
        o, lse = dilated_branch(q, k, v, window, dil)
        outs.append(o)
        lses.append(lse)
    wts = jax.nn.softmax(jnp.stack(lses, axis=0), axis=0)
    o = jnp.sum(wts[..., None] * jnp.stack(outs, axis=0), axis=0)
    return from_heads(o)

def conv_gated_mlp(h, w_up, conv_w, conv_b, w_down):
    u = h @ w_up
    u = lax.conv_general_dilated(u, conv_w[:, None, :].astype(u.dtype), window_strides=(1,),
                                 padding=[(CONV_WIDTH - 1, 0)],
                                 dimension_numbers=('NWC', 'WIO', 'NWC'),
                                 feature_group_count=u.shape[-1]) + conv_b
    gate, val = jnp.split(u, 2, axis=-1)
    return (jax.nn.silu(gate) * val) @ w_down

def first_inputs(seed: int = 0) -> dict:
    key = jax.random.key(seed)
    ks = jax.random.split(key, 16)
    nrm = jax.random.normal
    return {
        'x': nrm(ks[0], (BATCH, SEQ, D_MODEL), jnp.float32),
        'positions': jnp.broadcast_to(jnp.arange(SEQ, dtype=jnp.int32)[None, :], (BATCH, SEQ)),
        'g_mix': 1.0 + 0.02 * nrm(ks[1], (DEPTH, D_MODEL), jnp.float32),
        'w_in': nrm(ks[2], (DEPTH, D_MODEL, 3 * D_MODEL), jnp.float32) * D_MODEL ** -0.5,
        'w_out': nrm(ks[3], (DEPTH, D_MODEL, D_MODEL), jnp.float32) * D_MODEL ** -0.5,
        'lambda_q1': 0.1 * nrm(ks[4], (DEPTH, DIFF_DIM), jnp.float32),
        'lambda_k1': 0.1 * nrm(ks[5], (DEPTH, DIFF_DIM), jnp.float32),
        'lambda_q2': 0.1 * nrm(ks[6], (DEPTH, DIFF_DIM), jnp.float32),
        'lambda_k2': 0.1 * nrm(ks[7], (DEPTH, DIFF_DIM), jnp.float32),
        'g_diff': 1.0 + 0.02 * nrm(ks[8], (DEPTH, HEAD_DIM), jnp.float32),
        'g_ffn': 1.0 + 0.02 * nrm(ks[9], (DEPTH, D_MODEL), jnp.float32),
        'w_up': nrm(ks[10], (DEPTH, D_MODEL, 2 * D_FF), jnp.float32) * D_MODEL ** -0.5,
        'conv_w': nrm(ks[11], (DEPTH, CONV_WIDTH, 2 * D_FF), jnp.float32) * CONV_WIDTH ** -0.5,
        'conv_b': 0.01 * nrm(ks[12], (DEPTH, 2 * D_FF), jnp.float32),
        'w_down': nrm(ks[13], (DEPTH, D_FF, D_MODEL), jnp.float32) * D_FF ** -0.5,
        'g_final': 1.0 + 0.02 * nrm(ks[14], (D_MODEL,), jnp.float32),
    }

def first_block(x, positions, g_mix, w_in, w_out, lambda_q1, lambda_k1, lambda_q2, lambda_k2,
              g_diff, g_ffn, w_up, conv_w, conv_b, w_down, g_final):
    widths = [WIDTH_A] * 3 + [WIDTH_B] * 3 + [WIDTH_C] * 3
    cuts = []
    acc = 0
    for wd in widths[:-1]:
        acc += wd
        cuts.append(acc)
    for layer in range(DEPTH):
        h = rms_norm(x, g_mix[layer])
        qkv = h @ w_in[layer]
        qa, ka, va, qb, kb, vb, qc, kc, vc = jnp.split(qkv, cuts, axis=-1)
        lam_init = 0.8 - 0.6 * math.exp(-0.3 * layer)
        lam = (jnp.exp(jnp.sum(lambda_q1[layer].astype(jnp.float32) * lambda_k1[layer].astype(jnp.float32)))
               - jnp.exp(jnp.sum(lambda_q2[layer].astype(jnp.float32) * lambda_k2[layer].astype(jnp.float32)))
               + lam_init)
        o_a = differential_attention(qa, ka, va, positions, lam, g_diff[layer], lam_init).astype(x.dtype)
        o_b = moba_attention(qb, kb, vb, positions).astype(x.dtype)
        o_c = dilated_attention(qc, kc, vc, positions).astype(x.dtype)
        mix = jnp.concatenate([o_a, o_b, o_c], axis=-1)
        x = x + mix @ w_out[layer]
        h2 = rms_norm(x, g_ffn[layer])
        x = x + conv_gated_mlp(h2, w_up[layer], conv_w[layer], conv_b[layer], w_down[layer]).astype(x.dtype)
    return rms_norm(x, g_final)


DEPTH_2 = 1

SSM_WIDTH = D_MODEL // 2
SSM_GROUP = 16
SSM_GROUPS = SSM_WIDTH // SSM_GROUP
SSM_STATE = 64
DT_MIN = 1e-3
DT_MAX = 1e-1
ATTN_HEADS = 8
ATTN_KV_HEADS = 2
ATTN_WIDTH = ATTN_HEADS * HEAD_DIM
IDX_HEADS = 8
IDX_DIM = 32
TOPK_MAX = 256
ROPE_THETA_2 = 10000.0
NEG_BIG = -1e30
PEER_HEADS = 8
PEER_KEYS = 128
PEER_EXPERTS = PEER_KEYS * PEER_KEYS
PEER_KEY_DIM = 128
PEER_TOPK = 16
PEER_CHUNK = 128
NORM_EPS = 1e-6

IN_SPLITS = (SSM_WIDTH, ATTN_WIDTH, ATTN_KV_HEADS * HEAD_DIM, ATTN_KV_HEADS * HEAD_DIM,
             IDX_HEADS * IDX_DIM, IDX_DIM, IDX_HEADS, D_MODEL, D_MODEL)
IN_WIDTH = sum(IN_SPLITS)


def rmsnorm(x, g):
    xf = x.astype(jnp.float32)
    y = xf * lax.rsqrt(jnp.mean(xf * xf, axis=-1, keepdims=True) + NORM_EPS)
    return (y * g.astype(jnp.float32)).astype(x.dtype)

def rope_tables(seq, dim):
    pos = jnp.arange(seq, dtype=jnp.float32)
    inv = ROPE_THETA_2 ** (-jnp.arange(0, dim, 2, dtype=jnp.float32) / dim)
    ang = pos[:, None] * inv[None, :]
    return jnp.cos(ang), jnp.sin(ang)

def apply_rope(x, cos, sin):
    half = x.shape[-1] // 2
    shape = (cos.shape[0],) + (1,) * (x.ndim - 3) + (half,)
    c = cos.reshape(shape)
    s = sin.reshape(shape)
    xf = x.astype(jnp.float32)
    x1, x2 = xf[..., :half], xf[..., half:]
    return jnp.concatenate([x1 * c - x2 * s, x2 * c + x1 * s], axis=-1).astype(x.dtype)

def s5_branch(u, a_re, a_im, log_dt, b_re, b_im, c_re, c_im, d_skip, w_glu):
    bsz, seq, _ = u.shape
    f32 = jnp.float32
    uf = u.astype(f32).reshape(bsz, seq, SSM_GROUPS, SSM_GROUP)
    lam = lax.complex(a_re.astype(f32), a_im.astype(f32))
    dt = jnp.exp(log_dt.astype(f32))[:, None]
    a_bar = jnp.exp(lam * dt)
    b = lax.complex(b_re.astype(f32), b_im.astype(f32))
    b_bar = ((a_bar - 1.0) / lam)[..., None] * b
    bu = jnp.einsum('gpc,bsgc->bsgp', b_bar, uf)
    a_seq = jnp.broadcast_to(a_bar, bu.shape)

    def combine(left, right):
        a1, s1 = left
        a2, s2 = right
        return a2 * a1, a2 * s1 + s2

    _, states = lax.associative_scan(combine, (a_seq, bu), axis=1)
    c = lax.complex(c_re.astype(f32), c_im.astype(f32))
    y = jnp.real(jnp.einsum('gcp,bsgp->bsgc', c, states))
    y = y + d_skip.astype(f32).reshape(SSM_GROUPS, SSM_GROUP) * uf
    y = jax.nn.gelu(y.reshape(bsz, seq, SSM_WIDTH))
    y = y * jax.nn.sigmoid(y @ w_glu.astype(f32))
    return y.astype(u.dtype)

def dsa_branch(q, k, v, qi, ki, wi):
    bsz, seq = q.shape[0], q.shape[1]
    topk = min(TOPK_MAX, seq // 4)
    nb = seq // Q_BLOCK
    grp = ATTN_HEADS // ATTN_KV_HEADS
    f32 = jnp.float32
    kf = ki.astype(f32)
    idx_scale = (IDX_HEADS ** -0.5) * (IDX_DIM ** -0.5)
    s_pos = jnp.arange(seq)

    def to_blocks(t):
        return t.reshape((bsz, nb, Q_BLOCK) + t.shape[2:]).swapaxes(0, 1)

    def one_block(args):
        qb, qib, wib, blk = args
        t_pos = blk * Q_BLOCK + jnp.arange(Q_BLOCK)
        rel = jax.nn.relu(jnp.einsum('bthd,bsd->bths', qib.astype(f32), kf))
        score = jnp.einsum('bths,bth->bts', rel, wib.astype(f32)) * idx_scale
        causal = s_pos[None, :] <= t_pos[:, None]
        score = jnp.where(causal[None], score, NEG_BIG)
        _, sel = lax.top_k(score, topk)
        valid = sel <= t_pos[None, :, None]
        kg = jax.vmap(lambda kk, ii: kk[ii])(k, sel)
        vg = jax.vmap(lambda vv, ii: vv[ii])(v, sel)
        qg = qb.reshape(bsz, Q_BLOCK, ATTN_KV_HEADS, grp, HEAD_DIM).astype(f32)
        logits = jnp.einsum('btngd,btknd->btngk', qg, kg.astype(f32)) * (HEAD_DIM ** -0.5)
        logits = jnp.where(valid[:, :, None, None, :], logits, NEG_BIG)
        p = jax.nn.softmax(logits, axis=-1)
        o = jnp.einsum('btngk,btknd->btngd', p, vg.astype(f32))
        return o.reshape(bsz, Q_BLOCK, ATTN_WIDTH).astype(qb.dtype)

    out = lax.map(one_block, (to_blocks(q), to_blocks(qi), to_blocks(wi), jnp.arange(nb)))
    return out.swapaxes(0, 1).reshape(bsz, seq, ATTN_WIDTH)

def peer_ffn(x, w_q, sub_k1, sub_k2, u_tab, v_tab):
    bsz, seq, d = x.shape
    f32 = jnp.float32
    q = (x @ w_q).astype(f32).reshape(bsz, seq, PEER_HEADS, 2, PEER_KEY_DIM)
    s1 = jnp.einsum('bshd,hnd->bshn', q[..., 0, :], sub_k1.astype(f32))
    s2 = jnp.einsum('bshd,hnd->bshn', q[..., 1, :], sub_k2.astype(f32))
    v1, i1 = lax.top_k(s1, PEER_TOPK)
    v2, i2 = lax.top_k(s2, PEER_TOPK)
    cand_s = (v1[..., :, None] + v2[..., None, :]).reshape(bsz, seq, PEER_HEADS, PEER_TOPK * PEER_TOPK)
    cand_i = (i1[..., :, None] * PEER_KEYS + i2[..., None, :]).reshape(bsz, seq, PEER_HEADS, PEER_TOPK * PEER_TOPK)
    top_s, pos = lax.top_k(cand_s, PEER_TOPK)
    experts = jnp.take_along_axis(cand_i, pos, axis=-1)
    gates = jax.nn.softmax(top_s, axis=-1)
    n_tok = bsz * seq
    n_chunks = n_tok // PEER_CHUNK
    n_sel = PEER_HEADS * PEER_TOPK
    xc_all = x.reshape(n_chunks, PEER_CHUNK, d)
    ec_all = experts.reshape(n_chunks, PEER_CHUNK, n_sel)
    gc_all = gates.reshape(n_chunks, PEER_CHUNK, n_sel)

    def chunk(args):
        xc, ec, gc = args
        u = u_tab[ec].astype(f32)
        act = jax.nn.gelu(jnp.einsum('ced,cd->ce', u, xc.astype(f32))) * gc
        return jnp.einsum('ce,ced->cd', act, v_tab[ec].astype(f32)).astype(x.dtype)

    out = lax.map(chunk, (xc_all, ec_all, gc_all))
    return out.reshape(bsz, seq, d)

def second_inputs(seed: int = 0) -> dict:
    key = jax.random.key(seed)
    ks = jax.random.split(key, 24)
    f32 = jnp.float32
    L, D, G, P, N = DEPTH_2, D_MODEL, SSM_GROUPS, SSM_STATE, SSM_GROUP
    nrm = lambda k, shape, s: jax.random.normal(k, shape, f32) * s
    x = jax.random.normal(ks[0], (BATCH, SEQ, D), f32)
    norm1_g = 1.0 + nrm(ks[1], (L, D), 0.02)
    w_in = nrm(ks[2], (L, D, IN_WIDTH), D ** -0.5)
    a_re = -0.5 * (1.0 + nrm(ks[3], (L, G, P), 0.01))
    a_im = jnp.broadcast_to(math.pi * jnp.arange(P, dtype=f32), (L, G, P)) + nrm(ks[4], (L, G, P), 0.01)
    log_dt = jax.random.uniform(ks[5], (L, G), f32, math.log(DT_MIN), math.log(DT_MAX))
    b_re = nrm(ks[6], (L, G, P, N), (2.0 * N) ** -0.5)
    b_im = nrm(ks[7], (L, G, P, N), (2.0 * N) ** -0.5)
    c_re = nrm(ks[8], (L, G, N, P), P ** -0.5)
    c_im = nrm(ks[9], (L, G, N, P), P ** -0.5)
    d_skip = nrm(ks[10], (L, SSM_WIDTH), 1.0)
    w_glu = nrm(ks[11], (L, SSM_WIDTH, SSM_WIDTH), SSM_WIDTH ** -0.5)
    w_ssm_up = nrm(ks[12], (L, SSM_WIDTH, D), SSM_WIDTH ** -0.5)
    w_attn_up = nrm(ks[13], (L, ATTN_WIDTH, D), ATTN_WIDTH ** -0.5)
    w_out = nrm(ks[14], (L, D, D), D ** -0.5)
    norm2_g = 1.0 + nrm(ks[15], (L, D), 0.02)
    peer_wq = nrm(ks[16], (L, D, PEER_HEADS * 2 * PEER_KEY_DIM), D ** -0.5)
    peer_k1 = nrm(ks[17], (L, PEER_HEADS, PEER_KEYS, PEER_KEY_DIM), PEER_KEY_DIM ** -0.5)
    peer_k2 = nrm(ks[18], (L, PEER_HEADS, PEER_KEYS, PEER_KEY_DIM), PEER_KEY_DIM ** -0.5)
    peer_u = nrm(ks[19], (L, PEER_EXPERTS, D), D ** -0.5)
    peer_v = nrm(ks[20], (L, PEER_EXPERTS, D), PEER_HEADS ** -0.5)
    norm_f_g = 1.0 + nrm(ks[21], (D,), 0.02)
    return {"x": x, "norm1_g": norm1_g, "w_in": w_in, "a_re": a_re, "a_im": a_im,
            "log_dt": log_dt, "b_re": b_re, "b_im": b_im, "c_re": c_re, "c_im": c_im,
            "d_skip": d_skip, "w_glu": w_glu, "w_ssm_up": w_ssm_up, "w_attn_up": w_attn_up,
            "w_out": w_out, "norm2_g": norm2_g, "peer_wq": peer_wq, "peer_k1": peer_k1,
            "peer_k2": peer_k2, "peer_u": peer_u, "peer_v": peer_v, "norm_f_g": norm_f_g}

def second_block(x, norm1_g, w_in, a_re, a_im, log_dt, b_re, b_im, c_re, c_im, d_skip, w_glu,
              w_ssm_up, w_attn_up, w_out, norm2_g, peer_wq, peer_k1, peer_k2, peer_u, peer_v,
              norm_f_g):
    bsz, seq, _ = x.shape
    cos_a, sin_a = rope_tables(seq, HEAD_DIM)
    cos_i, sin_i = rope_tables(seq, IDX_DIM)
    offsets = np.cumsum(IN_SPLITS)[:-1].tolist()
    h = x
    for layer in range(DEPTH_2):
        xn = rmsnorm(h, norm1_g[layer])
        proj = xn @ w_in[layer]
        u, q, k, v, qi, ki, wi, g_ssm, g_attn = jnp.split(proj, offsets, axis=-1)
        y_ssm = s5_branch(u, a_re[layer], a_im[layer], log_dt[layer], b_re[layer], b_im[layer],
                          c_re[layer], c_im[layer], d_skip[layer], w_glu[layer])
        q = apply_rope(q.reshape(bsz, seq, ATTN_HEADS, HEAD_DIM), cos_a, sin_a)
        k = apply_rope(k.reshape(bsz, seq, ATTN_KV_HEADS, HEAD_DIM), cos_a, sin_a)
        v = v.reshape(bsz, seq, ATTN_KV_HEADS, HEAD_DIM)
        qi = apply_rope(qi.reshape(bsz, seq, IDX_HEADS, IDX_DIM), cos_i, sin_i)
        ki = apply_rope(ki, cos_i, sin_i)
        y_attn = dsa_branch(q, k, v, qi, ki, wi)
        merged = (jax.nn.sigmoid(g_ssm) * (y_ssm @ w_ssm_up[layer])
                  + jax.nn.sigmoid(g_attn) * (y_attn @ w_attn_up[layer]))
        h = h + merged @ w_out[layer]
        hn = rmsnorm(h, norm2_g[layer])
        h = h + peer_ffn(hn, peer_wq[layer], peer_k1[layer], peer_k2[layer], peer_u[layer], peer_v[layer])
    return rmsnorm(h, norm_f_g)


def setup_inputs(seed=0):
    out = dict(first_inputs(seed))
    for name, value in second_inputs(seed + 1).items():
        if name != "x":
            out[name + "_2"] = value
    return out


def reference(
    x, positions, g_mix, w_in, w_out, lambda_q1, lambda_k1, lambda_q2, lambda_k2, g_diff, g_ffn,
    w_up, conv_w, conv_b, w_down, g_final, norm1_g_2, w_in_2, a_re_2, a_im_2, log_dt_2, b_re_2,
    b_im_2, c_re_2, c_im_2, d_skip_2, w_glu_2, w_ssm_up_2, w_attn_up_2, w_out_2, norm2_g_2,
    peer_wq_2, peer_k1_2, peer_k2_2, peer_u_2, peer_v_2, norm_f_g_2,
):
    x = first_block(
        x, positions, g_mix, w_in, w_out, lambda_q1, lambda_k1, lambda_q2, lambda_k2, g_diff,
        g_ffn, w_up, conv_w, conv_b, w_down, g_final,
    )
    return second_block(
        x, norm1_g_2, w_in_2, a_re_2, a_im_2, log_dt_2, b_re_2, b_im_2, c_re_2, c_im_2,
        d_skip_2, w_glu_2, w_ssm_up_2, w_attn_up_2, w_out_2, norm2_g_2, peer_wq_2, peer_k1_2,
        peer_k2_2, peer_u_2, peer_v_2, norm_f_g_2,
    )


_drawn_inputs = setup_inputs


def setup_inputs(seed=0):
    import zlib

    import numpy as np

    out = dict(_drawn_inputs(seed))
    spreads = {}
    factors = {'a_re_2': 200.0,
     'norm_f_g_2': 22.961,
     'a_im_2': 32.4,
     'log_dt_2': 34.992,
     'b_re_2': 35.432,
     'b_im_2': 35.992,
     'c_re_2': 38.952,
     'c_im_2': 38.976}
    for name, (base, spread) in spreads.items():
        noise = np.random.default_rng([zlib.crc32(name.encode()), seed]).standard_normal(out[name].shape)
        drawn = base * np.exp(spread * noise) if base else spread * noise
        out[name] = __import__('jax').numpy.asarray(drawn.astype(out[name].dtype))
    for name, factor in factors.items():
        out[name] = (out[name] * factor).astype(out[name].dtype)
    return out
```

```python
import math
from contextlib import ExitStack

import numpy as np
import concourse.bass as bass
from concourse import mybir

F32 = mybir.dt.float32
I32 = mybir.dt.int32
U32 = mybir.dt.uint32
ALU = mybir.AluOpType
ACTF = mybir.ActivationFunctionType
AX = mybir.AxisListType.X

EPS = 1e-6
NEG = -1e30
TAKEN = -3e38
MAGIC = 12582912.0
TWO_PI = 6.283185307179586
C1 = 6.28125
C2 = float(np.float32(TWO_PI - C1))
C3 = TWO_PI - C1 - C2
SIN_SCALE = 6.283185
DEPTH = 2
NTILE = 22
LAM_INIT = [0.8 - 0.6 * math.exp(-0.3 * layer) for layer in range(DEPTH)]

K_ID, K_IOTA, K_MC, K_MD, K_CA, K_SA, K_CI, K_SI, K_INV, K_T = 0, 128, 256, 768, 1280, 1344, 1408, 1440, 1472, 1484
K_W = K_T + 256
S_G = 0
S_CONV = 48
S_LAM = S_CONV + 2 * 176
S_GD = S_LAM + 256
S_DSK = S_GD + 128
S_LDT = S_DSK + 4
S_ARE = S_LDT + 16
S_AIM = S_ARE + 16
S_W = S_AIM + 16


class Op:

    def __init__(self, eng, fn, after, sem=None, inc=1):
        self.eng, self.fn, self.after, self.sem, self.inc = eng, fn, after, sem, inc
        self.val, self.need = 0, sem is not None


def flat(xs):
    out = []
    for x in xs:
        if isinstance(x, (list, tuple)):
            out += flat(x)
        elif x is not None:
            out.append(x)
    return out


class Queues:

    def __init__(self):
        self.ops = {e: [] for e in ("pe", "act", "dve", "pool", "sp")}
        self.dma_count = {}

    def put(self, eng, fn, after):
        op = Op(eng, fn, flat(after))
        for a in op.after:
            a.need = True
        self.ops[eng].append(op)
        return op

    def dma(self, eng, out, in_, sem, after):
        op = Op(eng, lambda e: e.dma_start(out, in_), flat(after), sem, 16)
        for a in op.after:
            a.need = True
        self.dma_count[sem.name] = self.dma_count.get(sem.name, 0) + 16
        op.val = self.dma_count[sem.name]
        self.ops[eng].append(op)
        return op

    def number(self, sems):
        for name, ops in self.ops.items():
            n = 0
            for op in ops:
                if op.sem is None and op.need:
                    n += 1
                    op.sem, op.val = sems[name], n

    def emit(self, name, eng):
        seen = {}
        for op in self.ops[name]:
            for a in op.after:
                if seen.get(a.sem.name, 0) < a.val:
                    eng.wait_ge(a.sem, a.val)
                    seen[a.sem.name] = a.val
            ins = op.fn(eng)
            if op.need:
                ins.then_inc(op.sem, op.inc)


def program(nc, x_d, pos_d, consts_d, smalls_d, win_d, wout_d, wup_d, wdown_d, rows_d, win2_d, wqk_d, wsm_d,
            wglu_d, wsu_d, wau_d, wout2_d, wpq_d, keys_d, ut_d, vt_d, out_d):
    with ExitStack() as ctx:
        def sb(name, n, dt=F32):
            return ctx.enter_context(nc.sbuf_tensor(name, [128, n], dt))

        arena = sb("arena", 32768)
        ring = sb("ring", 3 * 4096)
        xs = sb("xs", 2048)
        hTs = sb("hTs", 2048)
        ids = sb("ids", 128)
        ext = sb("ext", 3840)
        banks = [ctx.enter_context(nc.psum_tensor(f"bank{i}", [128, 512], F32)) for i in range(8)]
        sems = {e: ctx.enter_context(nc.semaphore(f"s_{e}")) for e in ("pe", "act", "dve", "pool", "sp")}
        slot_sem = [ctx.enter_context(nc.semaphore(f"s_slot{i}")) for i in range(4)]
        s_x, s_pos, s_id, s_k, s_sm, s_ssm, s_out = [
            ctx.enter_context(nc.semaphore(n)) for n in ("s_x", "s_pos", "s_id", "s_k", "s_sm", "s_ssm", "s_out")]

        q = Queues()

        def PE(fn, *after):
            return q.put("pe", fn, after)

        def ACT(fn, *after):
            return q.put("act", fn, after)

        def DVE(fn, *after):
            return q.put("dve", fn, after + tuple(q.ops["dve"][-1:]))

        def POOL(fn, *after):
            return q.put("pool", fn, after + tuple(q.ops["pool"][-1:]))

        def A(off, n):
            return arena[:, off:off + n]

        def tt(E, out, a, b, op, *after):
            return E(lambda e: e.tensor_tensor(out, a, b, op), *after)

        def ts(E, out, a, s1, s2, op0, op1, *after):
            if op1 is None:
                return E(lambda e: e.tensor_scalar(out, a, s1, None, op0), *after)
            return E(lambda e: e.tensor_scalar(out, a, s1, s2, op0, op1), *after)

        def stt(out, a, s, b, op0, op1, *after):
            return DVE(lambda e: e.scalar_tensor_tensor(out, a, s, b, op0, op1), *after)

        def act(out, a, f, *after, **kw):
            return ACT(lambda e: e.activation(out, a, f, **kw), *after)

        def copy(i, out, a, *after):
            if i % 2:
                return ACT(lambda e: e.activation(out, a, ACTF.Copy), *after)
            return DVE(lambda e: e.tensor_copy(out, a), *after)

        def mm(out, pairs, *after):
            t = None
            for i, (l, r) in enumerate(pairs):
                t = PE(lambda e, l=l, r=r, i=i: e.matmul(out, l, r, start=i == 0, stop=i == len(pairs) - 1),
                       *(after if i == 0 else ()))
            return t

        def tr(out, a, *after):
            return PE(lambda e: e.transpose(out, a, ids[:, :]), *after)

        free = [[] for _ in range(8)]
        turn = [0]

        def bank(of=range(8)):
            of = list(of)
            turn[0] += 1
            return of[turn[0] % len(of)]

        slots = [ring[:, i * 4096:(i + 1) * 4096] for i in range(3)] + [A(0, 4096)]
        slot_free = [[] for _ in slots]
        use = {"n": 4, "i": 0}

        def load(src, n=4096):
            i = use["i"] % use["n"]
            use["i"] = i + 1
            dst = slots[i][:, 0:n]
            t = q.dma("sp", dst, src, slot_sem[i], [slot_free[i]])
            return i, dst, t

        x = xs[:, :].rearrange("p (t d) -> p t d", t=2)
        hT = hTs[:, :].rearrange("p (k t) -> p k t", k=8)
        cosT = A(4096, 4096).rearrange("p (n t) -> p n t", n=16)
        sinT = A(8192, 4096).rearrange("p (n t) -> p n t", n=16)
        QKV, QKT, MIX, CON = 12288, 18432, 22528, 24576
        SML = CON + K_W - 128
        ATT = 27136
        TMP = 30208
        STA = 32256
        assert SML + S_W <= ATT
        qkv = A(QKV, 6144).rearrange("p (t n) -> p t n", t=2)
        yT = A(QKV, NTILE * 256).rearrange("p (k t) -> p k t", k=NTILE)
        qkT = A(QKT, 4096).rearrange("p (k t) -> p k t", k=16)
        mix = A(MIX, 2048).rearrange("p (t d) -> p t d", t=2)
        sta_at = [STA]

        def stat(n):
            o = sta_at[0]
            sta_at[0] += n
            assert sta_at[0] <= 32768
            return A(o, n)

        def con(c, n):
            return A(CON + c - 128, n)

        def sml(c, n):
            return A(SML + c, n)

        iota = con(K_IOTA, 128)
        maskC = con(K_MC, 512).rearrange("p (t k) -> p t k", t=2)
        maskD = con(K_MD, 512).rearrange("p (t k) -> p t k", t=2)

        ld_x = q.dma("act", xs[:, :].rearrange("p (t d) -> p t d", t=2), x_d, s_x, [])
        pos_i = ext[:, 0:2].bitcast(I32)
        ld_pos = q.dma("act", pos_i, pos_d, s_pos, [])
        ld_id = q.dma("act", ids[:, :], consts_d[:, 0:128], s_id, [])
        ld_k = q.dma("act", A(CON, K_W - 128), consts_d[:, 128:K_W], s_k, [])
        ld_s = q.dma("act", sml(0, S_W), smalls_d, s_sm, [])

        neghalf = stat(8)
        c0 = POOL(lambda e: e.memset(neghalf, -0.5))
        ss = stat(2)
        ms = stat(2)
        rstd = stat(2)

        def rms_rstd(src, junk, t, scale, *after):
            a = act(junk, src, ACTF.Square, *after, accum_out=ss[:, t:t + 1])
            b = ts(DVE, ms[:, t:t + 1], ss[:, t:t + 1], scale, EPS, ALU.mult, ALU.add, a)
            return tt(POOL, rstd[:, t:t + 1], ms[:, t:t + 1], neghalf[:, 0:1], ALU.pow, b, c0)

        def transposed(src, ncol, dst, evac, *after):
            done = []
            for t in range(2):
                for k0 in range(0, ncol, 4):
                    n = min(4, ncol - k0)
                    b = bank()
                    for k in range(n):
                        w = tr(banks[b][:, k * 128:(k + 1) * 128], src[:, t, (k0 + k) * 128:(k0 + k + 1) * 128],
                               *(list(after) + [free[b]] if k == 0 else []))
                    e = evac(t, k0, n, banks[b][:, 0:n * 128].rearrange("p (k c) -> p k c", k=n), w)
                    free[b] = [e]
                    done.append(e)
            return done

        def norm_T(g, buf, *after):
            outs = []
            for t in range(2):
                p = rms_rstd(x[:, t, :], buf[:, t, :], t, 1.0 / 1024, *after)
                outs.append(ts(DVE, buf[:, t, :], x[:, t, :], rstd[:, t:t + 1], None, ALU.mult, None, p))

            def evac(t, k0, n, ps, w):
                return tt(DVE, hT[:, k0:k0 + n, t * 128:(t + 1) * 128], ps,
                          g[:, k0:k0 + n].unsqueeze(2).broadcast_to([128, n, 128]), ALU.mult, w, ld_s)

            return transposed(buf, 8, hT, evac, outs, ld_id)

        def plain_evac(dst):
            def evac(t, k0, n, ps, w):
                return copy(t + k0 // 4, dst[:, k0:k0 + n, t * 128:(t + 1) * 128], ps, w)
            return evac

        posf = stat(2)
        ang, ra, rb, rn = stat(24), stat(24), stat(24), stat(24)
        cosP, sinP = stat(24), stat(24)
        d = DVE(lambda e: e.tensor_copy(posf, pos_i), ld_pos)
        a3 = ang.rearrange("p (t f) -> p t f", t=2)
        inv3 = con(K_INV, 12).unsqueeze(1).broadcast_to([128, 2, 12])
        d = tt(DVE, a3, posf.unsqueeze(2).broadcast_to([128, 2, 12]), inv3, ALU.mult, d, ld_k)

        def reduced(E, out, src, tmp, quarter, *after):
            d = ts(E, tmp, src, 1.0 / TWO_PI, quarter, ALU.mult, ALU.add, *after)
            d = ts(E, tmp, tmp, MAGIC, None, ALU.add, None, d)
            n = ts(E, tmp, tmp, MAGIC, None, ALU.subtract, None, d)
            d = n
            cur = src
            for c in (C1, C2, C3):
                d = stt(out, tmp, -c, cur, ALU.mult, ALU.add, d)
                cur = out
            if quarter:
                d = ts(E, out, out, math.pi / 2, None, ALU.add, None, d)
            return ts(E, out, out, 3.1415925, -3.1415925, ALU.min, ALU.max, d)

        r1 = reduced(DVE, ra, ang, rn, 0.0, d)
        r2 = reduced(DVE, rb, ang, rn, 0.25, r1)
        ldt, are, aim = sml(S_LDT, 16), sml(S_ARE, 16), sml(S_AIM, 16)
        dt_, xr, th, rr, fr = [stat(16) for _ in range(5)]
        sn, cn, sh, e1, kr, ki = [stat(16) for _ in range(6)]
        t16 = [stat(16) for _ in range(4)]
        a_dt = act(dt_, ldt, ACTF.Exp, ld_s)
        d = tt(DVE, xr, are, dt_, ALU.mult, a_dt)
        d = tt(DVE, th, aim, dt_, ALU.mult, a_dt)
        d = reduced(DVE, t16[0], th, t16[1], 0.0, d)
        sred = d
        d = ts(DVE, fr, t16[0], 1.0 / TWO_PI, None, ALU.mult, None, d)
        f_tok = d
        d = reduced(DVE, t16[2], th, t16[1], 0.25, d)
        cred = d
        a_ex = act(rr, xr, ACTF.Exp, d)
        a_s = act(sinP, ra, ACTF.Sin, r1)
        a_s = act(cosP, rb, ACTF.Sin, r2)
        a_sn = act(sn, t16[0], ACTF.Sin, sred)
        a_sh = act(sh, t16[0], ACTF.Sin, sred, scale=0.5)
        a_cn = act(cn, t16[2], ACTF.Sin, cred)
        rope_tok = a_s
        d = ts(DVE, t16[1], xr, 0.5, -0.5, ALU.min, ALU.max, a_cn)
        d = ts(DVE, e1, t16[1], 1.0 / 9, 1.0, ALU.mult, ALU.add, d)
        for c in (8, 7, 6, 5, 4, 3, 2):
            d = tt(DVE, e1, e1, t16[1], ALU.mult, d)
            d = ts(DVE, e1, e1, 1.0 / c, 1.0, ALU.mult, ALU.add, d)
        d = tt(DVE, e1, e1, t16[1], ALU.mult, d)
        d = tt(DVE, t16[2], t16[1], xr, ALU.is_equal, d)
        d = ts(DVE, t16[3], rr, -1.0, None, ALU.add, None, d, a_ex)
        msk = t16[2].bitcast(I32)
        d = DVE(lambda e: e.copy_predicated(t16[3], msk, e1), d)
        d = ts(DVE, rr, t16[3], 1.0, None, ALU.add, None, d)
        d = tt(DVE, kr, t16[3], cn, ALU.mult, d)
        d = tt(DVE, t16[0], sh, sh, ALU.mult, d, a_sh)
        d = stt(kr, t16[0], -2.0, kr, ALU.mult, ALU.add, d)
        d = tt(DVE, ki, rr, sn, ALU.mult, d)
        d = tt(DVE, t16[0], are, are, ALU.mult, d)
        d = tt(DVE, t16[1], aim, aim, ALU.mult, d)
        d = tt(DVE, t16[0], t16[0], t16[1], ALU.add, d)
        d = DVE(lambda e: e.reciprocal(t16[0], t16[0]), d)
        d = tt(DVE, t16[1], kr, are, ALU.mult, d)
        d = tt(DVE, t16[2], ki, aim, ALU.mult, d)
        d = tt(DVE, t16[1], t16[1], t16[2], ALU.add, d)
        d = tt(DVE, t16[2], ki, are, ALU.mult, d)
        d = tt(DVE, t16[3], kr, aim, ALU.mult, d)
        d = tt(DVE, t16[2], t16[2], t16[3], ALU.subtract, d)
        d = tt(DVE, kr, t16[1], t16[0], ALU.mult, d)
        k_tok = tt(DVE, ki, t16[2], t16[0], ALU.mult, d)
        lam = [stat(1) for _ in range(DEPTH)]
        lj, l1, l2 = stat(32), stat(1), stat(1)
        gd = [sml(S_GD + 64 * i, 64) for i in range(DEPTH)]
        lam_tok = []
        for i in range(DEPTH):
            v = [sml(S_LAM + 128 * i + 32 * j, 32) for j in range(4)]
            d1 = DVE(lambda e, v=v: e.tensor_tensor_reduce(lj, v[0], v[1], 1.0, 0.0, ALU.mult, ALU.add, l1), ld_s, k_tok, lam_tok)
            d2 = DVE(lambda e, v=v: e.tensor_tensor_reduce(lj, v[2], v[3], 1.0, 0.0, ALU.mult, ALU.add, l2), d1)
            a1 = act(l1, l1, ACTF.Exp, d2)
            a2 = act(l2, l2, ACTF.Exp, a1)
            d = tt(DVE, l1, l1, l2, ALU.subtract, a2)
            d = ts(DVE, lam[i], l1, LAM_INIT[i], None, ALU.add, None, d)
            d = ts(DVE, gd[i], gd[i], 1.0 - LAM_INIT[i], None, ALU.mult, None, d)
            lam_tok = [d]
        tv = con(K_T, 256).unsqueeze(1).broadcast_to([128, 4, 256])
        ptmp = A(TMP, 1024).rearrange("p (n t) -> p n t", n=4)
        tab_tok = []
        p = None
        for n in range(0, 16, 4):
            fb = fr[:, n:n + 4].unsqueeze(2).broadcast_to([128, 4, 256])
            for tab, quarter in ((sinT, 0.0), (cosT, 0.25)):
                o = tab[:, n:n + 4, :]
                p = tt(POOL, o, tv, fb, ALU.mult, f_tok, ld_k, p)
                if quarter:
                    p = ts(POOL, o, o, quarter, None, ALU.add, None, p)
                p = ts(POOL, ptmp, o, MAGIC, None, ALU.add, None, p)
                p = ts(POOL, ptmp, ptmp, MAGIC, None, ALU.subtract, None, p)
                p = tt(POOL, o, o, ptmp, ALU.subtract, p)
        phase_tok = p

        def rope(E, view, half, cos, sin, tmp, *after):
            u = view.shape[2]
            n = 2 * u * half
            ts4 = [tmp[:, i * n:(i + 1) * n].rearrange("p (t u f) -> p t u f", t=2, u=u) for i in range(4)]
            x1, x2 = view[:, :, :, 0:half], view[:, :, :, half:2 * half]
            cb = cos.unsqueeze(2).broadcast_to([128, 2, u, half])
            sn_ = sin.unsqueeze(2).broadcast_to([128, 2, u, half])
            tt(E, ts4[0], x1, cb, ALU.mult, *after)
            o2 = tt(E, ts4[1], x2, sn_, ALU.mult)
            tt(E, ts4[2], x2, cb, ALU.mult)
            o4 = tt(E, ts4[3], x1, sn_, ALU.mult)
            o5 = tt(E, x1, ts4[0], ts4[1], ALU.subtract, o4)
            return tt(E, x2, ts4[2], ts4[3], ALU.add, o4)

        NB = 4
        bsm = [A(ATT + 256 * i, 256) for i in range(NB)]
        bE = [A(ATT + 1024 + 256 * i, 256) for i in range(NB)]
        bET = [A(ATT + 2048 + 256 * i, 256) for i in range(NB)]
        mx = stat(20)
        den = stat(20)
        rden = stat(20)
        rlam = stat(4)

        def attend(maps, t, obanks, *after):
            nk = t + 1
            n = len(maps)
            s_t, m_t, e_t, tr_t, c_t, pv_t = ({} for _ in range(6))

            def scores(i):
                qT, kT, v, mask, scale, o = maps[i]
                b = i % 2
                s_t[i] = mm(banks[b][:, 0:128 * nk], [(qT, kT)], free[b], after)
                m_t[i] = DVE(lambda e: e.tensor_tensor_reduce(
                    bsm[i % NB][:, 0:128 * nk], banks[b][:, 0:128 * nk], mask, -scale, 3e38, ALU.add, ALU.min,
                    mx[:, i:i + 1]), s_t[i], e_t.get(i - NB), after if i == 0 else None)
                free[b] = [m_t[i]]
                e_t[i] = act(bE[i % NB][:, 0:128 * nk], bsm[i % NB][:, 0:128 * nk], ACTF.Exp, m_t[i], tr_t.get(i - NB),
                             bias=mx[:, i:i + 1], scale=-1.0, accum_out=den[:, i:i + 1])

            def turned(i):
                b = 2 + i % 2
                for k in range(nk):
                    tr_t[i] = tr(banks[b][:, 128 * k:128 * k + 128], bE[i % NB][:, 128 * k:128 * k + 128],
                                 e_t[i], free[b])
                c_t[i] = copy(i, bET[i % NB][:, 0:128 * nk], banks[b][:, 0:128 * nk], tr_t[i], pv_t.get(i - NB))
                free[b] = [c_t[i]]

            def pv(i):
                qT, kT, v, mask, scale, (ob, oc) = maps[i]
                first = oc == 0
                pv_t[i] = mm(banks[ob][:, oc:oc + 64],
                             [(bET[i % NB][:, 128 * k:128 * k + 128], v(k)) for k in range(nk)],
                             c_t[i], free[ob] if first else None)

            for i in range(n + 4):
                if i < n:
                    scores(i)
                if 0 <= i - 2 < n:
                    turned(i - 2)
                if 0 <= i - 4 < n:
                    pv(i - 4)
            return pv_t[n - 1], e_t[n - 1]

        last = [ld_x]
        dve_tmp = A(TMP + 1024, 1024)
        pool_tmp = A(TMP, 1024)
        cosp = cosP.rearrange("p (t f) -> p t f", t=2)
        sinp = sinP.rearrange("p (t f) -> p t f", t=2)
        for layer in range(DEPTH):
            h_tok = norm_T(sml(S_G + 8 * layer, 8), mix, last)
            ev = []
            for n in range(6):
                i, w, lt = load(win_d[layer, n])
                w = w.rearrange("p (k c) -> p k c", k=8)
                pair = []
                for t in range(2):
                    b = bank()
                    m = mm(banks[b][:, :], [(hT[:, k, t * 128:(t + 1) * 128], w[:, k, :]) for k in range(8)],
                           h_tok, lt, free[b])
                    e = copy(t, qkv[:, t, n * 512:(n + 1) * 512], banks[b][:, :], m)
                    free[b] = [e]
                    pair.append(e)
                slot_free[i] = [m]
                ev.append(pair)
            view = [qkv[:, :, 0:512].rearrange("p t (u d) -> p t u d", d=32),
                    qkv[:, :, 768:1280].rearrange("p t (u d) -> p t u d", d=64),
                    qkv[:, :, 1536:2560].rearrange("p t (u d) -> p t u d", d=64)]
            rA = rope(DVE, view[0], 4, cosp[:, :, 0:4], sinp[:, :, 0:4], dve_tmp, ev[0], rope_tok)
            rB = rope(POOL, view[1], 8, cosp[:, :, 4:12], sinp[:, :, 4:12], pool_tmp, ev[1], ev[2], rope_tok)
            rC = rope(DVE, view[2], 8, cosp[:, :, 4:12], sinp[:, :, 4:12], dve_tmp, ev[3], ev[4])
            cols = [128 * j for j in range(4)] + [768 + 128 * j for j in range(4)] + [1536 + 128 * j for j in range(8)]
            qk_tok = []
            for j in range(0, 16, 2):
                b = bank()
                for s in range(2):
                    for t in range(2):
                        w = tr(banks[b][:, s * 256 + t * 128:s * 256 + t * 128 + 128],
                               qkv[:, t, cols[j + s]:cols[j + s] + 128], (rA, rB, rC)[min(j // 4, 2)], free[b])
                e = copy(j // 2, qkT[:, j:j + 2, :], banks[b][:, :].rearrange("p (s t) -> p s t", s=2), w)
                free[b] = [e]
                qk_tok.append(e)
            mix_tok = []
            for t in range(2):
                nk = t + 1
                ob = [(4, 5, 6), (7, 4, 5)][t]
                maps = []
                for u in range(8):
                    o = 32 * (u % 4)
                    maps.append((qkT[o:o + 32, u // 4, t * 128:(t + 1) * 128], qkT[o:o + 32, 2 + u // 4, 0:128 * nk],
                                 lambda k, u=u: qkv[:, k, 512 + 64 * (u // 2):576 + 64 * (u // 2)],
                                 maskC[:, t, 0:128 * nk], 32 ** -0.5, (ob[0], 64 * u)))
                for h in range(4):
                    o = 64 * (h % 2)
                    maps.append((qkT[o:o + 64, 4 + h // 2, t * 128:(t + 1) * 128], qkT[o:o + 64, 6 + h // 2, 0:128 * nk],
                                 lambda k, h=h: qkv[:, k, 1280 + 64 * h:1344 + 64 * h],
                                 maskC[:, t, 0:128 * nk], 0.125, (ob[1], 64 * h)))
                for h in range(8):
                    o = 64 * (h % 2)
                    maps.append((qkT[o:o + 64, 8 + h // 2, t * 128:(t + 1) * 128], qkT[o:o + 64, 12 + h // 2, 0:128 * nk],
                                 lambda k, h=h: qkv[:, k, 2560 + 64 * h:2624 + 64 * h],
                                 maskD[:, t, 0:128 * nk], 0.125, (ob[1 + (h + 4) // 8], 64 * ((h + 4) % 8))))
                pv, ex = attend(maps, t, ob, qk_tok, ev, mix_tok)
                d = DVE(lambda e: e.reciprocal(rden, den), ex)
                d = ts(DVE, rlam, rden[:, 1:8:2], lam[layer], None, ALU.mult, None, d, lam_tok)
                oA = banks[ob[0]][:, :].rearrange("p (h c d) -> p h c d", h=4, c=2)
                ta = dve_tmp[:, 0:256].rearrange("p (h d) -> p h d", h=4)
                tb = dve_tmp[:, 256:512].rearrange("p (h d) -> p h d", h=4)
                m1 = tt(DVE, ta, oA[:, :, 0, :], rden[:, 0:8:2].unsqueeze(2).broadcast_to([128, 4, 64]), ALU.mult, pv, d)
                m2 = tt(DVE, tb, oA[:, :, 1, :], rlam.unsqueeze(2).broadcast_to([128, 4, 64]), ALU.mult, d)
                free[ob[0]] = [m2]
                d = tt(DVE, ta, ta, tb, ALU.subtract, m2)
                d = tt(DVE, tb, ta, ta, ALU.mult, d)
                d = DVE(lambda e: e.tensor_reduce(rlam, tb, AX, ALU.add), d)
                d = ts(DVE, rlam, rlam, 1.0 / 64, EPS, ALU.mult, ALU.add, d)
                p = tt(POOL, rlam, rlam, neghalf[:, 0:4], ALU.pow, d)
                d = tt(DVE, ta, ta, rlam.unsqueeze(2).broadcast_to([128, 4, 64]), ALU.mult, p)
                d = tt(DVE, mix[:, t, 0:256].rearrange("p (h d) -> p h d", h=4), ta,
                       gd[layer].unsqueeze(1).broadcast_to([128, 4, 64]), ALU.mult, d)
                d1 = tt(DVE, mix[:, t, 256:768].rearrange("p (h d) -> p h d", h=8),
                        banks[ob[1]][:, :].rearrange("p (h d) -> p h d", h=8),
                        rden[:, 8:16].unsqueeze(2).broadcast_to([128, 8, 64]), ALU.mult)
                d2 = tt(DVE, mix[:, t, 768:1024].rearrange("p (h d) -> p h d", h=4),
                        banks[ob[2]][:, 0:256].rearrange("p (h d) -> p h d", h=4),
                        rden[:, 16:20].unsqueeze(2).broadcast_to([128, 4, 64]), ALU.mult)
                free[ob[1]] = [d1]
                free[ob[2]] = [d2]
                mix_tok = [d2]
            mT = transposed(mix, 8, hT, plain_evac(hT), mix_tok)
            x_tok = []
            for n in range(2):
                i, w, lt = load(wout_d[layer, n])
                w = w.rearrange("p (k c) -> p k c", k=8)
                for t in range(2):
                    b = bank()
                    m = mm(banks[b][:, :], [(hT[:, k, t * 128:(t + 1) * 128], w[:, k, :]) for k in range(8)],
                           mT, lt, free[b])
                    xv = x[:, t, n * 512:(n + 1) * 512]
                    e = tt(DVE, xv, xv, banks[b][:, :], ALU.add, m)
                    free[b] = [e]
                    x_tok.append(e)
                slot_free[i] = [m]
            h_tok = norm_T(sml(S_G + 16 + 8 * layer, 8), mix, x_tok)
            cv = sml(S_CONV + 176 * layer, 176).rearrange("p (n j) -> p n j", j=4)
            cb = [[A(ATT + 768 * s + 256 * j, 256) for j in range(3)] for s in range(4)]
            y_tok = {}
            for s in range(11):
                i, w, lt = load(wup_d[layer, s])
                w = w.rearrange("p (k i c) -> p k i c", k=8, i=4)
                for g in range(2):
                    f = 2 * s + g
                    b = bank()
                    for half in range(2):
                        m = mm(banks[b][:, 256 * half:256 * half + 256],
                               [(w[:, k, 2 * half + g, :], hT[:, k, :]) for k in range(8)], h_tok, lt, free[b])
                    c = cb[f % 4]
                    for half in range(2):
                        col = cv[:, f + NTILE * half, :]
                        u = banks[b][:, 256 * half:256 * half + 256]
                        a = act(c[half], u, ACTF.Identity, m, y_tok.get(f - 4), scale=col[:, 2:3], bias=col[:, 3:4])
                        d = stt(c[half][:, 1:256], u[:, 0:255], col[:, 1:2], c[half][:, 1:256], ALU.mult, ALU.add, a)
                        d = stt(c[half][:, 2:256], u[:, 0:254], col[:, 0:1], c[half][:, 2:256], ALU.mult, ALU.add, d)
                        if half == 0:
                            sg = act(c[2], c[0], ACTF.Silu, d)
                    free[b] = [d]
                    y_tok[f] = tt(POOL, yT[:, f, :], c[2], c[1], ALU.mult, sg, d)
                slot_free[i] = [m]
            acc = [[bank() for _ in range(2)] for _ in range(2)]
            for s in range(6):
                nk = min(4, NTILE - 4 * s)
                i, w, lt = load(wdown_d[layer, s, :, 0:nk * 1024], nk * 1024)
                w = w.rearrange("p (k c) -> p k c", k=nk)
                for kk in range(nk):
                    f = 4 * s + kk
                    for t in range(2):
                        for n in range(2):
                            b = acc[t][n]
                            m = PE(lambda e, b=b, f=f, t=t, n=n, kk=kk, w=w: e.matmul(
                                banks[b][:, :], yT[:, f, t * 128:(t + 1) * 128], w[:, kk, n * 512:(n + 1) * 512],
                                start=f == 0, stop=f == NTILE - 1), y_tok[f], lt, free[b] if f == 0 else None)
                slot_free[i] = [m]
            last = []
            for t in range(2):
                for n in range(2):
                    b = acc[t][n]
                    xv = x[:, t, n * 512:(n + 1) * 512]
                    e = tt(DVE, xv, xv, banks[b][:, :], ALU.add, m)
                    free[b] = [e]
                    last.append(e)
        i, grow, lt = load(rows_d[0], 1024)
        x_tok = []
        for t in range(2):
            p = rms_rstd(x[:, t, :], mix[:, t, :], t, 1.0 / 1024, last)
            x_tok.append(stt(x[:, t, :], x[:, t, :], rstd[:, t:t + 1], grow, ALU.mult, ALU.mult, p, lt))
        slot_free[i] = [x_tok[-1]]

        a_t1 = act(A(4096, 8192), A(4096, 8192), ACTF.Sin, phase_tok, scale=SIN_SCALE)
        h_tok = norm_T(sml(S_G + 32, 8), mix, x_tok)
        GAT, PRJ, UT, QT2 = QKV, QKV + 4096, QKV + 6224, QKV + 7248
        gates = A(GAT, 4096).rearrange("p (t n) -> p t n", t=2)
        proj = A(PRJ, 2128).rearrange("p (t n) -> p t n", t=2)
        uT = A(UT, 1024).rearrange("p (i t) -> p i t", i=4)
        qT2 = A(QT2, 2304).rearrange("p (k t) -> p k t", k=9)
        i, w, lt = load(win2_d[0])
        w = w.rearrange("p (k c) -> p k c", k=8)
        u_tok = []
        for c in range(4):
            b = bank()
            m = mm(banks[b][:, 0:256], [(w[:, k, c * 128:(c + 1) * 128], hT[:, k, :]) for k in range(8)],
                   h_tok, lt, free[b])
            e = copy(c, uT[:, c, :], banks[b][:, 0:256], m)
            free[b] = [e]
            u_tok.append(e)
        slot_free[i] = [m]
        pr_tok = []
        for n, (src, c0_, cw) in enumerate([(win2_d[1], 0, 512), (win2_d[2], 512, 512), (wqk_d, 1024, 40)]):
            i, w, lt = load(src, 8 * cw)
            w = w.rearrange("p (k c) -> p k c", k=8)
            for t in range(2):
                b = bank()
                m = mm(banks[b][:, 0:cw], [(hT[:, k, t * 128:(t + 1) * 128], w[:, k, :]) for k in range(8)],
                       h_tok, lt, free[b])
                e = copy(t, proj[:, t, c0_:c0_ + cw], banks[b][:, 0:cw], m)
                free[b] = [e]
                pr_tok.append(e)
            slot_free[i] = [m]
        g_tok = []
        for n in range(4):
            i, w, lt = load(win2_d[3 + n])
            w = w.rearrange("p (k c) -> p k c", k=8)
            for t in range(2):
                b = bank()
                m = mm(banks[b][:, :], [(hT[:, k, t * 128:(t + 1) * 128], w[:, k, :]) for k in range(8)],
                       h_tok, lt, free[b])
                e = act(gates[:, t, n * 512:(n + 1) * 512], banks[b][:, :], ACTF.Sigmoid, m)
                free[b] = [e]
                g_tok.append(e)
            slot_free[i] = [m]
        use["n"] = 3
        use["i"] = 0
        cosA = con(K_CA, 64).rearrange("p (t f) -> p t f", t=2)
        sinA = con(K_SA, 64).rearrange("p (t f) -> p t f", t=2)
        cosI = con(K_CI, 32).rearrange("p (t f) -> p t f", t=2)
        sinI = con(K_SI, 32).rearrange("p (t f) -> p t f", t=2)
        rQ = rope(DVE, proj[:, :, 0:640].rearrange("p t (u d) -> p t u d", d=64), 32, cosA, sinA, A(ATT, 2560), pr_tok)
        rI = rope(POOL, proj[:, :, 768:1056].rearrange("p t (u d) -> p t u d", d=32), 16, cosI, sinI, A(TMP, 1152), pr_tok)
        kk2 = A(MIX, 512).rearrange("p (t h r d) -> p t h r d", t=2, h=2, r=2)
        ki4 = A(MIX + 512, 256).rearrange("p (t r d) -> p t r d", t=2, r=4)
        dup = []
        for t in range(2):
            kv = proj[:, t, 512:640].rearrange("p (h d) -> p h d", h=2)
            for r in range(2):
                dup.append(DVE(lambda e, t=t, r=r, kv=kv: e.tensor_copy(kk2[:, t, :, r, :], kv), rQ))
            dup.append(DVE(lambda e, t=t: e.tensor_copy(
                ki4[:, t], proj[:, t, 1024:1056].unsqueeze(1).broadcast_to([128, 4, 32])), rI))
        srcs = [proj[:, :, 128 * j:128 * j + 128] for j in range(4)]
        srcs += [A(MIX, 512).rearrange("p (t c) -> p t c", t=2)[:, :, 128 * j:128 * j + 128] for j in range(2)]
        srcs += [proj[:, :, 768 + 128 * j:896 + 128 * j] for j in range(2)]
        srcs += [A(MIX + 512, 256).rearrange("p (t c) -> p t c", t=2)]
        q_tok = []
        for j in range(0, 9, 2):
            b = bank()
            ns = min(2, 9 - j)
            for s in range(ns):
                for t in range(2):
                    w = tr(banks[b][:, s * 256 + t * 128:s * 256 + t * 128 + 128], srcs[j + s][:, t, :],
                           rQ, rI, dup, free[b])
            e = copy(j // 2, qT2[:, j:j + ns, :], banks[b][:, 0:256 * ns].rearrange("p (s t) -> p s t", s=ns), w)
            free[b] = [e]
            q_tok.append(e)
        rel = [ext[:, 256 * j:256 * j + 256] for j in range(4)]
        sc = [ext[:, 1024 + 256 * t:1280 + 256 * t] for t in range(2)]
        mask2 = [ext[:, 1536 + 256 * t:1792 + 256 * t] for t in range(2)]
        m8 = stat(8)
        rel_free = [[] for _ in range(4)]
        sel_tok = []
        for t in range(2):
            nk = t + 1
            d = None
            for h in range(8):
                b = bank()
                o = 32 * (h % 4)
                m = mm(banks[b][:, 0:128 * nk],
                       [(qT2[o:o + 32, 6 + h // 4, t * 128:(t + 1) * 128], qT2[o:o + 32, 8, 0:128 * nk])],
                       q_tok, free[b])
                r = rel[h % 4][:, 0:128 * nk]
                a = act(r, banks[b][:, 0:128 * nk], ACTF.Relu, m, rel_free[h % 4])
                free[b] = [a]
                wcol = proj[:, t, 1056 + h:1057 + h]
                s_ = sc[t][:, 0:128 * nk]
                if h == 0:
                    d = ts(DVE, s_, r, wcol, None, ALU.mult, None, a, pr_tok)
                else:
                    d = stt(s_, r, wcol, s_, ALU.mult, ALU.add, a, d)
                rel_free[h % 4] = [d]
            d = stt(s_, s_, 0.0625, maskC[:, t, 0:128 * nk], ALU.mult, ALU.add, d)
            for r in range(8):
                d = DVE(lambda e, s_=s_: e.max(m8, s_), d)
                d = DVE(lambda e, s_=s_: e.match_replace(s_, m8, s_, TAKEN), d)
            m_ = mask2[t][:, 0:128 * nk]
            d = ts(DVE, m_, s_, -2e38, NEG, ALU.is_gt, ALU.mult, d)
            d = tt(DVE, m_, m_, maskC[:, t, 0:128 * nk], ALU.add, d)
            sel_tok.append(d)
        ya = A(MIX + 1024, 1024).rearrange("p (t n) -> p t n", t=2)
        yaT = A(QT2, 1024).rearrange("p (k t) -> p k t", k=4)
        ya_tok = []
        for t in range(2):
            nk = t + 1
            maps = []
            for h in range(8):
                o = 64 * (h % 2)
                maps.append((qT2[o:o + 64, h // 2, t * 128:(t + 1) * 128], qT2[o:o + 64, 4 + h // 4, 0:128 * nk],
                             lambda k, h=h: proj[:, k, 640 + 64 * (h // 4):704 + 64 * (h // 4)],
                             mask2[t][:, 0:128 * nk], 0.125, (4 + t, 64 * h)))
            pv, ex = attend(maps, t, (4 + t,), q_tok, sel_tok[t], ya_tok)
            d = DVE(lambda e: e.reciprocal(rden[:, 0:8], den[:, 0:8]), ex)
            d = tt(DVE, ya[:, t, :].rearrange("p (h d) -> p h d", h=8),
                   banks[4 + t][:, :].rearrange("p (h d) -> p h d", h=8),
                   rden[:, 0:8].unsqueeze(2).broadcast_to([128, 8, 64]), ALU.mult, d, pv)
            free[4 + t] = [d]
            ya_tok = [d]
        yaT_tok = transposed(ya, 4, yaT, plain_evac(yaT), ya_tok, pv)
        ld_w = q.dma("sp", A(0, 2048), wsm_d, s_ssm, [slot_free[3]])
        Bb = [A(512 * j, 512).rearrange("p (n c) -> p n c", n=16) for j in range(2)]
        Cb = [A(1024 + 512 * j, 512) for j in range(2)]
        nC = [A(2048 + 512 * j, 512) for j in range(2)]
        Br = [A(3072 + 512 * j, 512).rearrange("p (n c) -> p n c", n=16) for j in range(2)]
        st = A(TMP, 512).rearrange("p (n c) -> p n c", n=16)
        krb = kr.unsqueeze(2).broadcast_to([128, 16, 32])
        kib = ki.unsqueeze(2).broadcast_to([128, 16, 32])
        pc = ts(POOL, nC[0], Cb[0], -1.0, None, ALU.mult, None, ld_w)
        pc = ts(POOL, nC[1], Cb[1], -1.0, None, ALU.mult, None)
        p = tt(POOL, Br[0], Bb[0], krb, ALU.mult, k_tok, rI)
        p = tt(POOL, st, Bb[1], kib, ALU.mult)
        p = tt(POOL, Br[0], Br[0], st, ALU.subtract, p)
        p = tt(POOL, Br[1], Bb[1], krb, ALU.mult, p)
        p = tt(POOL, st, Bb[0], kib, ALU.mult, p)
        p = tt(POOL, Br[1], Br[1], st, ALU.add, p)
        BT = [A(MIX + 512 * j, 512).rearrange("p (i s) -> p i s", i=4) for j in range(2)]
        bt_tok = []
        for j in range(2):
            b = bank()
            for i in range(4):
                w = tr(banks[b][:, i * 128:(i + 1) * 128], Br[j][:, 4 * i:4 * i + 4, :].rearrange("p n c -> p (n c)"),
                       p, free[b])
            e = copy(j, BT[j], banks[b][:, :].rearrange("p (i s) -> p i s", i=4), w)
            free[b] = [e]
            bt_tok.append(e)
        P1, P2, W_, Z_, Q1, Q2 = [ext[:, 512 * j:512 * j + 512] for j in range(6)]
        gy = A(TMP, 1024).rearrange("p (i t) -> p i t", i=4)
        ylin = A(TMP + 1024, 1024).rearrange("p (i t) -> p i t", i=4)
        ysT = A(QT2 + 1024, 1024).rearrange("p (i t) -> p i t", i=4)
        dsk = sml(S_DSK, 4)
        zq = None
        yb = None
        bu_t, pm_t = {}, None
        gy_tok = []

        def bu(n):
            b = 4 + n % 2
            o = 32 * (n % 4)
            for j in range(2):
                m = mm(banks[b][:, 256 * j:256 * j + 256], [(BT[j][o:o + 32, n // 4, :], uT[o:o + 32, n // 4, :])],
                       bt_tok, u_tok, free[b], yaT_tok)
            bu_t[n] = (b, m)

        bu(0)
        for n in range(16):
            if n + 1 < 16:
                bu(n + 1)
            b, m = bu_t[n]
            cs = A(4096, 8192).rearrange("p (a n t) -> p a n t", a=2, n=16)[:, :, n, :]
            bv = banks[b][:, :].rearrange("p (a t) -> p a t", a=2)
            v = [y.rearrange("p (a t) -> p a t", a=2) for y in (P1, P2, W_, Z_, Q1, Q2)]
            d1 = tt(DVE, v[0], bv, cs, ALU.mult, m, a_t1, yaT_tok)
            d2a = tt(DVE, v[1][:, 0, :], bv[:, 1, :], cs[:, 0, :], ALU.mult)
            d2 = tt(DVE, v[1][:, 1, :], bv[:, 0, :], cs[:, 1, :], ALU.mult)
            free[b] = [d2]
            d3 = tt(DVE, v[2][:, 0, :], v[0][:, 0, :], v[0][:, 1, :], ALU.add, d2)
            d3 = tt(DVE, v[2][:, 1, :], v[1][:, 0, :], v[1][:, 1, :], ALU.subtract, d2)
            rb_ = rr[:, n:n + 1].broadcast_to([128, 256])
            for j in range(2):
                d4 = DVE(lambda e, j=j, rb_=rb_, v=v: e.tensor_tensor_scan(v[3][:, j, :], rb_, v[2][:, j, :], 0.0,
                                                                    ALU.mult, ALU.add), d3)
            d5 = tt(DVE, v[4], v[3], cs, ALU.mult, d4, pm_t)
            tt(DVE, v[5][:, 0, :], v[3][:, 0, :], cs[:, 1, :], ALU.mult)
            d6 = tt(DVE, v[5][:, 1, :], v[3][:, 1, :], cs[:, 0, :], ALU.mult)
            if n % 4 == 0:
                yb = 6 + (n // 4) % 2
            o = 32 * (n % 4)
            cc = slice(32 * n, 32 * n + 32)
            out = banks[yb][o:o + 32, 0:256]
            pm_t = None
            for j, (l, r) in enumerate([(Cb[0], v[4][:, 0, :]), (nC[0], v[4][:, 1, :]),
                                        (nC[1], v[5][:, 0, :]), (nC[1], v[5][:, 1, :])]):
                pm_t = PE(lambda e, l=l, r=r, j=j, out=out, cc=cc, o=o: e.matmul(
                    out, l[:, cc], r, start=j == 0, stop=j == 3, tile_position=(0, o)),
                    d6, pc, free[yb] if n % 4 == 0 else None)
            if n % 4 == 3:
                i = n // 4
                d = stt(ylin[:, i, :], uT[:, i, :], dsk[:, i:i + 1], banks[yb][:, 0:256], ALU.mult, ALU.add, pm_t)
                free[yb] = [d]
                gy_tok.append(act(gy[:, i, :], ylin[:, i, :], ACTF.Gelu_apprx_tanh, d, bt_tok))
        i, w, lt = load(wglu_d, 2048)
        w = w.rearrange("p (k c) -> p k c", k=4)
        ys_tok = []
        for c in range(4):
            b = bank()
            m = mm(banks[b][:, 0:256], [(w[:, k, c * 128:(c + 1) * 128], gy[:, k, :]) for k in range(4)],
                   gy_tok, lt, free[b])
            a = act(ylin[:, c, :], banks[b][:, 0:256], ACTF.Sigmoid, m)
            free[b] = [a]
            ys_tok.append(tt(DVE, ysT[:, c, :], ylin[:, c, :], gy[:, c, :], ALU.mult, a))
        slot_free[i] = [m]
        merged = A(4096, 2048).rearrange("p (t n) -> p t n", t=2)
        mtmp = A(6144, 2048).rearrange("p (t n) -> p t n", t=2)
        me_tok = []
        for which, (src, lhs, toks) in enumerate([(wsu_d, ysT, ys_tok), (wau_d, yaT, yaT_tok)]):
            i, w, lt = load(src)
            w = w.rearrange("p (k c) -> p k c", k=4)
            for t in range(2):
                for n in range(2):
                    b = bank()
                    m = mm(banks[b][:, :], [(lhs[:, k, t * 128:(t + 1) * 128], w[:, k, n * 512:(n + 1) * 512])
                                            for k in range(4)], toks, lt, free[b])
                    cs_ = slice(n * 512, (n + 1) * 512)
                    gsl = gates[:, t, which * 1024 + n * 512:which * 1024 + (n + 1) * 512]
                    dst = (merged, mtmp)[which][:, t, cs_]
                    d = tt(DVE, dst, banks[b][:, :], gsl, ALU.mult, m, g_tok, ys_tok, pm_t)
                    free[b] = [d]
                    if which:
                        d = tt(DVE, merged[:, t, cs_], merged[:, t, cs_], dst, ALU.add, d)
                    me_tok.append(d)
            slot_free[i] = [m]
        mT = transposed(merged, 8, hT, plain_evac(hT), me_tok)
        x_tok = []
        for n in range(2):
            i, w, lt = load(wout2_d[n])
            w = w.rearrange("p (k c) -> p k c", k=8)
            for t in range(2):
                b = bank()
                m = mm(banks[b][:, :], [(hT[:, k, t * 128:(t + 1) * 128], w[:, k, :]) for k in range(8)],
                       mT, lt, free[b])
                xv = x[:, t, n * 512:(n + 1) * 512]
                e = tt(DVE, xv, xv, banks[b][:, :], ALU.add, m)
                free[b] = [e]
                x_tok.append(e)
            slot_free[i] = [m]
        h_tok = norm_T(sml(S_G + 40, 8), merged, x_tok)
        pqT = A(QKV, 4096).rearrange("p (n t) -> p n t", n=16)
        pq_tok = []
        for s in range(4):
            i, w, lt = load(wpq_d[s])
            w = w.rearrange("p (k c) -> p k c", k=8)
            for c in range(4):
                b = bank()
                m = mm(banks[b][:, 0:256], [(w[:, k, c * 128:(c + 1) * 128], hT[:, k, :]) for k in range(8)],
                       h_tok, lt, free[b])
                e = copy(c, pqT[:, 4 * s + c, :], banks[b][:, 0:256], m)
                free[b] = [e]
                pq_tok.append(e)
            slot_free[i] = [m]
        i, keys, lt = load(keys_d, 2048)
        keys = keys.rearrange("p (n c) -> p n c", n=16)
        S = A(8192, 4096).rearrange("p (t n c) -> p t n c", t=2, n=16)
        s_tok = []
        for t in range(2):
            for n in range(0, 16, 4):
                b = bank()
                for j in range(4):
                    m = mm(banks[b][:, j * 128:(j + 1) * 128],
                           [(pqT[:, n + j, t * 128:(t + 1) * 128], keys[:, n + j, :])], pq_tok, lt, free[b])
                e = copy(n // 4, S[:, t, n:n + 4, :], banks[b][:, :].rearrange("p (n c) -> p n c", n=4), m)
                free[b] = [e]
                s_tok.append(e)
        slot_free[i] = [m]
        v16 = A(QKV + 4096, 256).rearrange("p (n k) -> p n k", n=16)
        i16 = A(QKV + 4352, 256).bitcast(U32).rearrange("p (n k) -> p n k", n=16)
        if16 = A(QKV + 4608, 256).rearrange("p (n k) -> p n k", n=16)
        tops = A(QKV + 4864, 128).rearrange("p (h k) -> p h k", h=8)
        pos = A(QKV + 4992, 128).bitcast(U32).rearrange("p (h k) -> p h k", h=8)
        pa = A(QKV + 5120, 128)
        pb = A(QKV + 5248, 128)
        pau = A(QKV + 5376, 128).bitcast(U32)
        pbu = A(QKV + 5504, 128).bitcast(U32)
        gt = A(QKV + 5632, 128).rearrange("p (h k) -> p h k", h=8)
        zs = A(QKV + 5760, 8)
        sel = A(QKV + 5888, 256).rearrange("p (a n) -> p a n", a=2)
        cand = A(4096, 2048).rearrange("p (h c) -> p h c", h=8)
        oh = A(6144, 2048).rearrange("p (h k j) -> p h k j", h=8, k=16)
        selT = ext[:, 0:768].rearrange("p (a t) -> p a t", a=3)
        iot = ext[:, 768:896]
        i_tok = DVE(lambda e: e.tensor_copy(iot, iota), h_tok)
        sT_tok = []
        prev = [h_tok, i_tok]
        for t in range(2):
            for n in range(16):
                sv = S[:, t, n, :]
                d = DVE(lambda e, n=n, sv=sv: e.max(v16[:, n, 0:8], sv), s_tok, prev)
                d = DVE(lambda e, n=n, sv=sv: e.max_index(i16[:, n, 0:8], v16[:, n, 0:8], sv), d)
                d = DVE(lambda e, n=n, sv=sv: e.match_replace(sv, v16[:, n, 0:8], sv, TAKEN), d)
                d = DVE(lambda e, n=n, sv=sv: e.max(v16[:, n, 8:16], sv), d)
                d = DVE(lambda e, n=n, sv=sv: e.max_index(i16[:, n, 8:16], v16[:, n, 8:16], sv), d)
            vv = v16.rearrange("p (h c) k -> p h c k", c=2)
            d = tt(DVE, cand.rearrange("p h (i j) -> p h i j", i=16),
                   vv[:, :, 0, :].unsqueeze(3).broadcast_to([128, 8, 16, 16]),
                   vv[:, :, 1, :].unsqueeze(2).broadcast_to([128, 8, 16, 16]), ALU.add, d)
            for h in range(8):
                cv_ = cand[:, h, :]
                d = DVE(lambda e, h=h, cv_=cv_: e.max(tops[:, h, 0:8], cv_), d)
                d = DVE(lambda e, h=h, cv_=cv_: e.max_index(pos[:, h, 0:8], tops[:, h, 0:8], cv_), d)
                d = DVE(lambda e, h=h, cv_=cv_: e.match_replace(cv_, tops[:, h, 0:8], cv_, TAKEN), d)
                d = DVE(lambda e, h=h, cv_=cv_: e.max(tops[:, h, 8:16], cv_), d)
                d = DVE(lambda e, h=h, cv_=cv_: e.max_index(pos[:, h, 8:16], tops[:, h, 8:16], cv_), d)
            d = tt(DVE, gt, tops, tops[:, :, 0:1].broadcast_to([128, 8, 16]), ALU.subtract, d)
            a = act(gt, gt, ACTF.Exp, d)
            posf_ = pos.rearrange("p h k -> p (h k)")
            d = ts(DVE, pau, posf_, 4, None, ALU.logical_shift_right, None, d)
            d = ts(DVE, pbu, posf_, 15, None, ALU.bitwise_and, None, d)
            d = DVE(lambda e: e.tensor_copy(pa, pau), d)
            d = DVE(lambda e: e.tensor_copy(pb, pbu), d)
            d = DVE(lambda e: e.tensor_copy(if16, i16), d)
            ifv = if16.rearrange("p (h c) k -> p h c k", c=2)
            for c, pp in ((0, pa), (1, pb)):
                d = tt(DVE, oh, pp.rearrange("p (h k) -> p h k", h=8).unsqueeze(3).broadcast_to([128, 8, 16, 16]),
                       iot[:, 0:16].unsqueeze(1).unsqueeze(1).broadcast_to([128, 8, 16, 16]), ALU.is_equal, d)
                d = tt(DVE, oh, oh, ifv[:, :, c, :].unsqueeze(2).broadcast_to([128, 8, 16, 16]), ALU.mult, d)
                d = DVE(lambda e, c=c: e.tensor_reduce(sel[:, c, :].rearrange("p (h k) -> p h k", h=8), oh, AX, ALU.add), d)
            d = DVE(lambda e: e.tensor_reduce(zs, gt, AX, ALU.add), a, d)
            d = DVE(lambda e: e.reciprocal(zs, zs), d)
            d = tt(DVE, gt, gt, zs.unsqueeze(2).broadcast_to([128, 8, 16]), ALU.mult, d)
            b = bank()
            for j, src in enumerate((gt.rearrange("p h k -> p (h k)"), sel[:, 0, :], sel[:, 1, :])):
                w = tr(banks[b][:, j * 128:(j + 1) * 128], src, d, free[b])
            e = DVE(lambda e, t=t, b=b: e.tensor_copy(selT[:, :, t * 128:(t + 1) * 128],
                                                     banks[b][:, 0:384].rearrange("p (a t) -> p a t", a=3)), w)
            free[b] = [e]
            prev = [e]
            sT_tok.append(e)
        G = arena[:, :].rearrange("p (j t) -> p j t", j=128)
        ohA = [ext[:, 1024 + 128 * j:1152 + 128 * j] for j in range(4)]
        ohB = [ext[:, 1536 + 128 * j:1664 + 128 * j] for j in range(4)]
        g_mm = {}
        G_tok = []
        for t0 in range(0, 256, 4):
            b = bank()
            for j in range(4):
                t = t0 + j
                dA = ts(DVE, ohA[t % 4], iot, selT[:, 1, t:t + 1], selT[:, 0, t:t + 1], ALU.is_equal, ALU.mult,
                        sT_tok, g_mm.get(t - 4))
                dB = ts(DVE, ohB[t % 4], iot, selT[:, 2, t:t + 1], None, ALU.is_equal, None)
                g_mm[t] = mm(banks[b][:, j * 128:(j + 1) * 128], [(ohA[t % 4], ohB[t % 4])], dB, free[b])
            e = copy(t0 // 4, G[:, :, t0:t0 + 4], banks[b][:, :].rearrange("p (t j) -> p j t", t=4), g_mm[t0 + 3])
            free[b] = [e]
            G_tok.append(e)
        G_tok = G_tok[-2:]
        hg = [ext[:, 2048 + 256 * j:2304 + 256 * j] for j in range(3)]
        ac = [ext[:, 2816 + 256 * j:3072 + 256 * j] for j in range(3)]
        h_mm, a_tk, v_mm = {}, {}, {}
        uw, vw = {}, {}

        def hidden(j):
            if j % 4 == 0:
                uw["i"], w, uw["t"] = load(ut_d[j // 4])
                uw["w"] = w.rearrange("p (j k c) -> p j k c", j=4, k=8)
            w, lt = uw["w"], uw["t"]
            b = 4 + j % 4
            m = mm(banks[b][:, 0:256], [(w[:, j % 4, k, :], hT[:, k, :]) for k in range(8)], lt, free[b], h_tok)
            if j % 4 == 3:
                slot_free[uw["i"]] = [m]
            a = act(hg[j % 3], banks[b][:, 0:256], ACTF.Gelu_apprx_tanh, m, a_tk.get(j - 3))
            free[b] = [a]
            a_tk[j] = tt(DVE, ac[j % 3], hg[j % 3], G[:, j, :], ALU.mult, a, G_tok, v_mm.get(j - 3))

        def down(j):
            if j % 4 == 0:
                vw["i"], w, vw["t"] = load(vt_d[j // 4])
                vw["w"] = w.rearrange("p (j c) -> p j c", j=4)
            w, lt = vw["w"], vw["t"]
            for t in range(2):
                for n in range(2):
                    b = 2 * t + n
                    v_mm[j] = PE(lambda e, b=b, t=t, n=n, w=w: e.matmul(
                        banks[b][:, :], ac[j % 3][:, t * 128:(t + 1) * 128], w[:, j % 4, n * 512:(n + 1) * 512],
                        start=j == 0, stop=j == 127), a_tk[j], lt, free[b] if j == 0 else None)
            if j % 4 == 3:
                slot_free[vw["i"]] = [v_mm[j]]

        for j in range(128 + 2):
            if j < 128:
                hidden(j)
            if j >= 2:
                down(j - 2)
        x_tok = []
        for t in range(2):
            for n in range(2):
                b = 2 * t + n
                xv = x[:, t, n * 512:(n + 1) * 512]
                x_tok.append(tt(DVE, xv, xv, banks[b][:, :], ALU.add, v_mm[127]))
        i, grow, lt = load(rows_d[1], 1024)
        y = A(0, 2048).rearrange("p (t d) -> p t d", t=2)
        fin = A(2048, 16)
        done = []
        for t in range(2):
            f = fin[:, 4 * t:4 * t + 4]
            a = act(y[:, t, :], x[:, t, :], ACTF.Square, x_tok, accum_out=f[:, 0:1])
            d = ts(DVE, f[:, 1:2], f[:, 0:1], 1.0 / 1024, EPS, ALU.mult, ALU.add, a)
            m_ = POOL(lambda e, f=f: e.memset(f[:, 3:4], -0.5), d)
            p = tt(POOL, f[:, 2:3], f[:, 1:2], f[:, 3:4], ALU.pow, m_)
            d = stt(y[:, t, :], x[:, t, :], f[:, 2:3], grow, ALU.mult, ALU.mult, p, lt)
            done.append(q.dma("sp", out_d[t * 128:(t + 1) * 128, :], y[:, t, :], s_out, [d]))
        fin_tok = done[-1]

        q.number(sems)
        block = ctx.enter_context(nc.Block())

        @block.sync
        def _(eng):
            q.emit("sp", eng)
            eng.wait_ge(s_out, fin_tok.val)

        @block.scalar
        def _(eng):
            q.emit("act", eng)

        @block.vector
        def _(eng):
            q.emit("dve", eng)

        @block.tensor
        def _(eng):
            q.emit("pe", eng)

        @block.gpsimd
        def _(eng):
            q.emit("pool", eng)


def constants():
    c = np.zeros((128, K_W), np.float32)
    c[:, K_ID:K_ID + 128] = np.eye(128, dtype=np.float32)
    c[:, K_IOTA:K_IOTA + 128] = np.arange(128)
    p = np.arange(128)
    k = np.arange(256)
    for t in range(2):
        qp = (t * 128 + p)[:, None]
        causal = k[None, :] <= qp
        c[:, K_MC + 256 * t:K_MC + 256 * t + 256] = np.where(causal, 0.0, NEG)
        dist = qp - k[None, :]
        count = (causal & (dist <= 128)) * 1 + (causal & (dist % 4 == 0)) * 1 + (causal & (dist % 16 == 0)) * 1
        c[:, K_MD + 256 * t:K_MD + 256 * t + 256] = np.where(count > 0, 8.0 * np.log(np.maximum(count, 1)), NEG)
        for dim, kc, ks in ((64, K_CA, K_SA), (32, K_CI, K_SI)):
            inv = np.float32(10000.0) ** (-np.arange(0, dim, 2, dtype=np.float32) / np.float32(dim))
            a = (np.float32(1.0) * qp.astype(np.float32)) * inv.astype(np.float32)[None, :]
            n = dim // 2
            c[:, kc + n * t:kc + n * t + n] = np.cos(a.astype(np.float64))
            c[:, ks + n * t:ks + n * t + n] = np.sin(a.astype(np.float64))
    for rot, o in ((8, 0), (16, 4)):
        h = rot // 2
        c[:, K_INV + o:K_INV + o + h] = np.power(np.float32(500000.0), -np.arange(h, dtype=np.float32) * 2.0 / rot)
    c[:, K_T:K_T + 256] = k
    return c


def slabs(w, width):
    d, n = w.shape
    return w.reshape(d // 128, 128, n // width, width).transpose(2, 1, 0, 3).reshape(n // width, 128, -1)


def feat(v):
    return v.reshape(-1, 128).T


def layout(i):
    a = {}
    x = np.asarray(i["x"])
    a["x"] = x[0].reshape(2, 128, 1024).transpose(1, 0, 2)
    a["pos"] = np.asarray(i["positions"])[0].reshape(2, 128).T
    a["consts"] = constants()
    s = np.zeros((128, S_W), np.float32)
    for j, g in enumerate([i["g_mix"][0], i["g_mix"][1], i["g_ffn"][0], i["g_ffn"][1], i["norm1_g_2"][0], i["norm2_g_2"][0]]):
        s[:, S_G + 8 * j:S_G + 8 * j + 8] = feat(np.asarray(g))
    for l in range(DEPTH):
        cv = np.stack([feat(np.asarray(i["conv_w"][l][j])) for j in range(3)] + [feat(np.asarray(i["conv_b"][l]))], axis=2)
        s[:, S_CONV + 176 * l:S_CONV + 176 * l + 176] = cv.reshape(128, 176)
        for j, n in enumerate(("lambda_q1", "lambda_k1", "lambda_q2", "lambda_k2")):
            s[:, S_LAM + 128 * l + 32 * j:S_LAM + 128 * l + 32 * j + 32] = np.asarray(i[n])[l]
        s[:, S_GD + 64 * l:S_GD + 64 * l + 64] = np.asarray(i["g_diff"])[l]
    s[:, S_DSK:S_DSK + 4] = feat(np.asarray(i["d_skip_2"])[0])
    s[:, S_LDT:S_LDT + 16] = np.repeat(np.asarray(i["log_dt_2"])[0].reshape(16, 2), 64, axis=1).T
    s[:, S_ARE:S_ARE + 16] = np.asarray(i["a_re_2"])[0].reshape(16, 128).T
    s[:, S_AIM:S_AIM + 16] = np.asarray(i["a_im_2"])[0].reshape(16, 128).T
    a["smalls"] = s
    w_in = np.asarray(i["w_in"])
    a["win"] = np.stack([slabs(w_in[l], 512) for l in range(DEPTH)])
    a["wout"] = np.stack([slabs(np.asarray(i["w_out"])[l], 512) for l in range(DEPTH)])
    ups = []
    for l in range(DEPTH):
        w = np.asarray(i["w_up"])[l].reshape(8, 128, 2, 11, 256)
        ups.append(w.transpose(3, 1, 0, 2, 4).reshape(11, 128, 4096))
    a["wup"] = np.stack(ups)
    wd = np.zeros((DEPTH, 24, 128, 1024), np.float32)
    wd[:, 0:NTILE] = np.asarray(i["w_down"]).reshape(DEPTH, NTILE, 128, 1024)
    a["wdown"] = wd.reshape(DEPTH, 6, 4, 128, 1024).transpose(0, 1, 3, 2, 4).reshape(DEPTH, 6, 128, 4096)
    a["rows"] = np.stack([np.broadcast_to(np.asarray(g), (128, 1024)) for g in (i["g_final"], i["norm_f_g_2"])])
    w2 = np.asarray(i["w_in_2"])[0]
    a["win2"] = np.concatenate([slabs(w2[:, 0:1536], 512), slabs(w2[:, 1576:3624], 512)])
    a["wqk"] = slabs(w2[:, 1536:1576], 40)[0]
    sw = np.zeros((4, 16, 2, 64, 2, 16), np.float32)
    for j, n in enumerate(("b_re_2", "b_im_2")):
        b = np.asarray(i[n])[0].reshape(16, 2, 64, 16)
        for g in range(2):
            sw[j, :, g, :, g, :] = b[:, g]
    for j, n in enumerate(("c_re_2", "c_im_2")):
        c = np.asarray(i[n])[0].reshape(16, 2, 16, 64).transpose(0, 1, 3, 2)
        for g in range(2):
            sw[2 + j, :, g, :, g, :] = c[:, g]
    a["wsm"] = sw.reshape(4, 16, 128, 32).transpose(2, 0, 1, 3).reshape(128, 2048)
    a["wglu"] = slabs(np.asarray(i["w_glu_2"])[0], 512)[0]
    a["wsu"] = slabs(np.asarray(i["w_ssm_up_2"])[0], 1024)[0]
    a["wau"] = slabs(np.asarray(i["w_attn_up_2"])[0], 1024)[0]
    a["wout2"] = slabs(np.asarray(i["w_out_2"])[0], 512)
    a["wpq"] = slabs(np.asarray(i["peer_wq_2"])[0], 512)
    keys = np.stack([np.asarray(i["peer_k1_2"])[0], np.asarray(i["peer_k2_2"])[0]], axis=1)
    a["keys"] = keys.reshape(16, 128, 128).transpose(2, 0, 1).reshape(128, 2048)
    u = np.asarray(i["peer_u_2"])[0].reshape(128, 32, 4, 8, 128)
    a["ut"] = u.transpose(1, 4, 2, 3, 0).reshape(32, 128, 4096)
    v = np.asarray(i["peer_v_2"])[0].reshape(128, 32, 4096)
    a["vt"] = v.transpose(1, 0, 2)
    return a


_ORDER = ["x", "pos", "consts", "smalls", "win", "wout", "wup", "wdown", "rows", "win2", "wqk", "wsm", "wglu", "wsu",
          "wau", "wout2", "wpq", "keys", "ut", "vt"]


def kernel(**inputs):
    import concourse.bacc as _bacc
    from concourse.bass_utils import run_bass_kernel_spmd as _run

    nc = _bacc.Bacc("TRN2", target_bir_lowering=False, num_devices=1)
    made = layout(inputs)
    arrays, args = {}, []
    for name in _ORDER:
        a = np.ascontiguousarray(made[name])
        arrays[f"in_{name}_dram"] = a
        args.append(nc.dram_tensor(f"in_{name}_dram", a.shape, mybir.dt.from_np(a.dtype), kind="ExternalInput").ap())
    out = nc.dram_tensor("out_0_dram", (256, 1024), F32, kind="ExternalOutput").ap()
    program(nc, *args, out)
    r = _run(nc, [arrays], core_ids=[0])
    return r.results[0]["out_0_dram"].reshape(1, 256, 1024)
```

```python
import math
from contextlib import ExitStack

import numpy as np
import concourse.bass as bass
from concourse import mybir

F32 = mybir.dt.float32
F32R = mybir.dt.float32r
I32 = mybir.dt.int32
U32 = mybir.dt.uint32
BF16 = mybir.dt.bfloat16
ALU = mybir.AluOpType
ACTF = mybir.ActivationFunctionType
AX = mybir.AxisListType.X

EPS = 1e-6
NEG = -1e30
TAKEN = -3e38
MAGIC = 12582912.0
TWO_PI = 6.283185307179586
C1 = 6.28125
C2 = float(np.float32(TWO_PI - C1))
C3 = TWO_PI - C1 - C2
SIN_SCALE = 6.283185
DEPTH = 2
NTILE = 22
LAM_INIT = [0.8 - 0.6 * math.exp(-0.3 * layer) for layer in range(DEPTH)]

K_ID, K_IOTA, K_MC, K_MD, K_CA, K_SA, K_CI, K_SI, K_INV, K_T = 0, 128, 256, 768, 1280, 1344, 1408, 1440, 1472, 1484
K_W = K_T + 256
S_G = 0
S_CONV = 48
S_LAM = S_CONV + 2 * 176
S_GD = S_LAM + 256
S_DSK = S_GD + 128
S_LDT = S_DSK + 4
S_ARE = S_LDT + 16
S_AIM = S_ARE + 16
S_W = S_AIM + 16


class Op:

    def __init__(self, eng, fn, after, sem=None, inc=1):
        self.eng, self.fn, self.after, self.sem, self.inc = eng, fn, after, sem, inc
        self.val, self.need = 0, sem is not None


def flat(xs):
    out = []
    for x in xs:
        if isinstance(x, (list, tuple)):
            out += flat(x)
        elif x is not None:
            out.append(x)
    return out


class Queues:

    def __init__(self):
        self.ops = {e: [] for e in ("pe", "act", "dve", "pool", "sp")}
        self.dma_count = {}

    def put(self, eng, fn, after):
        op = Op(eng, fn, flat(after))
        for a in op.after:
            a.need = True
        self.ops[eng].append(op)
        return op

    def dma(self, eng, out, in_, sem, after):
        op = Op(eng, lambda e: e.dma_start(out, in_), flat(after), sem, 16)
        for a in op.after:
            a.need = True
        self.dma_count[sem.name] = self.dma_count.get(sem.name, 0) + 16
        op.val = self.dma_count[sem.name]
        self.ops[eng].append(op)
        return op

    def number(self, sems):
        for name, ops in self.ops.items():
            n = 0
            for op in ops:
                if op.sem is None and op.need:
                    n += 1
                    op.sem, op.val = sems[name], n

    def emit(self, name, eng):
        seen = {}
        for op in self.ops[name]:
            for a in op.after:
                if seen.get(a.sem.name, 0) < a.val:
                    eng.wait_ge(a.sem, a.val)
                    seen[a.sem.name] = a.val
            ins = op.fn(eng)
            if op.need:
                ins.then_inc(op.sem, op.inc)


def program(nc, x_d, pos_d, consts_d, smalls_d, win_d, wout_d, wup_d, wdown_d, rows_d, wu_d, wqkv_d, wqk_d, wga_d, wsm_d,
            wglu_d, wsu_d, wau_d, wout2_d, wpq_d, keys_d, ut_d, vt_d, out_d, spill_d):
    with ExitStack() as ctx:
        def sb(name, n, dt=F32):
            return ctx.enter_context(nc.sbuf_tensor(name, [128, n], dt))

        def scoped(where, name, n, dt=F32):
            return where.enter_context(nc.sbuf_tensor(name, [128, n], dt))

        xs = sb("xs", 2048)
        ids = sb("ids", 128)
        hh, hl = sb("hh", 2048, F32R), sb("hl", 2048, F32R)
        sta = sb("sta", 760)
        raws = [sb(f"raw{i}", 1024) for i in range(4)]
        whs = [sb(f"wh{i}", 1024, F32R) for i in range(4)]
        wls = [sb(f"wl{i}", 1024, F32R) for i in range(4)]
        early = ExitStack()
        con_s = scoped(early, "con", K_W - 128)
        sml_s = scoped(early, "sml", S_W)
        tab_s = scoped(early, "tab", 8192)
        raws += [scoped(early, f"raw{i}", 1024) for i in (4, 5)]
        whs += [scoped(early, f"wh{i}", 1024, F32R) for i in (4, 5)]
        wls += [scoped(early, f"wl{i}", 1024, F32R) for i in (4, 5)]
        banks = [ctx.enter_context(nc.psum_tensor(f"bank{i}", [128, 512], F32)) for i in range(8)]
        sems = {e: ctx.enter_context(nc.semaphore(f"s_{e}")) for e in ("pe", "act", "dve", "pool", "sp")}
        slot_sem = [ctx.enter_context(nc.semaphore(f"s_slot{i}")) for i in range(6)]
        s_x, s_pos, s_id, s_k, s_sm, s_ssm, s_ssc, s_out, s_spill, s_back = [
            ctx.enter_context(nc.semaphore(n)) for n in ("s_x", "s_pos", "s_id", "s_k", "s_sm", "s_ssm", "s_ssc", "s_out", "s_spill", "s_back")]

        q = Queues()

        def PE(fn, *after):
            return q.put("pe", fn, after)

        def ACT(fn, *after):
            return q.put("act", fn, after)

        def DVE(fn, *after):
            return q.put("dve", fn, after + tuple(q.ops["dve"][-1:]))

        def POOL(fn, *after):
            return q.put("pool", fn, after + tuple(q.ops["pool"][-1:]))

        def tt(E, out, a, b, op, *after):
            return E(lambda e: e.tensor_tensor(out, a, b, op), *after)

        def ts(E, out, a, s1, s2, op0, op1, *after):
            if op1 is None:
                return E(lambda e: e.tensor_scalar(out, a, s1, None, op0), *after)
            return E(lambda e: e.tensor_scalar(out, a, s1, s2, op0, op1), *after)

        def stt(out, a, s, b, op0, op1, *after):
            return DVE(lambda e: e.scalar_tensor_tensor(out, a, s, b, op0, op1), *after)

        def act(out, a, f, *after, **kw):
            return ACT(lambda e: e.activation(out, a, f, **kw), *after)

        def copy(i, out, a, *after):
            if i % 2:
                return ACT(lambda e: e.activation(out, a, ACTF.Copy), *after)
            return DVE(lambda e: e.tensor_copy(out, a), *after)

        def mm(out, pairs, *after):
            t = None
            for i, (l, r) in enumerate(pairs):
                t = PE(lambda e, l=l, r=r, i=i: e.matmul(out, l, r, start=i == 0, stop=i == len(pairs) - 1),
                       *(after if i == 0 else ()))
            return t

        def tr(out, a, *after):
            return PE(lambda e: e.transpose(out, a, ids[:, :]), *after)

        free = [[] for _ in range(8)]
        turn = [0]

        def bank(of=range(8)):
            of = list(of)
            turn[0] += 1
            return of[turn[0] % len(of)]

        def quarters(w):
            return [(w[:, h * 1024:h * 1024 + 1024], 1024, True) for h in range(w.shape[1] // 1024)]

        plan = []
        for layer in range(DEPTH):
            for n in range(6):
                plan += quarters(win_d[layer, n])
            for n in range(2):
                plan += quarters(wout_d[layer, n])
            plan += [(wup_d[layer, f], 1024, True) for f in range(2 * NTILE)]
            plan += [(wdown_d[layer, f], 1024, True) for f in range(NTILE)]
        plan += [(rows_d[0], 1024, False)]
        plan += [(wu_d[n], 1024, True) for n in range(4)]
        plan += quarters(wqkv_d[0]) + quarters(wqkv_d[1])
        plan += [(wqk_d, 320, True)]
        for n in range(4):
            plan += quarters(wga_d[n])
        plan += [(wglu_d[n], 1024, True) for n in range(2)]
        plan += quarters(wsu_d[0]) + quarters(wsu_d[1])
        plan += quarters(wau_d[0]) + quarters(wau_d[1])
        plan += quarters(wout2_d[0]) + quarters(wout2_d[1])
        plan += [(wpq_d[n], 1024, True) for n in range(16)]
        plan += [(keys_d[:, h * 1024:h * 1024 + 1024], 1024, False) for h in range(2)]
        n_early = len(plan)
        plan += [(ut_d[n], 1024, True) for n in range(128)]
        plan += [(vt_d[n], 1024, True) for n in range(128)]
        plan += [(rows_d[1], 1024, False)]
        split_at = []
        for i, p in enumerate(plan):
            split_at.append(0 if i in (0, n_early) else split_at[-1] + plan[i - 1][2])
        raw_free = [[] for _ in raws]
        w_free = [[] for _ in whs]
        raw_busy = [False] * 6
        w_busy = [False] * 6
        units = {}
        st = {"ahead": 0, "at": 0, "lo": ["dve"], "used": None}

        def prefetch():
            i = st["ahead"]
            if i >= len(plan):
                return
            src, n, split = plan[i]
            first, depth = (0, 6) if i < n_early else (n_early, 4)
            r = (i - first) % depth
            s_ = split_at[i] % depth
            if raw_busy[r] or (split and w_busy[s_]):
                return
            st["ahead"] = i + 1
            raw = raws[r][:, 0:n]
            t = q.dma("sp", raw, src, slot_sem[r], [raw_free[r]])
            if not split:
                raw_busy[r] = True
                units[i] = (raw, None, t, r)
                return
            w_busy[s_] = True
            wh, wl = whs[s_][:, 0:n], wls[s_][:, 0:n]
            hi = act(wh, raw, ACTF.Copy, t, w_free[s_])
            E = {"dve": DVE, "pool": POOL}[st["lo"][i % len(st["lo"])]]
            lo = tt(E, wl, raw, wh.bitcast(F32), ALU.subtract, hi, t, w_free[s_])
            raw_free[r] = [lo, hi]
            units[i] = (wh, wl, lo, s_)

        def take():
            i = st["at"]
            st["at"] = i + 1
            assert i < st["ahead"]
            return units.pop(i)

        def mm3(out, lhs, rhs, start, stop, *after):
            t = None
            n = len(lhs)
            for i in range(n):
                for j, (a, b) in enumerate(((0, 0), (0, 1), (1, 0))):
                    t = PE(lambda e, l=lhs[i][a], r=rhs[i][b], i=i, j=j: e.matmul(
                        out, l, r, start=start and i == 0 and j == 0, stop=stop and i == n - 1 and j == 2),
                        *(after if i == 0 and j == 0 else ()))
            return t

        def halves(dh, dl, src, *after):
            a = act(dh, src, ACTF.Copy, *after)
            return tt(DVE, dl, src, dh.bitcast(F32), ALU.subtract, a, *after)

        x = xs[:, :].rearrange("p (t d) -> p t d", t=2)
        hTh = hh[:, :].rearrange("p (k t) -> p k t", k=8)
        hTl = hl[:, :].rearrange("p (k t) -> p k t", k=8)
        cosT = tab_s[:, 0:4096].rearrange("p (n t) -> p n t", n=16)
        sinT = tab_s[:, 4096:8192].rearrange("p (n t) -> p n t", n=16)
        sta_at = [0]

        def stat(n):
            o = sta_at[0]
            sta_at[0] += n
            assert sta_at[0] <= 760
            return sta[:, o:o + n]

        def con(c, n):
            return con_s[:, c - 128:c - 128 + n]

        def sml(c, n):
            return sml_s[:, c:c + n]

        def hT(k, cols):
            return hTh[:, k, cols], hTl[:, k, cols]

        iota = con(K_IOTA, 128)
        maskC = con(K_MC, 512).rearrange("p (t k) -> p t k", t=2)
        maskD = con(K_MD, 512).rearrange("p (t k) -> p t k", t=2)

        ld_x = q.dma("act", xs[:, :].rearrange("p (t d) -> p t d", t=2), x_d, s_x, [])
        pos_i = stat(2).bitcast(I32)
        ld_pos = q.dma("act", pos_i, pos_d, s_pos, [])
        ld_id = q.dma("act", ids[:, :], consts_d[:, 0:128], s_id, [])
        ld_k = q.dma("act", con_s[:, :], consts_d[:, 128:K_W], s_k, [])
        ld_s = q.dma("act", sml(0, S_W), smalls_d, s_sm, [])

        neghalf = stat(8)
        c0 = POOL(lambda e: e.memset(neghalf, -0.5))
        ss = stat(2)
        ms = stat(2)
        rstd = stat(2)

        def rms_rstd(src, junk, t, scale, *after):
            a = act(junk, src, ACTF.Square, *after, accum_out=ss[:, t:t + 1])
            b = ts(DVE, ms[:, t:t + 1], ss[:, t:t + 1], scale, EPS, ALU.mult, ALU.add, a)
            return tt(POOL, rstd[:, t:t + 1], ms[:, t:t + 1], neghalf[:, 0:1], ALU.pow, b, c0)

        def transposed(src, ncol, evac, *after):
            done = []
            for t in range(2):
                for k0 in range(0, ncol, 4):
                    n = min(4, ncol - k0)
                    b = bank()
                    for k in range(n):
                        w = tr(banks[b][:, k * 128:(k + 1) * 128], src[:, t, (k0 + k) * 128:(k0 + k + 1) * 128],
                               *(list(after) + [free[b]] if k == 0 else []))
                    e = evac(t, k0, n, banks[b][:, 0:n * 128].rearrange("p (k c) -> p k c", k=n), w)
                    free[b] = [e]
                    done.append(e)
            return done

        def norm_T(g, buf, *after):
            outs = []
            for t in range(2):
                p = rms_rstd(x[:, t, :], buf[:, t, :], t, 1.0 / 1024, *after)
                outs.append(ts(DVE, buf[:, t, :], x[:, t, :], rstd[:, t:t + 1], None, ALU.mult, None, p))

            def evac(t, k0, n, ps, w):
                d = tt(DVE, ps, ps, g[:, k0:k0 + n].unsqueeze(2).broadcast_to([128, n, 128]), ALU.mult, w, ld_s)
                cols = slice(t * 128, (t + 1) * 128)
                return halves(hTh[:, k0:k0 + n, cols], hTl[:, k0:k0 + n, cols], ps, d)

            return transposed(buf, 8, evac, outs, ld_id)

        def halves_evac(k_off=0):
            def evac(t, k0, n, ps, w):
                ks, cols = slice(k_off + k0, k_off + k0 + n), slice(t * 128, (t + 1) * 128)
                return halves(hTh[:, ks, cols], hTl[:, ks, cols], ps, w)
            return evac

        iot = stat(128)

        def first_norm(buf):
            h_tok = norm_T(sml(S_G, 8), buf, ld_x)
            for _ in range(6):
                prefetch()
            opening()
            return h_tok

        posf = stat(2)
        ang, ra, rb, rn = stat(24), stat(24), stat(24), stat(24)
        cosP, sinP = stat(24), stat(24)
        def reduced(E, out, src, tmp, quarter, *after):
            d = ts(E, tmp, src, 1.0 / TWO_PI, quarter, ALU.mult, ALU.add, *after)
            d = ts(E, tmp, tmp, MAGIC, None, ALU.add, None, d)
            n = ts(E, tmp, tmp, MAGIC, None, ALU.subtract, None, d)
            d = n
            cur = src
            for c in (C1, C2, C3):
                d = stt(out, tmp, -c, cur, ALU.mult, ALU.add, d)
                cur = out
            if quarter:
                d = ts(E, out, out, math.pi / 2, None, ALU.add, None, d)
            return ts(E, out, out, 3.1415925, -3.1415925, ALU.min, ALU.max, d)

        ldt, are, aim = sml(S_LDT, 16), sml(S_ARE, 16), sml(S_AIM, 16)
        dt_, xr, th, rr, fr = [stat(16) for _ in range(5)]
        sn, cn, sh, e1, kr, ki = [stat(16) for _ in range(6)]
        t16 = [stat(16) for _ in range(4)]

        def state_constants():
            a_dt = act(dt_, ldt, ACTF.Exp, ld_s)
            d = tt(DVE, xr, are, dt_, ALU.mult, a_dt)
            d = tt(DVE, th, aim, dt_, ALU.mult, a_dt)
            d = reduced(DVE, t16[0], th, t16[1], 0.0, d)
            sred = d
            d = ts(DVE, fr, t16[0], 1.0 / TWO_PI, None, ALU.mult, None, d)
            f_tok = d
            d = reduced(DVE, t16[2], th, t16[1], 0.25, d)
            cred = d
            a_ex = act(rr, xr, ACTF.Exp, d)
            a_sn = act(sn, t16[0], ACTF.Sin, sred)
            a_sh = act(sh, t16[0], ACTF.Sin, sred, scale=0.5)
            a_cn = act(cn, t16[2], ACTF.Sin, cred)
            d = ts(DVE, t16[1], xr, 0.5, -0.5, ALU.min, ALU.max, a_cn)
            d = ts(DVE, e1, t16[1], 1.0 / 9, 1.0, ALU.mult, ALU.add, d)
            for c in (8, 7, 6, 5, 4, 3, 2):
                d = tt(DVE, e1, e1, t16[1], ALU.mult, d)
                d = ts(DVE, e1, e1, 1.0 / c, 1.0, ALU.mult, ALU.add, d)
            d = tt(DVE, e1, e1, t16[1], ALU.mult, d)
            d = tt(DVE, t16[2], t16[1], xr, ALU.is_equal, d)
            d = ts(DVE, t16[3], rr, -1.0, None, ALU.add, None, d, a_ex)
            msk = t16[2].bitcast(I32)
            d = DVE(lambda e: e.copy_predicated(t16[3], msk, e1), d)
            d = ts(DVE, rr, t16[3], 1.0, None, ALU.add, None, d)
            d = tt(DVE, kr, t16[3], cn, ALU.mult, d)
            d = tt(DVE, t16[0], sh, sh, ALU.mult, d, a_sh)
            d = stt(kr, t16[0], -2.0, kr, ALU.mult, ALU.add, d)
            d = tt(DVE, ki, rr, sn, ALU.mult, d)
            d = tt(DVE, t16[0], are, are, ALU.mult, d)
            d = tt(DVE, t16[1], aim, aim, ALU.mult, d)
            d = tt(DVE, t16[0], t16[0], t16[1], ALU.add, d)
            d = DVE(lambda e: e.reciprocal(t16[0], t16[0]), d)
            d = tt(DVE, t16[1], kr, are, ALU.mult, d)
            d = tt(DVE, t16[2], ki, aim, ALU.mult, d)
            d = tt(DVE, t16[1], t16[1], t16[2], ALU.add, d)
            d = tt(DVE, t16[2], ki, are, ALU.mult, d)
            d = tt(DVE, t16[3], kr, aim, ALU.mult, d)
            d = tt(DVE, t16[2], t16[2], t16[3], ALU.subtract, d)
            d = tt(DVE, kr, t16[1], t16[0], ALU.mult, d)
            k_tok = tt(DVE, ki, t16[2], t16[0], ALU.mult, d)
            return f_tok, k_tok

        def phase_tables(groups, f_tok, ptmp):
            tv = con(K_T, 256).unsqueeze(1).broadcast_to([128, 2, 256])
            p = None
            for n in groups:
                fb = fr[:, n:n + 2].unsqueeze(2).broadcast_to([128, 2, 256])
                for tab, quarter in ((sinT, 0.0), (cosT, 0.25)):
                    o = tab[:, n:n + 2, :]
                    p = tt(POOL, o, tv, fb, ALU.mult, f_tok, ld_k, p)
                    if quarter:
                        p = ts(POOL, o, o, quarter, None, ALU.add, None, p)
                    p = ts(POOL, ptmp, o, MAGIC, None, ALU.add, None, p)
                    p = ts(POOL, ptmp, ptmp, MAGIC, None, ALU.subtract, None, p)
                    p = tt(POOL, o, o, ptmp, ALU.subtract, p)
            return p


        lam = [stat(1) for _ in range(DEPTH)]
        lj, l1, l2 = stat(32), stat(1), stat(1)
        gd = [sml(S_GD + 64 * i, 64) for i in range(DEPTH)]
        rope_tok, lam_tok = [], []

        def opening():
            d = DVE(lambda e: e.tensor_copy(posf, pos_i), ld_pos)
            a3 = ang.rearrange("p (t f) -> p t f", t=2)
            inv3 = con(K_INV, 12).unsqueeze(1).broadcast_to([128, 2, 12])
            d = tt(DVE, a3, posf.unsqueeze(2).broadcast_to([128, 2, 12]), inv3, ALU.mult, d, ld_k)
            r1 = reduced(DVE, ra, ang, rn, 0.0, d)
            r2 = reduced(DVE, rb, ang, rn, 0.25, r1)
            a_s = act(sinP, ra, ACTF.Sin, r1)
            a_s = act(cosP, rb, ACTF.Sin, r2)
            d = DVE(lambda e: e.tensor_copy(iot, iota), ld_k)
            rope_tok.append(a_s)
            last = None
            for i in range(DEPTH):
                v = [sml(S_LAM + 128 * i + 32 * j, 32) for j in range(4)]
                d1 = DVE(lambda e, v=v: e.tensor_tensor_reduce(lj, v[0], v[1], 1.0, 0.0, ALU.mult, ALU.add, l1), ld_s, last)
                d2 = DVE(lambda e, v=v: e.tensor_tensor_reduce(lj, v[2], v[3], 1.0, 0.0, ALU.mult, ALU.add, l2), d1)
                a1 = act(l1, l1, ACTF.Exp, d2)
                a2 = act(l2, l2, ACTF.Exp, a1)
                d = tt(DVE, l1, l1, l2, ALU.subtract, a2)
                d = ts(DVE, lam[i], l1, LAM_INIT[i], None, ALU.add, None, d)
                d = ts(DVE, gd[i], gd[i], 1.0 - LAM_INIT[i], None, ALU.mult, None, d)
                last = d
            lam_tok.append(last)

        def rope(E, view, half, cos, sin, tmp, *after):
            u = view.shape[2]
            n = 2 * u * half
            ts4 = [tmp[:, i * n:(i + 1) * n].rearrange("p (t u f) -> p t u f", t=2, u=u) for i in range(4)]
            x1, x2 = view[:, :, :, 0:half], view[:, :, :, half:2 * half]
            cb = cos.unsqueeze(2).broadcast_to([128, 2, u, half])
            sn_ = sin.unsqueeze(2).broadcast_to([128, 2, u, half])
            tt(E, ts4[0], x1, cb, ALU.mult, *after)
            o2 = tt(E, ts4[1], x2, sn_, ALU.mult)
            tt(E, ts4[2], x2, cb, ALU.mult)
            o4 = tt(E, ts4[3], x1, sn_, ALU.mult)
            o5 = tt(E, x1, ts4[0], ts4[1], ALU.subtract, o4)
            return tt(E, x2, ts4[2], ts4[3], ALU.add, o4)

        NB = 4
        mx = stat(20)
        den = stat(20)
        rden = stat(20)
        rlam = stat(4)

        def attend(buf, maps, t, *after):
            nk = t + 1
            n = len(maps)
            bsm, bE, bET = [[buf[:, 1024 * j + 256 * i:1024 * j + 256 * i + 256] for i in range(NB)] for j in range(3)]
            s_t, m_t, e_t, tr_t, c_t, pv_t = ({} for _ in range(6))

            def scores(i):
                qT, kT, v, mask, scale, o = maps[i]
                b = i % 2
                s_t[i] = mm(banks[b][:, 0:128 * nk], [(qT, kT)], free[b], after)
                m_t[i] = DVE(lambda e: e.tensor_tensor_reduce(
                    bsm[i % NB][:, 0:128 * nk], banks[b][:, 0:128 * nk], mask, -scale, 3e38, ALU.add, ALU.min,
                    mx[:, i:i + 1]), s_t[i], e_t.get(i - NB), after if i == 0 else None)
                free[b] = [m_t[i]]
                e_t[i] = act(bE[i % NB][:, 0:128 * nk], bsm[i % NB][:, 0:128 * nk], ACTF.Exp, m_t[i], tr_t.get(i - NB),
                             bias=mx[:, i:i + 1], scale=-1.0, accum_out=den[:, i:i + 1])

            def turned(i):
                b = 2 + i % 2
                for k in range(nk):
                    tr_t[i] = tr(banks[b][:, 128 * k:128 * k + 128], bE[i % NB][:, 128 * k:128 * k + 128],
                                 e_t[i], free[b])
                c_t[i] = copy(i, bET[i % NB][:, 0:128 * nk], banks[b][:, 0:128 * nk], tr_t[i], pv_t.get(i - NB))
                free[b] = [c_t[i]]

            def pv(i):
                qT, kT, v, mask, scale, (ob, oc) = maps[i]
                first = oc == 0
                pv_t[i] = mm(banks[ob][:, oc:oc + 64],
                             [(bET[i % NB][:, 128 * k:128 * k + 128], v(k)) for k in range(nk)],
                             c_t[i], free[ob] if first else None)

            for i in range(n + 4):
                if i < n:
                    scores(i)
                if 0 <= i - 2 < n:
                    turned(i - 2)
                if 0 <= i - 4 < n:
                    pv(i - 4)
            return pv_t[n - 1], e_t[n - 1]

        ALLC = slice(0, 256)

        class Unit:

            def __init__(self, k):
                wh, wl, self.tok, self.slot = take()
                self.plain = wl is None
                if not self.plain:
                    self.h, self.l = (w.rearrange("p (k c) -> p k c", k=k) for w in (wh, wl))
                else:
                    self.h = wh

            def pair(self, k, cols):
                return self.h[:, k, cols], self.l[:, k, cols]

            def used(self, m):
                before, st["used"] = st["used"], (self, m)
                if before:
                    u, m = before
                    if u.plain:
                        raw_free[u.slot] = [m]
                        raw_busy[u.slot] = False
                    else:
                        w_free[u.slot] = [m]
                        w_busy[u.slot] = False
                    prefetch()
                    prefetch()

        def tcols(t):
            return slice(t * 128, (t + 1) * 128)

        def by_tokens(n_slabs, cw, nu, kper, lhs, evac, out, *after, of=range(8)):
            for n in range(n_slabs):
                bs = [bank(of), bank(of)]
                for h in range(nu):
                    u = Unit(kper)
                    for t in range(2):
                        m = mm3(banks[bs[t]][:, 0:cw], [lhs(h * kper + k, tcols(t)) for k in range(kper)],
                                [u.pair(k, slice(0, cw)) for k in range(kper)], h == 0, h == nu - 1,
                                after, u.tok, free[bs[t]] if h == 0 else None)
                        if h == nu - 1:
                            e = evac(n, t, banks[bs[t]][:, 0:cw], m)
                            free[bs[t]] = [e]
                            out.append(e)
                    u.used(m)
                    yield

        def by_features(n_units, kt, lhs, evac, out, *after):
            for n in range(n_units):
                u = Unit(kt)
                c2 = u.h.shape[2] // 128
                for c in range(c2):
                    b = bank()
                    m = mm3(banks[b][:, 0:256], [u.pair(k, tcols(c)) for k in range(kt)],
                            [lhs(k, ALLC) for k in range(kt)], True, True, after, u.tok, free[b])
                    e = evac(c2 * n + c, banks[b][:, 0:256], m)
                    free[b] = [e]
                    out.append(e)
                u.used(m)
                yield

        def run(gen):
            for _ in gen:
                pass

        def add_to_x(n, t, ps, m):
            xv = x[:, t, n * 512:(n + 1) * 512]
            return tt(DVE, xv, xv, ps, ALU.add, m)

        last = [ld_x]
        cosp = cosP.rearrange("p (t f) -> p t f", t=2)
        sinp = sinP.rearrange("p (t f) -> p t f", t=2)
        tab_half = [tab_s[:, :].rearrange("p (a n t) -> p a n t", a=2, n=16)[:, :, 8 * i:8 * i + 8, :] for i in range(2)]
        sc_l = ExitStack()
        mix = scoped(sc_l, "mix", 2048)[:, :].rearrange("p (t d) -> p t d", t=2)
        att = scoped(sc_l, "att", 3072)[:, :]
        headtmp = scoped(sc_l, "headtmp", 512)[:, :]
        for layer in range(DEPTH):
            sc_a = ExitStack()
            qkv = scoped(sc_a, f"qkv{layer}", 6144)[:, :].rearrange("p (t n) -> p t n", t=2)
            qkT = scoped(sc_a, f"qkT{layer}", 4096)[:, :].rearrange("p (k t) -> p k t", k=16)
            ptmp = scoped(sc_a, f"ptmp{layer}", 512)[:, :].rearrange("p (n t) -> p n t", n=2)
            dve_tmp, pool_tmp = att[:, 0:1024], att[:, 1024:1536]
            if layer == 0:
                h_tok = first_norm(mix)
            else:
                h_tok = norm_T(sml(S_G + 8 * layer, 8), mix, last)
            ev = []
            st["lo"] = ["dve", "dve", "pool"]
            run(by_tokens(6, 512, 4, 2, hT,
                          lambda n, t, ps, m: copy(t, qkv[:, t, n * 512:(n + 1) * 512], ps, m), ev, h_tok))
            ev = [ev[2 * n:2 * n + 2] for n in range(6)]
            view = [qkv[:, :, 0:512].rearrange("p t (u d) -> p t u d", d=32),
                    qkv[:, :, 768:1280].rearrange("p t (u d) -> p t u d", d=64),
                    qkv[:, :, 1536:2560].rearrange("p t (u d) -> p t u d", d=64)]
            rA = rope(DVE, view[0], 4, cosp[:, :, 0:4], sinp[:, :, 0:4], dve_tmp, ev[0], rope_tok)
            rB = rope(POOL, view[1], 8, cosp[:, :, 4:12], sinp[:, :, 4:12], pool_tmp, ev[1], ev[2], rope_tok)
            if layer == 0:
                f_tok, k_tok = state_constants()
            rC = rope(DVE, view[2], 8, cosp[:, :, 4:12], sinp[:, :, 4:12], dve_tmp, ev[3], ev[4])
            cols = [128 * j for j in range(4)] + [768 + 128 * j for j in range(4)] + [1536 + 128 * j for j in range(8)]
            qk_tok = []
            for j in range(0, 16, 2):
                b = bank()
                for s in range(2):
                    for t in range(2):
                        w = tr(banks[b][:, s * 256 + t * 128:s * 256 + t * 128 + 128],
                               qkv[:, t, cols[j + s]:cols[j + s] + 128], (rA, rB, rC)[min(j // 4, 2)], free[b])
                e = copy(j // 2, qkT[:, j:j + 2, :], banks[b][:, :].rearrange("p (s t) -> p s t", s=2), w)
                free[b] = [e]
                qk_tok.append(e)
            mix_tok = []
            for t in range(2):
                nk = t + 1
                phase_tok = phase_tables(range(8 * layer + 4 * t, 8 * layer + 4 * t + 4, 2), f_tok, ptmp)
                ob = [(4, 5, 6), (7, 4, 5)][t]
                maps = []
                for u in range(8):
                    o = 32 * (u % 4)
                    maps.append((qkT[o:o + 32, u // 4, tcols(t)], qkT[o:o + 32, 2 + u // 4, 0:128 * nk],
                                 lambda k, u=u: qkv[:, k, 512 + 64 * (u // 2):576 + 64 * (u // 2)],
                                 maskC[:, t, 0:128 * nk], 32 ** -0.5, (ob[0], 64 * u)))
                for h in range(4):
                    o = 64 * (h % 2)
                    maps.append((qkT[o:o + 64, 4 + h // 2, tcols(t)], qkT[o:o + 64, 6 + h // 2, 0:128 * nk],
                                 lambda k, h=h: qkv[:, k, 1280 + 64 * h:1344 + 64 * h],
                                 maskC[:, t, 0:128 * nk], 0.125, (ob[1], 64 * h)))
                for h in range(8):
                    o = 64 * (h % 2)
                    maps.append((qkT[o:o + 64, 8 + h // 2, tcols(t)], qkT[o:o + 64, 12 + h // 2, 0:128 * nk],
                                 lambda k, h=h: qkv[:, k, 2560 + 64 * h:2624 + 64 * h],
                                 maskD[:, t, 0:128 * nk], 0.125, (ob[1 + (h + 4) // 8], 64 * ((h + 4) % 8))))
                pv, ex = attend(att, maps, t, qk_tok, ev, mix_tok)
                d = DVE(lambda e: e.reciprocal(rden, den), ex)
                d = ts(DVE, rlam, rden[:, 1:8:2], lam[layer], None, ALU.mult, None, d, lam_tok)
                oA = banks[ob[0]][:, :].rearrange("p (h c d) -> p h c d", h=4, c=2)
                ta = headtmp[:, 0:256].rearrange("p (h d) -> p h d", h=4)
                tb = headtmp[:, 256:512].rearrange("p (h d) -> p h d", h=4)
                m1 = tt(DVE, ta, oA[:, :, 0, :], rden[:, 0:8:2].unsqueeze(2).broadcast_to([128, 4, 64]), ALU.mult, pv, d)
                m2 = tt(DVE, tb, oA[:, :, 1, :], rlam.unsqueeze(2).broadcast_to([128, 4, 64]), ALU.mult, d)
                free[ob[0]] = [m2]
                d = tt(DVE, ta, ta, tb, ALU.subtract, m2)
                d = tt(DVE, tb, ta, ta, ALU.mult, d)
                d = DVE(lambda e: e.tensor_reduce(rlam, tb, AX, ALU.add), d)
                d = ts(DVE, rlam, rlam, 1.0 / 64, EPS, ALU.mult, ALU.add, d)
                p = tt(POOL, rlam, rlam, neghalf[:, 0:4], ALU.pow, d)
                d1 = tt(DVE, mix[:, t, 256:768].rearrange("p (h d) -> p h d", h=8),
                        banks[ob[1]][:, :].rearrange("p (h d) -> p h d", h=8),
                        rden[:, 8:16].unsqueeze(2).broadcast_to([128, 8, 64]), ALU.mult)
                d2 = tt(DVE, mix[:, t, 768:1024].rearrange("p (h d) -> p h d", h=4),
                        banks[ob[2]][:, 0:256].rearrange("p (h d) -> p h d", h=4),
                        rden[:, 16:20].unsqueeze(2).broadcast_to([128, 4, 64]), ALU.mult)
                free[ob[1]] = [d1]
                free[ob[2]] = [d2]
                d = tt(DVE, ta, ta, rlam.unsqueeze(2).broadcast_to([128, 4, 64]), ALU.mult, p)
                d = tt(DVE, mix[:, t, 0:256].rearrange("p (h d) -> p h d", h=4), ta,
                       gd[layer].unsqueeze(1).broadcast_to([128, 4, 64]), ALU.mult, d)
                mix_tok = [d]
            mT = transposed(mix, 8, halves_evac(), mix_tok)
            x_tok = []
            run(by_tokens(2, 512, 4, 2, hT, add_to_x, x_tok, mT))
            sc_a.close()
            sc_f = ExitStack()
            yTh, yTl = [scoped(sc_f, f"y{c}{layer}", NTILE * 256, F32R)[:, :].rearrange("p (k t) -> p k t", k=NTILE)
                        for c in "hl"]
            cbuf = att
            cb = [[cbuf[:, 768 * s + 256 * j:768 * s + 256 * j + 256] for j in range(3)] for s in range(4)]
            h_tok = norm_T(sml(S_G + 16 + 8 * layer, 8), mix, x_tok)
            a_tab = act(tab_half[layer], tab_half[layer], ACTF.Sin, phase_tok, scale=SIN_SCALE)
            cv = sml(S_CONV + 176 * layer, 176).rearrange("p (n j) -> p n j", j=4)
            y_tok, y_mul = {}, {}

            def finish(f):
                a = act(yTh[:, f, :], cb[f % 4][0], ACTF.Copy, y_mul[f])
                y_tok[f] = tt(POOL, yTl[:, f, :], cb[f % 4][0], yTh[:, f, :].bitcast(F32), ALU.subtract, a)

            for f in range(NTILE):
                b = bank()
                for half in range(2):
                    u = Unit(8)
                    m = mm3(banks[b][:, 256 * half:256 * half + 256],
                            [u.pair(k, tcols(0)) for k in range(8)], [hT(k, ALLC) for k in range(8)],
                            True, True, h_tok, u.tok, free[b])
                    if half == 0:
                        u.used(m)
                c = cb[f % 4]
                for half in range(2):
                    col = cv[:, f + NTILE * half, :]
                    ps = banks[b][:, 256 * half:256 * half + 256]
                    a = act(c[half], ps, ACTF.Identity, m, y_tok.get(f - 4), scale=col[:, 2:3], bias=col[:, 3:4])
                    d = stt(c[half][:, 1:256], ps[:, 0:255], col[:, 1:2], c[half][:, 1:256], ALU.mult, ALU.add, a)
                    d = stt(c[half][:, 2:256], ps[:, 0:254], col[:, 0:1], c[half][:, 2:256], ALU.mult, ALU.add, d)
                    if half == 0:
                        sg = act(c[2], c[0], ACTF.Silu, d)
                free[b] = [d]
                y_mul[f] = tt(POOL, c[0], c[2], c[1], ALU.mult, sg, d)
                if f:
                    finish(f - 1)
                u.used(m)
            finish(NTILE - 1)
            st["lo"] = ["dve"]
            acc = [[bank() for _ in range(2)] for _ in range(2)]
            for f in range(NTILE):
                u = Unit(1)
                for t in range(2):
                    for n in range(2):
                        b = acc[t][n]
                        m = mm3(banks[b][:, :], [(yTh[:, f, tcols(t)], yTl[:, f, tcols(t)])],
                                [u.pair(0, slice(n * 512, (n + 1) * 512))], f == 0, f == NTILE - 1,
                                y_tok[f], u.tok, free[b] if f == 0 else None)
                u.used(m)
            last = []
            for t in range(2):
                for n in range(2):
                    b = acc[t][n]
                    e = add_to_x(n, t, banks[b][:, :], m)
                    free[b] = [e]
                    last.append(e)
            sc_f.close()
        sc_l.close()

        sc_2 = ExitStack()

        def S2(name, n):
            return scoped(sc_2, name, n)[:, :]

        gates_s = S2("gates", 4096)
        gates = gates_s.rearrange("p (t n) -> p t n", t=2)
        proj = S2("proj", 2128).rearrange("p (t n) -> p t n", t=2)
        uT = S2("uT", 1024).rearrange("p (i t) -> p i t", i=4)
        qT2 = S2("qT2", 2304).rearrange("p (k t) -> p k t", k=9)
        ssb = S2("ssb", 2560)
        BT = S2("BT", 1024).rearrange("p (j i s) -> p j i s", j=2, i=4)
        cw = S2("cw", 1024)
        gy = S2("gy", 1024).rearrange("p (i t) -> p i t", i=4)
        ssv = S2("ssv", 1536)
        gt2 = ssb[:, 0:512]
        hn = gates_s[:, 0:2048].rearrange("p (t d) -> p t d", t=2)
        ld_b = q.dma("act", ssb[:, 0:1024], wsm_d[:, 0:1024], s_ssm, [last])
        ld_c = q.dma("act", cw, wsm_d[:, 1024:2048], s_ssc, [last])
        u = Unit(1)
        x_tok = []
        for t in range(2):
            p = rms_rstd(x[:, t, :], hn[:, t, :], t, 1.0 / 1024, last)
            x_tok.append(stt(x[:, t, :], x[:, t, :], rstd[:, t:t + 1], u.h, ALU.mult, ALU.mult, p, u.tok))
        u.used(x_tok[-1])
        h_tok = norm_T(sml(S_G + 32, 8), hn, x_tok)
        st["lo"] = ["dve", "pool"]
        Bb = [ssb[:, 512 * j:512 * j + 512].rearrange("p (n c) -> p n c", n=16) for j in range(2)]
        Br = [ssb[:, 1024 + 512 * j:1536 + 512 * j].rearrange("p (n c) -> p n c", n=16) for j in range(2)]
        tmpb = ssb[:, 2048:2560].rearrange("p (n c) -> p n c", n=16)
        Cr, nCi = cw[:, 0:512], cw[:, 512:1024]
        krb = kr.unsqueeze(2).broadcast_to([128, 16, 32])
        kib = ki.unsqueeze(2).broadcast_to([128, 16, 32])
        d = tt(DVE, Br[0], Bb[0], krb, ALU.mult, k_tok, ld_b)
        d = tt(DVE, tmpb, Bb[1], kib, ALU.mult, d)
        d = tt(DVE, Br[0], Br[0], tmpb, ALU.subtract, d)
        d = tt(DVE, Br[1], Bb[1], krb, ALU.mult, d)
        d = tt(DVE, tmpb, Bb[0], kib, ALU.mult, d)
        d = tt(DVE, Br[1], Br[1], tmpb, ALU.add, d)
        nc_tok = ts(DVE, nCi, nCi, -1.0, None, ALU.mult, None, ld_c, d)
        u_tok = []
        run(by_features(4, 8, hT, lambda c, ps, m: copy(c, uT[:, c, :], ps, m), u_tok, h_tok))
        bt_tok = []
        for j in range(2):
            b = bank()
            for i in range(4):
                w = tr(banks[b][:, i * 128:(i + 1) * 128], Br[j][:, 4 * i:4 * i + 4, :].rearrange("p n c -> p (n c)"),
                       d, free[b])
            e = copy(j, BT[:, j], banks[b][:, :].rearrange("p (i s) -> p i s", i=4), w)
            free[b] = [e]
            bt_tok.append(e)

        pr_tok, g_tok = [], []

        def projections():
            yield from by_tokens(2, 512, 4, 2, hT,
                                 lambda n, t, ps, m: act(proj[:, t, n * 512:(n + 1) * 512], ps, ACTF.Copy, m), pr_tok, h_tok, of=low)
            yield from by_tokens(1, 40, 1, 8, hT,
                                 lambda n, t, ps, m: act(proj[:, t, 1024:1064], ps, ACTF.Copy, m), pr_tok, h_tok, of=low)
            yield from by_tokens(4, 512, 4, 2, hT,
                                 lambda n, t, ps, m: act(gates[:, t, n * 512:(n + 1) * 512], ps, ACTF.Sigmoid, m), g_tok, h_tok, of=low)

        st["lo"] = ["dve"]
        low, high = (0, 1, 2, 3), (4, 5, 6, 7)
        fill = projections()
        prod = [ssb[:, 1024 * j:1024 * j + 1024].rearrange("p (a b t) -> p a b t", a=2, b=2) for j in range(2)]
        w_in, z, *states = [a.rearrange("p (a t) -> p a t", a=2) for a in
                            [ssb[:, 2048:2560]] + [ssv[:, 512 * j:512 * j + 512] for j in range(3)]]
        dsk = sml(S_DSK, 4)
        bu_t = {}
        ym = {}
        gy_tok = []

        def bu(n):
            b = 4 + n % 2
            o = 32 * (n % 4)
            for j in range(2):
                m = mm(banks[b][:, 256 * j:256 * j + 256], [(BT[o:o + 32, j, n // 4, :], uT[o:o + 32, n // 4, :])],
                       bt_tok, u_tok, free[b])
            bu_t[n] = (b, m)

        def ssm_out(n):
            yb = 6 + (n // 4) % 2
            o = 32 * (n % 4)
            cc = slice(32 * n, 32 * n + 32)
            xs_ = states[n % 2]
            for j, l in enumerate((Cr, nCi)):
                ym[n] = PE(lambda e, l=l, j=j, o=o, yb=yb, cc=cc, xs_=xs_: e.matmul(
                    banks[yb][o:o + 32, 0:256], l[:, cc], xs_[:, j, :], start=j == 0, stop=j == 1, tile_position=(0, o)),
                    st_tk[n], nc_tok, free[yb] if n % 4 == 0 else None)
            if n % 4 == 3:
                i = n // 4
                d = stt(gy[:, i, :], uT[:, i, :], dsk[:, i:i + 1], banks[yb][:, 0:256], ALU.mult, ALU.add, ym[n])
                free[yb] = [d]
                gy_tok.append(act(gy[:, i, :], gy[:, i, :], ACTF.Gelu_apprx_tanh, d))

        bu(0)
        st_tk, q_tk, z_tk = {}, {}, {}
        for n in range(16):
            if n + 1 < 16:
                bu(n + 1)
            b, m = bu_t[n]
            cs = tab_s[:, :].rearrange("p (a n t) -> p a n t", a=2, n=16)[:, :, n, :]
            csb = cs.unsqueeze(1).broadcast_to([128, 2, 2, 256])
            bv = banks[b][:, :].rearrange("p (a t) -> p a t", a=2)
            d = tt(DVE, prod[0], bv.unsqueeze(2).broadcast_to([128, 2, 2, 256]), csb, ALU.mult, m, a_tab, bt_tok)
            free[b] = [d]
            tt(DVE, w_in[:, 0, :], prod[0][:, 0, 0, :], prod[0][:, 1, 1, :], ALU.add)
            tt(DVE, w_in[:, 1, :], prod[0][:, 1, 0, :], prod[0][:, 0, 1, :], ALU.subtract)
            rb_ = rr[:, n:n + 1].broadcast_to([128, 256])
            for j in range(2):
                d = DVE(lambda e, j=j, rb_=rb_: e.tensor_tensor_scan(z[:, j, :], rb_, w_in[:, j, :], 0.0, ALU.mult, ALU.add),
                        q_tk.get(n - 1))
            q_tk[n] = tt(POOL, prod[1], z.unsqueeze(2).broadcast_to([128, 2, 2, 256]), csb, ALU.mult, d, bt_tok)
            xs_ = states[n % 2]
            tt(POOL, xs_[:, 0, :], prod[1][:, 0, 0, :], prod[1][:, 1, 1, :], ALU.subtract, ym.get(n - 2))
            st_tk[n] = tt(POOL, xs_[:, 1, :], prod[1][:, 0, 1, :], prod[1][:, 1, 0, :], ALU.add)
            if n:
                ssm_out(n - 1)
            next(fill, None)
        ssm_out(15)
        d = st_tk[15]
        st["lo"] = ["pool"]
        att2 = tab_s[:, 0:3072]
        kk_s, ki_s = tab_s[:, 3072:3584], tab_s[:, 3584:3840]
        cosA = con(K_CA, 64).rearrange("p (t f) -> p t f", t=2)
        sinA = con(K_SA, 64).rearrange("p (t f) -> p t f", t=2)
        cosI = con(K_CI, 32).rearrange("p (t f) -> p t f", t=2)
        sinI = con(K_SI, 32).rearrange("p (t f) -> p t f", t=2)
        rQ = rope(DVE, proj[:, :, 0:640].rearrange("p t (u d) -> p t u d", d=64), 32, cosA, sinA, tab_s[:, 0:2560], pr_tok, d)
        rI = rope(POOL, proj[:, :, 768:1056].rearrange("p t (u d) -> p t u d", d=32), 16, cosI, sinI,
                  tab_s[:, 3840:4992], pr_tok, d)
        kk2 = kk_s.rearrange("p (t h r d) -> p t h r d", t=2, h=2, r=2)
        ki4 = ki_s.rearrange("p (t r d) -> p t r d", t=2, r=4)
        dup = []
        for t in range(2):
            dup.append(DVE(lambda e, t=t: e.tensor_copy(
                ki4[:, t], proj[:, t, 1024:1056].unsqueeze(1).broadcast_to([128, 4, 32])), rI))
        for t in range(2):
            kv = proj[:, t, 512:640].rearrange("p (h d) -> p h d", h=2)
            for r in range(2):
                dup.append(DVE(lambda e, t=t, r=r, kv=kv: e.tensor_copy(kk2[:, t, :, r, :], kv), rQ))
        srcs = [proj[:, :, 128 * j:128 * j + 128] for j in range(4)]
        srcs += [kk_s.rearrange("p (t c) -> p t c", t=2)[:, :, 128 * j:128 * j + 128] for j in range(2)]
        srcs += [proj[:, :, 768 + 128 * j:896 + 128 * j] for j in range(2)]
        srcs += [ki_s.rearrange("p (t c) -> p t c", t=2)]
        q_tok = []
        for j in (8, 6, 0, 2, 4):
            b = bank(high)
            ns = min(2, 9 - j)
            for s in range(ns):
                for t in range(2):
                    w = tr(banks[b][:, s * 256 + t * 128:s * 256 + t * 128 + 128], srcs[j + s][:, t, :],
                           rQ, rI, dup, free[b])
            e = act(qT2[:, j:j + ns, :], banks[b][:, 0:256 * ns].rearrange("p (s t) -> p s t", s=ns), ACTF.Copy, w)
            free[b] = [e]
            q_tok.append(e)
        rel = [tab_s[:, 4992 + 256 * j:5248 + 256 * j] for j in range(4)]
        sc = [tab_s[:, 6016 + 256 * t:6272 + 256 * t] for t in range(2)]
        mask2 = [tab_s[:, 6528 + 256 * t:6784 + 256 * t] for t in range(2)]
        m8 = stat(8)
        rel_free = [[] for _ in range(4)]
        sel_tok = []
        for t in range(2):
            nk = t + 1
            d = None
            s_ = sc[t][:, 0:128 * nk]
            for h in range(8):
                b = bank(high)
                o = 32 * (h % 4)
                m = mm(banks[b][:, 0:128 * nk],
                       [(qT2[o:o + 32, 6 + h // 4, tcols(t)], qT2[o:o + 32, 8, 0:128 * nk])], q_tok, free[b])
                r = rel[h % 4][:, 0:128 * nk]
                a = act(r, banks[b][:, 0:128 * nk], ACTF.Relu, m, rel_free[h % 4])
                free[b] = [a]
                wcol = proj[:, t, 1056 + h:1057 + h]
                if h == 0:
                    d = ts(DVE, s_, r, wcol, None, ALU.mult, None, a, pr_tok)
                else:
                    d = stt(s_, r, wcol, s_, ALU.mult, ALU.add, a, d)
                rel_free[h % 4] = [d]
            d = stt(s_, s_, 0.0625, maskC[:, t, 0:128 * nk], ALU.mult, ALU.add, d)
            for r in range(8):
                d = DVE(lambda e, s_=s_: e.max(m8, s_), d)
                d = DVE(lambda e, s_=s_: e.match_replace(s_, m8, s_, TAKEN), d)
            m_ = mask2[t][:, 0:128 * nk]
            d = ts(DVE, m_, s_, -2e38, NEG, ALU.is_gt, ALU.mult, d)
            d = tt(DVE, m_, m_, maskC[:, t, 0:128 * nk], ALU.add, d)
            sel_tok.append(d)
        run(fill)
        st["lo"] = ["dve", "pool"]
        gyl = []
        for i in range(4):
            gyl.append(halves(hTh[:, i, :], hTl[:, i, :], gy[:, i, :], gy_tok, g_tok))
        ys_tok = []

        def glu(c, ps, m):
            a = act(ps, ps, ACTF.Sigmoid, m)
            tmp = gt2[:, 256 * (c % 2):256 * (c % 2) + 256]
            d = tt(DVE, tmp, gy[:, c, :], ps, ALU.mult, a, ys_tok[-2:])
            ys_tok.append(halves(hTh[:, 4 + c, :], hTl[:, 4 + c, :], tmp, d))
            return d

        run(by_features(2, 4, hT, glu, [], gyl))
        me_tok = []

        def gated(which):
            def evac(n, t, ps, m):
                sl = gates[:, t, which * 1024 + n * 512:which * 1024 + (n + 1) * 512]
                d = tt(DVE, sl, ps, sl, ALU.mult, m, g_tok)
                if which:
                    s0 = gates[:, t, n * 512:(n + 1) * 512]
                    d2 = tt(DVE, s0, s0, sl, ALU.add, d)
                    me_tok.append(d2)
                return d
            return evac

        run(by_tokens(2, 512, 2, 2, lambda k, c: hT(4 + k, c), gated(0), [], ys_tok))
        ya = tab_s[:, 7040:8064].rearrange("p (t n) -> p t n", t=2)
        ya_tok = []
        for t in range(2):
            nk = t + 1
            maps = []
            for h in range(8):
                o = 64 * (h % 2)
                maps.append((qT2[o:o + 64, h // 2, tcols(t)], qT2[o:o + 64, 4 + h // 4, 0:128 * nk],
                             lambda k, h=h: proj[:, k, 640 + 64 * (h // 4):704 + 64 * (h // 4)],
                             mask2[t][:, 0:128 * nk], 0.125, (4 + t, 64 * h)))
            pv, ex = attend(att2, maps, t, q_tok, sel_tok[t], ya_tok)
            d = DVE(lambda e: e.reciprocal(rden[:, 0:8], den[:, 0:8]), ex)
            d = tt(DVE, ya[:, t, :].rearrange("p (h d) -> p h d", h=8),
                   banks[4 + t][:, :].rearrange("p (h d) -> p h d", h=8),
                   rden[:, 0:8].unsqueeze(2).broadcast_to([128, 8, 64]), ALU.mult, d, pv)
            free[4 + t] = [d]
            ya_tok = [d]
        ya_h = transposed(ya, 4, halves_evac(), ya_tok)
        run(by_tokens(2, 512, 2, 2, hT, gated(1), [], ya_h))
        mT = transposed(gates, 8, halves_evac(), me_tok)
        x_tok = []
        run(by_tokens(2, 512, 4, 2, hT, add_to_x, x_tok, mT))
        h_tok = norm_T(sml(S_G + 40, 8), gates[:, :, 1024:2048], x_tok)
        spill = q.dma("act", spill_d, xs[:, :], s_spill, [x_tok, h_tok])
        sc_2.close()
        early.close()
        sc_p = ExitStack()
        H_s = scoped(sc_p, "H", 32768)
        ach = [scoped(sc_p, f"ach{j}", 256, F32R)[:, :] for j in range(2)]
        acl = [scoped(sc_p, f"acl{j}", 256, F32R)[:, :] for j in range(2)]
        H = H_s[:, :].rearrange("p (j t) -> p j t", j=128)
        R_AT = 16800
        assert R_AT >= K_W - 128 + S_W + 8192 + 6144
        at = [R_AT]

        def RT(n):
            at[0] += n
            assert at[0] <= 32768
            return H_s[:, at[0] - n:at[0]]

        pqT = RT(4096).rearrange("p (n t) -> p n t", n=16)
        pq_tok = []
        run(by_features(16, 8, hT, lambda c, ps, m: copy(c, pqT[:, c, :], ps, m), pq_tok, h_tok))
        us = [Unit(8), Unit(8)]
        S = RT(4096).rearrange("p (t n c) -> p t n c", t=2, n=16)
        s_tok = []
        for t in range(2):
            for n in range(0, 16, 4):
                b = bank()
                for j in range(4):
                    m = mm(banks[b][:, j * 128:(j + 1) * 128],
                           [(pqT[:, n + j, tcols(t)], us[n // 8].h.rearrange("p (n c) -> p n c", n=8)[:, (n + j) % 8, :])], pq_tok, us[n // 8].tok, free[b])
                e = copy(n // 4, S[:, t, n:n + 4, :], banks[b][:, :].rearrange("p (n c) -> p n c", n=4), m)
                free[b] = [e]
                s_tok.append(e)
        st["lo"] = ["dve", "pool"]
        for u in us:
            u.used(m)
        v16 = RT(256).rearrange("p (n k) -> p n k", n=16)
        i16 = RT(256).bitcast(U32).rearrange("p (n k) -> p n k", n=16)
        if16 = RT(256).rearrange("p (n k) -> p n k", n=16)
        tops = RT(128).rearrange("p (h k) -> p h k", h=8)
        pos = RT(128).bitcast(U32).rearrange("p (h k) -> p h k", h=8)
        pa, pb = RT(128), RT(128)
        pau, pbu = RT(128).bitcast(U32), RT(128).bitcast(U32)
        gt = RT(128).rearrange("p (h k) -> p h k", h=8)
        zs = RT(8)
        sel = RT(256).rearrange("p (a n) -> p a n", a=2)
        cand = RT(2048).rearrange("p (h c) -> p h c", h=8)
        oh = RT(2048).rearrange("p (h k j) -> p h k j", h=8, k=16)
        selG = xs[:, 0:256]
        sel1, sel2 = [xs[:, 256 + 128 * j:384 + 128 * j].bitcast(BF16) for j in range(2)]
        sT_tok = []

        def routing(t, prev, done):
            d = None
            for n in range(16):
                sv = S[:, t, n, :]
                d = DVE(lambda e, n=n, sv=sv: e.max(v16[:, n, 0:8], sv), s_tok, prev)
                d = DVE(lambda e, n=n, sv=sv: e.max_index(i16[:, n, 0:8], v16[:, n, 0:8], sv), d)
                d = DVE(lambda e, n=n, sv=sv: e.match_replace(sv, v16[:, n, 0:8], sv, TAKEN), d)
                d = DVE(lambda e, n=n, sv=sv: e.max(v16[:, n, 8:16], sv), d)
                d = DVE(lambda e, n=n, sv=sv: e.max_index(i16[:, n, 8:16], v16[:, n, 8:16], sv), d)
                yield
            vv = v16.rearrange("p (h c) k -> p h c k", c=2)
            d = tt(DVE, cand.rearrange("p h (i j) -> p h i j", i=16),
                   vv[:, :, 0, :].unsqueeze(3).broadcast_to([128, 8, 16, 16]),
                   vv[:, :, 1, :].unsqueeze(2).broadcast_to([128, 8, 16, 16]), ALU.add, d)
            for h in range(8):
                cv_ = cand[:, h, :]
                d = DVE(lambda e, h=h, cv_=cv_: e.max(tops[:, h, 0:8], cv_), d)
                d = DVE(lambda e, h=h, cv_=cv_: e.max_index(pos[:, h, 0:8], tops[:, h, 0:8], cv_), d)
                d = DVE(lambda e, h=h, cv_=cv_: e.match_replace(cv_, tops[:, h, 0:8], cv_, TAKEN), d)
                d = DVE(lambda e, h=h, cv_=cv_: e.max(tops[:, h, 8:16], cv_), d)
                d = DVE(lambda e, h=h, cv_=cv_: e.max_index(pos[:, h, 8:16], tops[:, h, 8:16], cv_), d)
                yield
            d = tt(DVE, gt, tops, tops[:, :, 0:1].broadcast_to([128, 8, 16]), ALU.subtract, d)
            a = act(gt, gt, ACTF.Exp, d)
            posf_ = pos.rearrange("p h k -> p (h k)")
            d = ts(DVE, pau, posf_, 4, None, ALU.logical_shift_right, None, d)
            d = ts(DVE, pbu, posf_, 15, None, ALU.bitwise_and, None, d)
            d = DVE(lambda e: e.tensor_copy(pa, pau), d)
            d = DVE(lambda e: e.tensor_copy(pb, pbu), d)
            d = DVE(lambda e: e.tensor_copy(if16, i16), d)
            yield
            ifv = if16.rearrange("p (h c) k -> p h c k", c=2)
            for c, pp in ((0, pa), (1, pb)):
                d = tt(DVE, oh, pp.rearrange("p (h k) -> p h k", h=8).unsqueeze(3).broadcast_to([128, 8, 16, 16]),
                       iot[:, 0:16].unsqueeze(1).unsqueeze(1).broadcast_to([128, 8, 16, 16]), ALU.is_equal, d)
                yield
                d = tt(DVE, oh, oh, ifv[:, :, c, :].unsqueeze(2).broadcast_to([128, 8, 16, 16]), ALU.mult, d)
                d = DVE(lambda e, c=c: e.tensor_reduce(sel[:, c, :].rearrange("p (h k) -> p h k", h=8), oh, AX, ALU.add), d)
                yield
            d = DVE(lambda e: e.tensor_reduce(zs, gt, AX, ALU.add), a, d)
            d = DVE(lambda e: e.reciprocal(zs, zs), d)
            done.append(tt(DVE, gt, gt, zs.unsqueeze(2).broadcast_to([128, 8, 16]), ALU.mult, d))

        def sel_turned(t, d):
            b = 2 + t
            for j, src in enumerate((gt.rearrange("p h k -> p (h k)"), sel[:, 0, :], sel[:, 1, :])):
                w = tr(banks[b][:, j * 128:(j + 1) * 128], src, d, free[b])
            for j, dst in enumerate((selG, sel1, sel2)):
                e = DVE(lambda e, t=t, b=b, j=j, dst=dst: e.tensor_copy(dst[:, tcols(t)], banks[b][:, j * 128:j * 128 + 128]),
                        w, spill)
            free[b] = [e]
            sT_tok.append(e)
            return e

        h_tk = {}

        def hidden(j):
            u = Unit(8)
            b = j % 2
            m = mm3(banks[b][:, 0:256], [u.pair(k, slice(0, 128)) for k in range(8)],
                    [hT(k, ALLC) for k in range(8)], True, True, u.tok, h_tok, free[b])
            h_tk[j] = act(H[:, j, :], banks[b][:, 0:256], ACTF.Gelu_apprx_tanh, m, sT_tok if j * 256 + 256 > R_AT else None,
                          s_tok)
            free[b] = [h_tk[j]]
            u.used(m)

        ohA = [xs[:, 512 + 512 * j:1024 + 512 * j].rearrange("p (t n) -> p t n", t=4) for j in range(2)]
        ohB = [xs[:, 1536 + 256 * j:1792 + 256 * j].rearrange("p (t n) -> p t n", t=4) for j in range(2)]
        g_mm = []
        oh_tk = {}
        G_tok = {0: [], 1: []}

        def one_hot(i):
            half, g = i // 64, i % 64
            ts4 = slice(4 * g, 4 * g + 4)
            prev = g_mm[i - 2] if i >= 2 else None
            dA = tt(DVE, ohA[i % 2], iot.unsqueeze(1).broadcast_to([128, 4, 128]),
                    sel1[:, ts4].unsqueeze(2).broadcast_to([128, 4, 128]), ALU.is_equal, sT_tok, prev)
            dB = tt(DVE, ohB[i % 2], iot[:, 64 * half:64 * half + 64].unsqueeze(1).broadcast_to([128, 4, 64]),
               sel2[:, ts4].unsqueeze(2).broadcast_to([128, 4, 64]), ALU.is_equal, sT_tok, prev)
            dB = tt(POOL, ohB[i % 2], ohB[i % 2], selG[:, ts4].unsqueeze(2).broadcast_to([128, 4, 64]), ALU.mult, dB)
            oh_tk[i] = [dA, dB]

        def gates_of(half, g):
            i = 64 * half + g
            if i == 0:
                one_hot(0)
            if i < 127:
                one_hot(i + 1)
            b = 2 + i % 2
            for j in range(4):
                m = mm(banks[b][:, j * 64:(j + 1) * 64], [(ohA[i % 2][:, j, :], ohB[i % 2][:, j, :])], oh_tk[i], free[b])
            g_mm.append(m)
            hv = H[:, 64 * half:64 * half + 64, 4 * g:4 * g + 4]
            e = tt(DVE, hv, hv, banks[b][:, 0:256].rearrange("p (t j) -> p j t", t=4), ALU.mult, m, h_tk[64 * half + 63])
            free[b] = [e]
            G_tok[half] = [e]

        def split_gated(j):
            a = act(ach[j % 2], H[:, j, :], ACTF.Copy, G_tok[j // 64], v_mm.get(j - 2))
            ac_tk[j] = tt(DVE, acl[j % 2], H[:, j, :], ach[j % 2].bitcast(F32), ALU.subtract, a)

        v_mm, ac_tk = {}, {}

        def down(j):
            u = Unit(1)
            for t in range(2):
                for n in range(2):
                    b = 4 + 2 * t + n
                    v_mm[j] = mm3(banks[b][:, :], [(ach[j % 2][:, tcols(t)], acl[j % 2][:, tcols(t)])],
                                  [u.pair(0, slice(n * 512, (n + 1) * 512))], j == 0, j == 127,
                                  ac_tk[j], u.tok, free[b] if j == 0 else None)
            u.used(v_mm[j])

        picked = [[], []]
        steps = routing(0, h_tok, picked[0])
        for j in range(128):
            if j == 31:
                run(steps)
                steps = routing(1, sel_turned(0, picked[0]), picked[1])
            if j == 63:
                run(steps)
                sel_turned(1, picked[1])
            next(steps, None)
            hidden(j)
            if j >= 65:
                gates_of(0, j - 65)
        gates_of(0, 63)
        split_gated(0)
        for j in range(128):
            if j < 64:
                gates_of(1, j)
            if j + 1 < 128:
                split_gated(j + 1)
            down(j)
        back = q.dma("act", xs[:, :], spill_d, s_back, [spill, G_tok[1]])
        x_tok = [tt(DVE, x[:, t, n * 512:(n + 1) * 512], x[:, t, n * 512:(n + 1) * 512], banks[4 + 2 * t + n][:, :],
                    ALU.add, v_mm[127], back) for t in range(2) for n in range(2)]
        u = Unit(1)
        done = []
        for t in range(2):
            p = rms_rstd(x[:, t, :], H_s[:, 1024 * t:1024 * t + 1024], t, 1.0 / 1024, x_tok)
            d = stt(x[:, t, :], x[:, t, :], rstd[:, t:t + 1], u.h, ALU.mult, ALU.mult, p, u.tok)
            done.append(q.dma("sp", out_d[tcols(t), :], x[:, t, :], s_out, [d]))
        fin_tok = done[-1]
        sc_p.close()

        q.number(sems)
        block = ctx.enter_context(nc.Block())

        @block.sync
        def _(eng):
            q.emit("sp", eng)
            eng.wait_ge(s_out, fin_tok.val)

        @block.scalar
        def _(eng):
            q.emit("act", eng)

        @block.vector
        def _(eng):
            q.emit("dve", eng)

        @block.tensor
        def _(eng):
            q.emit("pe", eng)

        @block.gpsimd
        def _(eng):
            q.emit("pool", eng)


def constants():
    c = np.zeros((128, K_W), np.float32)
    c[:, K_ID:K_ID + 128] = np.eye(128, dtype=np.float32)
    c[:, K_IOTA:K_IOTA + 128] = np.arange(128)
    p = np.arange(128)
    k = np.arange(256)
    for t in range(2):
        qp = (t * 128 + p)[:, None]
        causal = k[None, :] <= qp
        c[:, K_MC + 256 * t:K_MC + 256 * t + 256] = np.where(causal, 0.0, NEG)
        dist = qp - k[None, :]
        count = (causal & (dist <= 128)) * 1 + (causal & (dist % 4 == 0)) * 1 + (causal & (dist % 16 == 0)) * 1
        c[:, K_MD + 256 * t:K_MD + 256 * t + 256] = np.where(count > 0, 8.0 * np.log(np.maximum(count, 1)), NEG)
        for dim, kc, ks in ((64, K_CA, K_SA), (32, K_CI, K_SI)):
            inv = np.float32(10000.0) ** (-np.arange(0, dim, 2, dtype=np.float32) / np.float32(dim))
            a = (np.float32(1.0) * qp.astype(np.float32)) * inv.astype(np.float32)[None, :]
            n = dim // 2
            c[:, kc + n * t:kc + n * t + n] = np.cos(a.astype(np.float64))
            c[:, ks + n * t:ks + n * t + n] = np.sin(a.astype(np.float64))
    for rot, o in ((8, 0), (16, 4)):
        h = rot // 2
        c[:, K_INV + o:K_INV + o + h] = np.power(np.float32(500000.0), -np.arange(h, dtype=np.float32) * 2.0 / rot)
    c[:, K_T:K_T + 256] = k
    return c


def slabs(w, width):
    d, n = w.shape
    return w.reshape(d // 128, 128, n // width, width).transpose(2, 1, 0, 3).reshape(n // width, 128, -1)


def feat(v):
    return v.reshape(-1, 128).T


def layout(i):
    a = {}
    x = np.asarray(i["x"])
    a["x"] = x[0].reshape(2, 128, 1024).transpose(1, 0, 2)
    a["pos"] = np.asarray(i["positions"])[0].reshape(2, 128).T
    a["consts"] = constants()
    s = np.zeros((128, S_W), np.float32)
    for j, g in enumerate([i["g_mix"][0], i["g_mix"][1], i["g_ffn"][0], i["g_ffn"][1], i["norm1_g_2"][0], i["norm2_g_2"][0]]):
        s[:, S_G + 8 * j:S_G + 8 * j + 8] = feat(np.asarray(g))
    for l in range(DEPTH):
        cv = np.stack([feat(np.asarray(i["conv_w"][l][j])) for j in range(3)] + [feat(np.asarray(i["conv_b"][l]))], axis=2)
        s[:, S_CONV + 176 * l:S_CONV + 176 * l + 176] = cv.reshape(128, 176)
        for j, n in enumerate(("lambda_q1", "lambda_k1", "lambda_q2", "lambda_k2")):
            s[:, S_LAM + 128 * l + 32 * j:S_LAM + 128 * l + 32 * j + 32] = np.asarray(i[n])[l]
        s[:, S_GD + 64 * l:S_GD + 64 * l + 64] = np.asarray(i["g_diff"])[l]
    s[:, S_DSK:S_DSK + 4] = feat(np.asarray(i["d_skip_2"])[0])
    s[:, S_LDT:S_LDT + 16] = np.repeat(np.asarray(i["log_dt_2"])[0].reshape(16, 2), 64, axis=1).T
    s[:, S_ARE:S_ARE + 16] = np.asarray(i["a_re_2"])[0].reshape(16, 128).T
    s[:, S_AIM:S_AIM + 16] = np.asarray(i["a_im_2"])[0].reshape(16, 128).T
    a["smalls"] = s
    w_in = np.asarray(i["w_in"])
    a["win"] = np.stack([slabs(w_in[l], 512) for l in range(DEPTH)])
    a["wout"] = np.stack([slabs(np.asarray(i["w_out"])[l], 512) for l in range(DEPTH)])
    up = np.asarray(i["w_up"]).reshape(DEPTH, 8, 128, 2, NTILE, 128)
    a["wup"] = up.transpose(0, 4, 3, 2, 1, 5).reshape(DEPTH, 2 * NTILE, 128, 1024)
    a["wdown"] = np.asarray(i["w_down"]).reshape(DEPTH, NTILE, 128, 1024)
    a["rows"] = np.stack([np.broadcast_to(np.asarray(g), (128, 1024)) for g in (i["g_final"], i["norm_f_g_2"])])
    w2 = np.asarray(i["w_in_2"])[0]
    a["wu"] = slabs(w2[:, 0:512], 128)
    a["wqkv"] = slabs(w2[:, 512:1536], 512)
    a["wga"] = slabs(w2[:, 1576:3624], 512)
    a["wqk"] = slabs(w2[:, 1536:1576], 40)[0]
    sw = np.zeros((4, 16, 2, 64, 2, 16), np.float32)
    for j, n in enumerate(("b_re_2", "b_im_2")):
        b = np.asarray(i[n])[0].reshape(16, 2, 64, 16)
        for g in range(2):
            sw[j, :, g, :, g, :] = b[:, g]
    for j, n in enumerate(("c_re_2", "c_im_2")):
        c = np.asarray(i[n])[0].reshape(16, 2, 16, 64).transpose(0, 1, 3, 2)
        for g in range(2):
            sw[2 + j, :, g, :, g, :] = c[:, g]
    a["wsm"] = sw.reshape(4, 16, 128, 32).transpose(2, 0, 1, 3).reshape(128, 2048)
    a["wglu"] = slabs(np.asarray(i["w_glu_2"])[0], 256)
    a["wsu"] = slabs(np.asarray(i["w_ssm_up_2"])[0], 512)
    a["wau"] = slabs(np.asarray(i["w_attn_up_2"])[0], 512)
    a["wout2"] = slabs(np.asarray(i["w_out_2"])[0], 512)
    a["wpq"] = slabs(np.asarray(i["peer_wq_2"])[0], 128)
    keys = np.stack([np.asarray(i["peer_k1_2"])[0], np.asarray(i["peer_k2_2"])[0]], axis=1)
    a["keys"] = keys.reshape(16, 128, 128).transpose(2, 0, 1).reshape(128, 2048)
    u = np.asarray(i["peer_u_2"])[0].reshape(128, 128, 8, 128)
    a["ut"] = u.transpose(1, 3, 2, 0).reshape(128, 128, 1024)
    v = np.asarray(i["peer_v_2"])[0].reshape(128, 128, 1024)
    a["vt"] = v.transpose(1, 0, 2)
    return a


_ORDER = ["x", "pos", "consts", "smalls", "win", "wout", "wup", "wdown", "rows", "wu", "wqkv", "wqk", "wga", "wsm", "wglu", "wsu",
          "wau", "wout2", "wpq", "keys", "ut", "vt"]


def kernel(**inputs):
    import concourse.bacc as _bacc
    from concourse.bass_utils import run_bass_kernel_spmd as _run

    nc = _bacc.Bacc("TRN2", target_bir_lowering=False, num_devices=1)
    made = layout(inputs)
    arrays, args = {}, []
    for name in _ORDER:
        a = np.ascontiguousarray(made[name])
        arrays[f"in_{name}_dram"] = a
        args.append(nc.dram_tensor(f"in_{name}_dram", a.shape, mybir.dt.from_np(a.dtype), kind="ExternalInput").ap())
    out = nc.dram_tensor("out_0_dram", (256, 1024), F32, kind="ExternalOutput").ap()
    spill = nc.dram_tensor("spill_dram", (128, 2048), F32, kind="Internal").ap()
    program(nc, *args, out, spill)
    r = _run(nc, [arrays], core_ids=[0])
    return r.results[0]["out_0_dram"].reshape(1, 256, 1024)
```

```python
import math
from contextlib import ExitStack

import numpy as np
import concourse.bass as bass
from concourse import mybir

F32 = mybir.dt.float32
F32R = mybir.dt.float32r
I32 = mybir.dt.int32
U32 = mybir.dt.uint32
BF16 = mybir.dt.bfloat16
ALU = mybir.AluOpType
ACTF = mybir.ActivationFunctionType
AX = mybir.AxisListType.X

EPS = 1e-6
NEG = -1e30
TAKEN = -3e38
MAGIC = 12582912.0
TWO_PI = 6.283185307179586
C1 = 6.28125
C2 = float(np.float32(TWO_PI - C1))
C3 = TWO_PI - C1 - C2
SIN_SCALE = 6.283185
DEPTH = 2
NTILE = 22
LAM_INIT = [0.8 - 0.6 * math.exp(-0.3 * layer) for layer in range(DEPTH)]

K_ID, K_IOTA, K_MC, K_MD, K_CA, K_SA, K_CI, K_SI, K_INV, K_T = 0, 128, 256, 768, 1280, 1344, 1408, 1440, 1472, 1484
K_W = K_T + 256
S_CONV = 0
S_LAM = S_CONV + 2 * 176
S_GD = S_LAM + 256
S_DSK = S_GD + 128
S_LDT = S_DSK + 4
S_ARE = S_LDT + 16
S_AIM = S_ARE + 16
S_W = S_AIM + 16


class Op:

    def __init__(self, eng, fn, after, sem=None, inc=1):
        self.eng, self.fn, self.after, self.sem, self.inc = eng, fn, after, sem, inc
        self.val, self.need = 0, sem is not None


def flat(xs):
    out = []
    for x in xs:
        if isinstance(x, dict):
            out += flat(list(x.values()))
        elif isinstance(x, (list, tuple)):
            out += flat(x)
        elif x is not None:
            out.append(x)
    return out


class Queues:

    def __init__(self):
        self.ops = {e: [] for e in ("pe", "act", "dve", "pool", "sp")}
        self.dma_count = {}

    def put(self, eng, fn, after):
        op = Op(eng, fn, flat(after))
        for a in op.after:
            a.need = True
        self.ops[eng].append(op)
        return op

    def dma(self, eng, out, in_, sem, after):
        op = Op(eng, lambda e: e.dma_start(out, in_), flat(after), sem, 16)
        for a in op.after:
            a.need = True
        self.dma_count[sem.name] = self.dma_count.get(sem.name, 0) + 16
        op.val = self.dma_count[sem.name]
        self.ops[eng].append(op)
        return op

    def number(self, sems):
        for name, ops in self.ops.items():
            n = 0
            for op in ops:
                if op.sem is None and op.need:
                    n += 1
                    op.sem, op.val = sems[name], n

    def emit(self, name, eng):
        seen = {}
        for op in self.ops[name]:
            for a in op.after:
                if seen.get(a.sem.name, 0) < a.val:
                    eng.wait_ge(a.sem, a.val)
                    seen[a.sem.name] = a.val
            ins = op.fn(eng)
            if op.need:
                ins.then_inc(op.sem, op.inc)


def program(nc, x_d, pos_d, consts_d, smalls_d, win_d, wout_d, wup_d, wdown_d, rows_d, wu_d, wqkv_d, wqk_d, wga_d, wsm_d,
            wglu_d, wsu_d, wau_d, wout2_d, wpq_d, keys_d, ut_d, vt_d, out_d, spill_d):
    with ExitStack() as ctx:
        def sb(name, n, dt=F32):
            return ctx.enter_context(nc.sbuf_tensor(name, [128, n], dt))

        def scoped(where, name, n, dt=F32):
            return where.enter_context(nc.sbuf_tensor(name, [128, n], dt))

        xs = sb("xs", 2048)
        ids = sb("ids", 128)
        hh, hl = sb("hh", 2048, F32R), sb("hl", 2048, F32R)
        sta = sb("sta", 760)
        raws = [sb(f"raw{i}", 1024) for i in range(4)]
        whs = [sb(f"wh{i}", 1024, F32R) for i in range(4)]
        wls = [sb(f"wl{i}", 1024, F32R) for i in range(4)]
        early = ExitStack()
        con_s = scoped(early, "con", K_W - 128)
        sml_s = scoped(early, "sml", S_W)
        tab_s = scoped(early, "tab", 8192)
        raws += [scoped(early, f"raw{i}", 1024) for i in (4, 5)]
        whs += [scoped(early, f"wh{i}", 1024, F32R) for i in (4, 5)]
        wls += [scoped(early, f"wl{i}", 1024, F32R) for i in (4, 5)]
        banks = [ctx.enter_context(nc.psum_tensor(f"bank{i}", [128, 512], F32)) for i in range(8)]
        sems = {e: ctx.enter_context(nc.semaphore(f"s_{e}")) for e in ("pe", "act", "dve", "pool", "sp")}
        slot_sem = [ctx.enter_context(nc.semaphore(f"s_slot{i}")) for i in range(6)]
        s_x, s_pos, s_id, s_k, s_sm, s_ssm, s_ssc, s_out, s_spill, s_back = [
            ctx.enter_context(nc.semaphore(n)) for n in ("s_x", "s_pos", "s_id", "s_k", "s_sm", "s_ssm", "s_ssc", "s_out", "s_spill", "s_back")]

        q = Queues()

        def PE(fn, *after):
            return q.put("pe", fn, after)

        def ACT(fn, *after):
            return q.put("act", fn, after)

        chain = {"dve": [], "pool": []}

        def DVE(fn, *after):
            chain["dve"] = [q.put("dve", fn, after + tuple(chain["dve"]))]
            return chain["dve"][0]

        def POOL(fn, *after):
            chain["pool"] = [q.put("pool", fn, after + tuple(chain["pool"]))]
            return chain["pool"][0]

        def DVE_ON(fn, *after):
            chain["dve"] = [q.put("dve", fn, after)]
            return chain["dve"][0]

        def POOL_ON(fn, *after):
            chain["pool"] = [q.put("pool", fn, after)]
            return chain["pool"][0]

        def tt(E, out, a, b, op, *after):
            return E(lambda e: e.tensor_tensor(out, a, b, op), *after)

        def ts(E, out, a, s1, s2, op0, op1, *after):
            if op1 is None:
                return E(lambda e: e.tensor_scalar(out, a, s1, None, op0), *after)
            return E(lambda e: e.tensor_scalar(out, a, s1, s2, op0, op1), *after)

        def stt(out, a, s, b, op0, op1, *after):
            return DVE(lambda e: e.scalar_tensor_tensor(out, a, s, b, op0, op1), *after)

        def act(out, a, f, *after, **kw):
            return ACT(lambda e: e.activation(out, a, f, **kw), *after)

        def copy(i, out, a, *after):
            if i % 2:
                return ACT(lambda e: e.activation(out, a, ACTF.Copy), *after)
            return DVE_ON(lambda e: e.tensor_copy(out, a), *after)

        def mm(out, pairs, *after):
            t = None
            for i, (l, r) in enumerate(pairs):
                t = PE(lambda e, l=l, r=r, i=i: e.matmul(out, l, r, start=i == 0, stop=i == len(pairs) - 1),
                       *(after if i == 0 else ()))
            return t

        def tr(out, a, *after):
            return PE(lambda e: e.transpose(out, a, ids[:, :]), *after)

        free = [[] for _ in range(8)]
        turn = [0]

        def bank(of=range(8)):
            of = list(of)
            turn[0] += 1
            return of[turn[0] % len(of)]

        def quarters(w):
            return [(w[:, h * 1024:h * 1024 + 1024], 1024, True) for h in range(w.shape[1] // 1024)]

        plan = []
        for layer in range(DEPTH):
            plan += [(rows_d[layer], 1024, False)]
            for n in range(6):
                plan += quarters(win_d[layer, n])
            for n in range(2):
                plan += quarters(wout_d[layer, n])
            plan += [(rows_d[2 + layer], 1024, False)]
            plan += [(wup_d[layer, f], 1024, True) for f in range(2 * NTILE)]
            plan += [(wdown_d[layer, f], 1024, True) for f in range(NTILE)]
        plan += [(rows_d[n], 1024, False) for n in (4, 5)]
        plan += [(wu_d[n], 1024, True) for n in range(4)]
        plan += quarters(wqkv_d[0]) + quarters(wqkv_d[1])
        plan += [(wqk_d, 320, True)]
        for n in range(4):
            plan += quarters(wga_d[n])
        plan += [(wglu_d[n], 1024, True) for n in range(2)]
        plan += quarters(wsu_d[0]) + quarters(wsu_d[1])
        plan += quarters(wau_d[0]) + quarters(wau_d[1])
        plan += quarters(wout2_d[0]) + quarters(wout2_d[1])
        plan += [(rows_d[6], 1024, False)]
        plan += [(wpq_d[n], 1024, True) for n in range(16)]
        plan += [(keys_d[:, h * 1024:h * 1024 + 1024], 1024, False) for h in range(2)]
        n_early = len(plan)
        plan += [(ut_d[n], 1024, True) for n in range(128)]
        plan += [(vt_d[n], 1024, True) for n in range(128)]
        plan += [(rows_d[7], 1024, False)]
        split_at = []
        for i, p in enumerate(plan):
            split_at.append(0 if i in (0, n_early) else split_at[-1] + plan[i - 1][2])
        raw_free = [[] for _ in raws]
        w_free = [[] for _ in whs]
        raw_busy = [False] * 6
        w_busy = [False] * 6
        units = {}
        st = {"ahead": 0, "at": 0, "lo": ["dve", "pool"], "used": None}

        def prefetch():
            i = st["ahead"]
            if i >= len(plan):
                return
            src, n, split = plan[i]
            first, depth = (0, 6) if i < n_early else (n_early, 4)
            r = (i - first) % depth
            s_ = split_at[i] % depth
            if raw_busy[r] or (split and w_busy[s_]):
                return
            st["ahead"] = i + 1
            raw = raws[r][:, 0:n]
            t = q.dma("sp", raw, src, slot_sem[r], [raw_free[r]])
            if not split:
                raw_busy[r] = True
                units[i] = (raw, None, t, r)
                return
            w_busy[s_] = True
            wh, wl = whs[s_][:, 0:n], wls[s_][:, 0:n]
            hi = act(wh, raw, ACTF.Copy, t, w_free[s_])
            eng = st["lo"][i % len(st["lo"])]
            lo = q.put(eng, lambda e: e.tensor_tensor(wl, raw, wh.bitcast(F32), ALU.subtract), [hi, t, w_free[s_]])
            raw_free[r] = [lo, hi]
            units[i] = (wh, wl, lo, s_)

        def take():
            i = st["at"]
            st["at"] = i + 1
            assert i < st["ahead"]
            return units.pop(i)

        def mm3(out, lhs, rhs, start, stop, *after, each=None):
            t = None
            n = len(lhs)
            for i in range(n):
                for j, (a, b) in enumerate(((0, 0), (0, 1), (1, 0))):
                    t = PE(lambda e, l=lhs[i][a], r=rhs[i][b], i=i, j=j: e.matmul(
                        out, l, r, start=start and i == 0 and j == 0, stop=stop and i == n - 1 and j == 2),
                        *(after if i == 0 and j == 0 else ()), each(i) if each and j == 0 else None)
            return t

        def halves(dh, dl, src, *after):
            a = act(dh, src, ACTF.Copy, *after)
            return tt(DVE_ON, dl, src, dh.bitcast(F32), ALU.subtract, a, *after)

        x = xs[:, :].rearrange("p (t d) -> p t d", t=2)
        hTh = hh[:, :].rearrange("p (k t) -> p k t", k=8)
        hTl = hl[:, :].rearrange("p (k t) -> p k t", k=8)
        cosT = tab_s[:, 0:4096].rearrange("p (n t) -> p n t", n=16)
        sinT = tab_s[:, 4096:8192].rearrange("p (n t) -> p n t", n=16)
        sta_at = [0]

        def stat(n):
            o = sta_at[0]
            sta_at[0] += n
            assert sta_at[0] <= 760
            return sta[:, o:o + n]

        def con(c, n):
            return con_s[:, c - 128:c - 128 + n]

        def sml(c, n):
            return sml_s[:, c:c + n]

        def hT(k, cols):
            return hTh[:, k, cols], hTl[:, k, cols]

        iota = con(K_IOTA, 128)
        maskC = con(K_MC, 512).rearrange("p (t k) -> p t k", t=2)
        maskD = con(K_MD, 512).rearrange("p (t k) -> p t k", t=2)

        ld_x = q.dma("act", xs[:, :].rearrange("p (t d) -> p t d", t=2), x_d, s_x, [])
        pos_i = stat(2).bitcast(I32)
        ld_pos = q.dma("act", pos_i, pos_d, s_pos, [])
        ld_id = q.dma("act", ids[:, :], consts_d[:, 0:128], s_id, [])
        ld_k = q.dma("act", con_s[:, :], consts_d[:, 128:K_W], s_k, [])
        ld_s = q.dma("act", sml(0, S_W), smalls_d, s_sm, [])

        neghalf = stat(8)
        c0 = POOL(lambda e: e.memset(neghalf, -0.5))
        ss = stat(2)
        ms = stat(2)
        rstd = stat(2)

        def rms_rstd(src, junk, t, scale, *after):
            a = act(junk, src, ACTF.Square, *after, accum_out=ss[:, t:t + 1])
            b = ts(DVE, ms[:, t:t + 1], ss[:, t:t + 1], scale, EPS, ALU.mult, ALU.add, a)
            return tt(POOL, rstd[:, t:t + 1], ms[:, t:t + 1], neghalf[:, 0:1], ALU.pow, b, c0)

        def transposed(src, ncol, evac, after, ts=range(2), of=range(8)):
            done = {}
            for t in ts:
                for k0 in range(0, ncol, 4):
                    n = min(4, ncol - k0)
                    b = bank(of)
                    for k in range(n):
                        w = tr(banks[b][:, k * 128:(k + 1) * 128], src[:, t, (k0 + k) * 128:(k0 + k + 1) * 128],
                               *([after[t], ld_id, free[b]] if k == 0 else []))
                    e = evac(t, k0, n, banks[b][:, 0:n * 128].rearrange("p (k c) -> p k c", k=n), w)
                    free[b] = [e]
                    done[t, k0 // 4] = e
            return done

        def upon(toks, t, k):
            return toks[t, k // 4] if isinstance(toks, dict) else toks

        class Norm:

            def __init__(self, buf):
                self.buf, self.u, self.outs, self.done = buf, Unit(1), [], {}

            def scale(self, t, after):
                p = rms_rstd(x[:, t, :], self.buf[:, t, :], t, 1.0 / 1024, after)
                self.outs.append(stt(self.buf[:, t, :], x[:, t, :], rstd[:, t:t + 1], self.u.h, ALU.mult, ALU.mult, p, self.u.tok))
                if t:
                    self.u.used(self.outs[-1])

            def turned(self, *ts):
                self.done.update(transposed(self.buf, 8, halves_evac(), self.outs, ts=ts))
                return self.done

        def halves_evac(k_off=0):
            def evac(t, k0, n, ps, w):
                ks, cols = slice(k_off + k0, k_off + k0 + n), slice(t * 128, (t + 1) * 128)
                return halves(hTh[:, ks, cols], hTl[:, ks, cols], ps, w)
            return evac

        iot = stat(16)
        iob = stat(64).bitcast(BF16)

        posf = stat(2)
        ang, ra, rb, rn = stat(24), stat(24), stat(24), stat(24)
        cosP, sinP = stat(24), stat(24)
        def reduced(E, out, src, tmp, quarter, *after):
            d = ts(E, tmp, src, 1.0 / TWO_PI, quarter, ALU.mult, ALU.add, *after)
            d = ts(E, tmp, tmp, MAGIC, None, ALU.add, None, d)
            n = ts(E, tmp, tmp, MAGIC, None, ALU.subtract, None, d)
            d = n
            cur = src
            for c in (C1, C2, C3):
                d = stt(out, tmp, -c, cur, ALU.mult, ALU.add, d)
                cur = out
            if quarter:
                d = ts(E, out, out, math.pi / 2, None, ALU.add, None, d)
            return ts(E, out, out, 3.1415925, -3.1415925, ALU.min, ALU.max, d)

        ldt, are, aim = sml(S_LDT, 16), sml(S_ARE, 16), sml(S_AIM, 16)
        dt_, xr, th, rr, fr = [stat(16) for _ in range(5)]
        sn, cn, sh, e1, kr, ki = [stat(16) for _ in range(6)]
        t16 = [stat(16) for _ in range(4)]

        state = []

        def state_constants():
            a_dt = act(dt_, ldt, ACTF.Exp, ld_s)
            d = tt(DVE, xr, are, dt_, ALU.mult, a_dt)
            yield
            d = tt(DVE, th, aim, dt_, ALU.mult, a_dt)
            yield
            d = reduced(DVE, t16[0], th, t16[1], 0.0, d)
            sred = d
            yield
            d = ts(DVE, fr, t16[0], 1.0 / TWO_PI, None, ALU.mult, None, d)
            yield
            f_tok = d
            d = reduced(DVE, t16[2], th, t16[1], 0.25, d)
            cred = d
            yield
            a_ex = act(rr, xr, ACTF.Exp, d)
            a_sn = act(sn, t16[0], ACTF.Sin, sred)
            a_sh = act(sh, t16[0], ACTF.Sin, sred, scale=0.5)
            a_cn = act(cn, t16[2], ACTF.Sin, cred)
            d = ts(DVE, t16[1], xr, 0.5, -0.5, ALU.min, ALU.max, a_cn)
            yield
            d = ts(DVE, e1, t16[1], 1.0 / 9, 1.0, ALU.mult, ALU.add, d)
            yield
            for c in (8, 7, 6, 5, 4, 3, 2):
                d = tt(DVE, e1, e1, t16[1], ALU.mult, d)
                yield
                d = ts(DVE, e1, e1, 1.0 / c, 1.0, ALU.mult, ALU.add, d)
                yield
            d = tt(DVE, e1, e1, t16[1], ALU.mult, d)
            yield
            d = tt(DVE, t16[2], t16[1], xr, ALU.is_equal, d)
            yield
            d = ts(DVE, t16[3], rr, -1.0, None, ALU.add, None, d, a_ex)
            yield
            msk = t16[2].bitcast(I32)
            d = DVE(lambda e: e.copy_predicated(t16[3], msk, e1), d)
            d = ts(DVE, rr, t16[3], 1.0, None, ALU.add, None, d)
            yield
            d = tt(DVE, kr, t16[3], cn, ALU.mult, d)
            yield
            d = tt(DVE, t16[0], sh, sh, ALU.mult, d, a_sh)
            yield
            d = stt(kr, t16[0], -2.0, kr, ALU.mult, ALU.add, d)
            yield
            d = tt(DVE, ki, rr, sn, ALU.mult, d)
            yield
            d = tt(DVE, t16[0], are, are, ALU.mult, d)
            yield
            d = tt(DVE, t16[1], aim, aim, ALU.mult, d)
            yield
            d = tt(DVE, t16[0], t16[0], t16[1], ALU.add, d)
            yield
            d = DVE(lambda e: e.reciprocal(t16[0], t16[0]), d)
            d = tt(DVE, t16[1], kr, are, ALU.mult, d)
            yield
            d = tt(DVE, t16[2], ki, aim, ALU.mult, d)
            yield
            d = tt(DVE, t16[1], t16[1], t16[2], ALU.add, d)
            yield
            d = tt(DVE, t16[2], ki, are, ALU.mult, d)
            yield
            d = tt(DVE, t16[3], kr, aim, ALU.mult, d)
            yield
            d = tt(DVE, t16[2], t16[2], t16[3], ALU.subtract, d)
            yield
            d = tt(DVE, kr, t16[1], t16[0], ALU.mult, d)
            yield
            k_tok = tt(DVE, ki, t16[2], t16[0], ALU.mult, d)
            state.extend([f_tok, k_tok])

        def phase_tables(groups, f_tok, ptmp, p):
            tv = con(K_T, 256).unsqueeze(1).broadcast_to([128, 2, 256])
            for n in groups:
                fb = fr[:, n:n + 2].unsqueeze(2).broadcast_to([128, 2, 256])
                for tab, quarter in ((sinT, 0.0), (cosT, 0.25)):
                    o = tab[:, n:n + 2, :]
                    p = tt(DVE, o, tv, fb, ALU.mult, f_tok, ld_k, p)
                    if quarter:
                        p = ts(DVE, o, o, quarter, None, ALU.add, None, p)
                    p = ts(DVE, ptmp, o, MAGIC, None, ALU.add, None, p)
                    p = ts(DVE, ptmp, ptmp, MAGIC, None, ALU.subtract, None, p)
                    p = tt(DVE, o, o, ptmp, ALU.subtract, p)
            return p


        lam = [stat(1) for _ in range(DEPTH)]
        lj, l1, l2 = stat(32), stat(1), stat(1)
        gd = [sml(S_GD + 64 * i, 64) for i in range(DEPTH)]
        rope_tok, lam_tok = [], []

        def opening():
            d = DVE(lambda e: e.tensor_copy(posf, pos_i), ld_pos)
            a3 = ang.rearrange("p (t f) -> p t f", t=2)
            inv3 = con(K_INV, 12).unsqueeze(1).broadcast_to([128, 2, 12])
            d = tt(DVE, a3, posf.unsqueeze(2).broadcast_to([128, 2, 12]), inv3, ALU.mult, d, ld_k)
            r1 = reduced(DVE, ra, ang, rn, 0.0, d)
            r2 = reduced(DVE, rb, ang, rn, 0.25, r1)
            a_s = act(sinP, ra, ACTF.Sin, r1)
            a_s = act(cosP, rb, ACTF.Sin, r2)
            d = DVE(lambda e: e.tensor_copy(iot, iota[:, 0:16]), ld_k)
            d = DVE(lambda e: e.tensor_copy(iob, iota), d)
            rope_tok.append(a_s)
            last = None
            for i in range(DEPTH):
                v = [sml(S_LAM + 128 * i + 32 * j, 32) for j in range(4)]
                d1 = DVE(lambda e, v=v: e.tensor_tensor_reduce(lj, v[0], v[1], 1.0, 0.0, ALU.mult, ALU.add, l1), ld_s, last)
                d2 = DVE(lambda e, v=v: e.tensor_tensor_reduce(lj, v[2], v[3], 1.0, 0.0, ALU.mult, ALU.add, l2), d1)
                a1 = act(l1, l1, ACTF.Exp, d2)
                a2 = act(l2, l2, ACTF.Exp, a1)
                d = tt(DVE, l1, l1, l2, ALU.subtract, a2)
                d = ts(DVE, lam[i], l1, LAM_INIT[i], None, ALU.add, None, d)
                d = ts(DVE, gd[i], gd[i], 1.0 - LAM_INIT[i], None, ALU.mult, None, d)
                last = d
            lam_tok.append(last)

        def rope(E, view, half, cos, sin, tmp, *after):
            u = view.shape[2]
            n = 2 * u * half
            per = tmp[0].shape[1] // n
            ts4 = [tmp[i // per][:, i % per * n:(i % per + 1) * n].rearrange("p (t u f) -> p t u f", t=2, u=u) for i in range(4)]
            x1, x2 = view[:, :, :, 0:half], view[:, :, :, half:2 * half]
            cb = cos.unsqueeze(2).broadcast_to([128, 2, u, half])
            sn_ = sin.unsqueeze(2).broadcast_to([128, 2, u, half])
            tt(E, ts4[0], x1, cb, ALU.mult, *after)
            o2 = tt(E, ts4[1], x2, sn_, ALU.mult)
            tt(E, ts4[2], x2, cb, ALU.mult)
            o4 = tt(E, ts4[3], x1, sn_, ALU.mult)
            o5 = tt(E, x1, ts4[0], ts4[1], ALU.subtract, o4)
            return tt(E, x2, ts4[2], ts4[3], ALU.add, o4)

        NB = 4
        mx, den, rden = stat(40), stat(40), stat(40)
        rlam = [stat(4) for _ in range(2)]

        def attend(buf, maps, *after):
            n = len(maps)
            bsm, bE, bET = [[buf[:, 1024 * j + 256 * i:1024 * j + 256 * i + 256] for i in range(NB)] for j in range(3)]
            s_t, m_t, e_t, tr_t, c_t, pv_t = ({} for _ in range(6))

            def scores(i):
                nk, qT, kT, v, mask, scale, o, ready = maps[i]
                b = i % 2
                s_t[i] = mm(banks[b][:, 0:128 * nk], [(qT, kT)], free[b], ready)
                m_t[i] = DVE_ON(lambda e: e.tensor_tensor_reduce(
                    bsm[i % NB][:, 0:128 * nk], banks[b][:, 0:128 * nk], mask, -scale, 3e38, ALU.add, ALU.min,
                    mx[:, i:i + 1]), s_t[i], e_t.get(i - NB), after)
                free[b] = [m_t[i]]
                e_t[i] = act(bE[i % NB][:, 0:128 * nk], bsm[i % NB][:, 0:128 * nk], ACTF.Exp, m_t[i], tr_t.get(i - NB), after,
                             bias=mx[:, i:i + 1], scale=-1.0, accum_out=den[:, i:i + 1])

            def turned(i):
                nk = maps[i][0]
                b = 2 + i % 2
                for k in range(nk):
                    tr_t[i] = tr(banks[b][:, 128 * k:128 * k + 128], bE[i % NB][:, 128 * k:128 * k + 128],
                                 e_t[i], free[b])
                c_t[i] = copy(i, bET[i % NB][:, 0:128 * nk], banks[b][:, 0:128 * nk], tr_t[i], pv_t.get(i - NB), after)
                free[b] = [c_t[i]]

            def pv(i):
                nk, qT, kT, v, mask, scale, (ob, oc), ready = maps[i]
                pv_t[i] = mm(banks[ob][:, oc:oc + 64],
                             [(bET[i % NB][:, 128 * k:128 * k + 128], v(k)) for k in range(nk)],
                             c_t[i], free[ob] if oc == 0 else None)

            for i in range(n + 4):
                if i < n:
                    scores(i)
                if 0 <= i - 2 < n:
                    turned(i - 2)
                if 0 <= i - 4 < n:
                    pv(i - 4)
                yield i - 4, pv_t.get(i - 4), e_t.get(i - 4)

        ALLC = slice(0, 256)

        class Unit:

            def __init__(self, k):
                wh, wl, self.tok, self.slot = take()
                self.plain = wl is None
                if not self.plain:
                    self.h, self.l = (w.rearrange("p (k c) -> p k c", k=k) for w in (wh, wl))
                else:
                    self.h = wh

            def pair(self, k, cols):
                return self.h[:, k, cols], self.l[:, k, cols]

            def used(self, m):
                before, st["used"] = st["used"], (self, m)
                if before:
                    u, m = before
                    if u.plain:
                        raw_free[u.slot] = [m]
                        raw_busy[u.slot] = False
                    else:
                        w_free[u.slot] = [m]
                        w_busy[u.slot] = False
                    prefetch()
                    prefetch()

        def tcols(t):
            return slice(t * 128, (t + 1) * 128)

        def by_tokens(n_slabs, cw, nu, kper, lhs, evac, out, after, of=range(8), skew=(), between=None):
            for n in range(n_slabs):
                bs = [bank(of), bank(of)]
                us = {}
                order = [(h, t) for h in range(nu) for t in range(2)]
                if n in skew:
                    order.sort(key=lambda ht: ht[1])
                for h, t in order:
                    if t == 0:
                        us[h] = Unit(kper)
                    elif n in skew and h == 0 and between:
                        between()
                    u = us[h]
                    m = mm3(banks[bs[t]][:, 0:cw], [lhs(h * kper + k, tcols(t)) for k in range(kper)],
                            [u.pair(k, slice(0, cw)) for k in range(kper)], h == 0, h == nu - 1,
                            u.tok, free[bs[t]] if h == 0 else None, each=lambda i: upon(after, t, h * kper + i))
                    if h == nu - 1:
                        e = evac(n, t, banks[bs[t]][:, 0:cw], m)
                        free[bs[t]] = [e]
                        out.append(e)
                    if t == 1:
                        u.used(m)
                        yield

        def by_features(n_units, kt, lhs, evac, out, after):
            for n in range(n_units):
                u = Unit(kt)
                c2 = u.h.shape[2] // 128
                for c in range(c2):
                    b = bank()
                    m = mm3(banks[b][:, 0:256], [u.pair(k, tcols(c)) for k in range(kt)],
                            [lhs(k, ALLC) for k in range(kt)], True, True, u.tok, free[b],
                            each=lambda i: [upon(after, t, i) for t in range(2)])
                    e = evac(c2 * n + c, banks[b][:, 0:256], m)
                    free[b] = [e]
                    out.append(e)
                u.used(m)
                yield

        def run(gen):
            for _ in gen:
                pass

        def add_to_x(n, t, ps, m):
            xv = x[:, t, n * 512:(n + 1) * 512]
            return tt(DVE_ON, xv, xv, ps, ALU.add, m)

        def add_and_norm(buf, after):
            norms = []

            def evac(n, t, ps, m):
                e = add_to_x(n, t, ps, m)
                if n:
                    if t == 0:
                        norms.append(Norm(buf))
                    norms[0].scale(t, e)
                return e

            run(by_tokens(2, 512, 4, 2, hT, evac, [], after, skew=(0, 1)))
            return norms[0]

        cosp = cosP.rearrange("p (t f) -> p t f", t=2)
        sinp = sinP.rearrange("p (t f) -> p t f", t=2)
        tab_half = [tab_s[:, :].rearrange("p (a n t) -> p a n t", a=2, n=16)[:, :, 8 * i:8 * i + 8, :] for i in range(2)]
        sc_l = ExitStack()
        mix = scoped(sc_l, "mix", 2048)[:, :].rearrange("p (t d) -> p t d", t=2)
        att = scoped(sc_l, "att", 3072)[:, :]
        headtmp = scoped(sc_l, "headtmp", 512)[:, :]
        for layer in range(DEPTH):
            sc_a = ExitStack()
            qkv = scoped(sc_a, f"qkv{layer}", 6144)[:, :].rearrange("p (t n) -> p t n", t=2)
            qkT = scoped(sc_a, f"qkT{layer}", 4096)[:, :].rearrange("p (k t) -> p k t", k=16)
            if layer == 0:
                prefetch()
                norm = Norm(mix)
                norm.scale(0, ld_x)
                norm.scale(1, ld_x)
                norm.turned(0, 1)
                for _ in range(5):
                    prefetch()
                opening()
                steps = state_constants()
                st["lo"] = ["pool"]
            second_half = (lambda norm=norm: norm.turned(1)) if layer else None
            ev = []
            qkv_banks = list(range(8))
            slabs = by_tokens(6, 512, 4, 2, hT,
                              lambda n, t, ps, m: copy(t, qkv[:, t, n * 512:(n + 1) * 512], ps, m), ev, norm.done, of=qkv_banks, skew=(0,), between=second_half)

            cols = [128 * j for j in range(4)] + [768 + 128 * j for j in range(4)] + [1536 + 128 * j for j in range(8)]

            def qk_turned(first, n, roped, toks):
                for j in range(first, first + n, 2):
                    b = bank((0, 1))
                    for s in range(2):
                        for t in range(2):
                            w = tr(banks[b][:, s * 256 + t * 128:s * 256 + t * 128 + 128],
                                   qkv[:, t, cols[j + s]:cols[j + s] + 128], roped, free[b])
                    e = copy(j // 2, qkT[:, j:j + 2, :], banks[b][:, :].rearrange("p (s t) -> p s t", s=2), w)
                    free[b] = [e]
                    toks.append(e)

            view = [qkv[:, :, 0:512].rearrange("p t (u d) -> p t u d", d=32),
                    qkv[:, :, 768:1280].rearrange("p t (u d) -> p t u d", d=64),
                    qkv[:, :, 1536:2560].rearrange("p t (u d) -> p t u d", d=64)]
            qA, qB, qC, vA, vB, vC = [[] for _ in range(6)]
            maps = []
            outs = {"A": (4, 7), "B": (4, 4), "C": (5, 7)}
            for t in range(2):
                nk = t + 1
                for u in range(8):
                    o = 32 * (u % 4)
                    maps.append((nk, qkT[o:o + 32, u // 4, tcols(t)], qkT[o:o + 32, 2 + u // 4, 0:128 * nk],
                                 lambda k, u=u: qkv[:, k, 512 + 64 * (u // 2):576 + 64 * (u // 2)],
                                 maskC[:, t, 0:128 * nk], 32 ** -0.5, (outs["A"][t], 64 * u), [qA, vA]))
            for t in range(2):
                nk = t + 1
                for h in range(4):
                    o = 64 * (h % 2)
                    maps.append((nk, qkT[o:o + 64, 4 + h // 2, tcols(t)], qkT[o:o + 64, 6 + h // 2, 0:128 * nk],
                                 lambda k, h=h: qkv[:, k, 1280 + 64 * h:1344 + 64 * h],
                                 maskC[:, t, 0:128 * nk], 0.125, (outs["B"][t], 256 * t + 64 * h), [qB, vB]))
            for t in range(2):
                nk = t + 1
                for h in range(8):
                    o = 64 * (h % 2)
                    maps.append((nk, qkT[o:o + 64, 8 + h // 2, tcols(t)], qkT[o:o + 64, 12 + h // 2, 0:128 * nk],
                                 lambda k, h=h: qkv[:, k, 2560 + 64 * h:2624 + 64 * h],
                                 maskD[:, t, 0:128 * nk], 0.125, (outs["C"][t], 64 * h), [qC, vC]))
            ta = headtmp[:, 0:256].rearrange("p (h d) -> p h d", h=4)
            tb = headtmp[:, 256:512].rearrange("p (h d) -> p h d", h=4)
            mix_tok = [[], []]

            def difference(t, pv, ex):
                r, rl, b = rden[:, 8 * t:8 * t + 8], rlam[t], outs["A"][t]
                d = DVE(lambda e: e.reciprocal(r, den[:, 8 * t:8 * t + 8]), ex)
                d = ts(DVE, rl, r[:, 1:8:2], lam[layer], None, ALU.mult, None, d, lam_tok)
                yield
                oA = banks[b][:, :].rearrange("p (h c d) -> p h c d", h=4, c=2)
                tt(DVE, ta, oA[:, :, 0, :], r[:, 0:8:2].unsqueeze(2).broadcast_to([128, 4, 64]), ALU.mult, pv, d)
                d = tt(DVE, tb, oA[:, :, 1, :], rl.unsqueeze(2).broadcast_to([128, 4, 64]), ALU.mult, d)
                free[b] = [d]
                yield
                d = tt(DVE, ta, ta, tb, ALU.subtract, d)
                d = tt(DVE, tb, ta, ta, ALU.mult, d)
                yield
                d = DVE(lambda e: e.tensor_reduce(rl, tb, AX, ALU.add), d)
                d = ts(DVE, rl, rl, 1.0 / 64, EPS, ALU.mult, ALU.add, d)
                p = tt(POOL, rl, rl, neghalf[:, 0:4], ALU.pow, d)
                yield
                d = tt(DVE, ta, ta, gd[layer].unsqueeze(1).broadcast_to([128, 4, 64]), ALU.mult, d)
                mix_tok[t].append(tt(DVE, mix[:, t, 0:256].rearrange("p (h d) -> p h d", h=4), ta,
                              rl.unsqueeze(2).broadcast_to([128, 4, 64]), ALU.mult, p, d))

            def normalised(i, n, t, b, c, col, pv, ex):
                r = rden[:, i:i + n]
                d = DVE(lambda e: e.reciprocal(r, den[:, i:i + n]), ex)
                d = tt(DVE, mix[:, t, col:col + 64 * n].rearrange("p (h d) -> p h d", h=n),
                       banks[b][:, c:c + 64 * n].rearrange("p (h d) -> p h d", h=n),
                       r.unsqueeze(2).broadcast_to([128, n, 64]), ALU.mult, pv, d)
                free[b] = [d]
                mix_tok[t].append(d)

            heads = attend(att, maps)

            def attend_on():
                i, pv, ex = next(heads)
                if i in (7, 15):
                    later.append(difference(i // 8, pv, ex))
                for g in later:
                    next(g, None)
                if i == 35:
                    mT.update(transposed(mix, 8, halves_evac(), mix_tok, ts=(0,), of=(0, 1)))
                if i == 23:
                    for t in range(2):
                        normalised(16 + 4 * t, 4, t, outs["B"][t], 256 * t, 256, pv, ex)
                if i in (31, 39):
                    t = (i - 31) // 8
                    normalised(24 + 8 * t, 8, t, outs["C"][t], 0, 512, pv, ex)

            later, mT = [], {}
            spare = [mix[:, t, c:c + 256] for t in range(2) for c in (256, 512, 768)]
            for k in range(24):
                next(slabs)
                for _ in range(3):
                    next(steps, None)
                if k == 3:
                    st["lo"] = ["dve", "dve", "pool"]
                    rA = rope(DVE, view[0], 4, cosp[:, :, 0:4], sinp[:, :, 0:4], spare[:4], ev[0:2], rope_tok)
                if k == 7:
                    vA += ev[2:4]
                    qk_turned(0, 4, rA, qA)
                    qkv_banks[:] = [5, 6]
                if k == 11:
                    vB += ev[4:6]
                    rB = rope(POOL, view[1], 8, cosp[:, :, 4:12], sinp[:, :, 4:12], spare[4:], ev[2:6], rope_tok)
                if k in (16, 18):
                    qk_turned(k - 12, 2, rB, qB)
                if k >= 20:
                    qk_turned(2 * k - 32, 2, rC, qC)
                if k == 19:
                    rC = rope(DVE, view[2], 8, cosp[:, :, 4:12], sinp[:, :, 4:12], spare[:4], ev[6:10])
                if k >= 8:
                    attend_on()
                    if k % 2:
                        attend_on()
            vC += ev[10:12]
            for _ in range(20):
                attend_on()
            k_tok = state[1]
            mT.update(transposed(mix, 8, halves_evac(), mix_tok, ts=(1,)))
            norm = add_and_norm(mix, mT)
            st["lo"] = ["dve", "dve", "pool"]
            sc_a.close()
            sc_f = ExitStack()
            yTh, yTl = [scoped(sc_f, f"y{c}{layer}", NTILE * 256, F32R)[:, :].rearrange("p (k t) -> p k t", k=NTILE)
                        for c in "hl"]
            cbuf = att
            cb = [[cbuf[:, 768 * s + 256 * j:768 * s + 256 * j + 256] for j in range(3)] for s in range(4)]
            h_tok = norm.turned(0, 1)
            if layer:
                act(tab_half[0], tab_half[0], ACTF.Sin, phase_tok, scale=SIN_SCALE)
            cv = sml(S_CONV + 176 * layer, 176).rearrange("p (n j) -> p n j", j=4)
            y_tok, y_mul = {}, {}

            def finish(f):
                a = act(yTh[:, f, :], cb[f % 4][0], ACTF.Copy, y_mul[f])
                y_tok[f] = tt(POOL, yTl[:, f, :], cb[f % 4][0], yTh[:, f, :].bitcast(F32), ALU.subtract, a)

            for f in range(NTILE):
                b = bank()
                for half in range(2):
                    u = Unit(8)
                    m = mm3(banks[b][:, 256 * half:256 * half + 256],
                            [u.pair(k, tcols(0)) for k in range(8)], [hT(k, ALLC) for k in range(8)],
                            True, True, u.tok, free[b], each=lambda i: [upon(h_tok, t, i) for t in range(2)])
                    u.used(m)
                c = cb[f % 4]
                for half in range(2):
                    col = cv[:, f + NTILE * half, :]
                    ps = banks[b][:, 256 * half:256 * half + 256]
                    a = act(c[half], ps, ACTF.Identity, m, y_tok.get(f - 4), scale=col[:, 2:3], bias=col[:, 3:4])
                    d = stt(c[half][:, 1:256], ps[:, 0:255], col[:, 1:2], c[half][:, 1:256], ALU.mult, ALU.add, a)
                    d = stt(c[half][:, 2:256], ps[:, 0:254], col[:, 0:1], c[half][:, 2:256], ALU.mult, ALU.add, d)
                    if half == 0:
                        sg = act(c[2], c[0], ACTF.Silu, d)
                free[b] = [d]
                y_mul[f] = tt(POOL, c[0], c[2], c[1], ALU.mult, sg, d)
                if f:
                    finish(f - 1)
            finish(NTILE - 1)
            st["lo"] = ["pool"]
            phase_tok = phase_tables(range(8 * layer, 8 * layer + 8, 2), state[0],
                                     cbuf[:, 0:512].rearrange("p (n t) -> p n t", n=2), list(y_tok.values()))
            ended = {}
            acc = [[bank() for _ in range(2)] for _ in range(2)]
            norms = []

            def x_done(t):
                for n in range(2):
                    b = acc[t][n]
                    e = add_to_x(n, t, banks[b][:, :], ended[t, n])
                    free[b] = [e]
                if layer:
                    if t == 0:
                        norms.append(Unit(1))
                    g = norms[0]
                    p = rms_rstd(x[:, t, :], mix[:, t, :], t, 1.0 / 1024, e)
                    e = stt(x[:, t, :], x[:, t, :], rstd[:, t:t + 1], g.h, ALU.mult, ALU.mult, p, g.tok)
                if t == 0:
                    norms.append(Norm(mix))
                norms[-1].scale(t, e)
                if layer and t:
                    g.used(e)

            order = [(f, t) for f in range(NTILE - 4) for t in range(2)]
            order += [(f, t) for t in range(2) for f in range(NTILE - 4, NTILE)]
            us = {}
            for f, t in order:
                if t == 0:
                    us[f] = Unit(1)
                for n in range(2):
                    b = acc[t][n]
                    m = mm3(banks[b][:, :], [(yTh[:, f, tcols(t)], yTl[:, f, tcols(t)])],
                            [us[f].pair(0, slice(n * 512, (n + 1) * 512))], f == 0, f == NTILE - 1,
                            y_tok[f], us[f].tok, free[b] if f == 0 else None)
                    ended[t, n] = m
                if t == 1:
                    us[f].used(m)
                if f == NTILE - 8:
                    st["lo"] = ["dve"]
                if f == NTILE - 1:
                    if t and layer == 0:
                        norms[-1].turned(0)
                    x_done(t)
                    st["lo"] = ["dve", "pool"]
            norm = norms[-1]
            sc_f.close()
        sc_l.close()

        sc_2 = ExitStack()

        def S2(name, n):
            return scoped(sc_2, name, n)[:, :]

        gates_s = S2("gates", 4096)
        gates = gates_s.rearrange("p (t n) -> p t n", t=2)
        proj = S2("proj", 2128).rearrange("p (t n) -> p t n", t=2)
        uT = S2("uT", 1024).rearrange("p (i t) -> p i t", i=4)
        qT2 = S2("qT2", 2304).rearrange("p (k t) -> p k t", k=9)
        ssb = S2("ssb", 2560)
        BT = S2("BT", 1024).rearrange("p (j i s) -> p j i s", j=2, i=4)
        cw = S2("cw", 1024)
        gy = S2("gy", 1024).rearrange("p (i t) -> p i t", i=4)
        ssv = S2("ssv", 1536)
        gt2 = ssb[:, 0:512]
        ld_b = q.dma("act", ssb[:, 0:1024], wsm_d[:, 0:1024], s_ssm, list(ended.values()))
        ld_c = q.dma("act", cw, wsm_d[:, 1024:2048], s_ssc, list(ended.values()))
        h_tok = norm.turned(0, 1)
        a_tab = act(tab_half[1], tab_half[1], ACTF.Sin, phase_tok, scale=SIN_SCALE)
        st["lo"] = ["dve", "pool"]
        Bb = [ssb[:, 512 * j:512 * j + 512].rearrange("p (n c) -> p n c", n=16) for j in range(2)]
        Br = [ssb[:, 1024 + 512 * j:1536 + 512 * j].rearrange("p (n c) -> p n c", n=16) for j in range(2)]
        tmpb = ssb[:, 2048:2560].rearrange("p (n c) -> p n c", n=16)
        Cr, nCi = cw[:, 0:512], cw[:, 512:1024]
        krb = kr.unsqueeze(2).broadcast_to([128, 16, 32])
        kib = ki.unsqueeze(2).broadcast_to([128, 16, 32])
        d = tt(DVE, Br[0], Bb[0], krb, ALU.mult, k_tok, ld_b)
        d = tt(DVE, tmpb, Bb[1], kib, ALU.mult, d)
        d = tt(DVE, Br[0], Br[0], tmpb, ALU.subtract, d)
        d = tt(DVE, Br[1], Bb[1], krb, ALU.mult, d)
        d = tt(DVE, tmpb, Bb[0], kib, ALU.mult, d)
        d = tt(DVE, Br[1], Br[1], tmpb, ALU.add, d)
        nc_tok = ts(DVE, nCi, nCi, -1.0, None, ALU.mult, None, ld_c, d)
        u_tok = []
        run(by_features(4, 8, hT, lambda c, ps, m: copy(c, uT[:, c, :], ps, m), u_tok, h_tok))
        bt_tok = []
        for j in range(2):
            b = bank()
            for i in range(4):
                w = tr(banks[b][:, i * 128:(i + 1) * 128], Br[j][:, 4 * i:4 * i + 4, :].rearrange("p n c -> p (n c)"),
                       d, free[b])
            e = copy(j, BT[:, j], banks[b][:, :].rearrange("p (i s) -> p i s", i=4), w)
            free[b] = [e]
            bt_tok.append(e)

        pr_tok, g_tok = [], []

        def projections():
            yield from by_tokens(2, 512, 4, 2, hT,
                                 lambda n, t, ps, m: act(proj[:, t, n * 512:(n + 1) * 512], ps, ACTF.Copy, m), pr_tok, h_tok, of=low)
            yield from by_tokens(1, 40, 1, 8, hT,
                                 lambda n, t, ps, m: act(proj[:, t, 1024:1064], ps, ACTF.Copy, m), pr_tok, h_tok, of=low)
            yield from by_tokens(4, 512, 4, 2, hT,
                                 lambda n, t, ps, m: act(gates[:, t, n * 512:(n + 1) * 512], ps, ACTF.Sigmoid, m), g_tok, h_tok, of=low)

        st["lo"] = ["dve"]
        low, high = (0, 1, 2, 3), (4, 5, 6, 7)
        fill = projections()
        prod = [ssb[:, 1024 * j:1024 * j + 1024].rearrange("p (a b t) -> p a b t", a=2, b=2) for j in range(2)]
        w_in, z, *states = [a.rearrange("p (a t) -> p a t", a=2) for a in
                            [ssb[:, 2048:2560]] + [ssv[:, 512 * j:512 * j + 512] for j in range(3)]]
        dsk = sml(S_DSK, 4)
        bu_t = {}
        ym = {}
        gy_tok = []

        def bu(n):
            b = 4 + n % 2
            o = 32 * (n % 4)
            for j in range(2):
                m = mm(banks[b][:, 256 * j:256 * j + 256], [(BT[o:o + 32, j, n // 4, :], uT[o:o + 32, n // 4, :])],
                       bt_tok, u_tok, free[b])
            bu_t[n] = (b, m)

        def ssm_out(n):
            yb = 6 + (n // 4) % 2
            o = 32 * (n % 4)
            cc = slice(32 * n, 32 * n + 32)
            xs_ = states[n % 2]
            for j, l in enumerate((Cr, nCi)):
                ym[n] = PE(lambda e, l=l, j=j, o=o, yb=yb, cc=cc, xs_=xs_: e.matmul(
                    banks[yb][o:o + 32, 0:256], l[:, cc], xs_[:, j, :], start=j == 0, stop=j == 1, tile_position=(0, o)),
                    st_tk[n], nc_tok, free[yb] if n % 4 == 0 else None)
            if n % 4 == 3:
                i = n // 4
                d = stt(gy[:, i, :], uT[:, i, :], dsk[:, i:i + 1], banks[yb][:, 0:256], ALU.mult, ALU.add, ym[n])
                free[yb] = [d]
                if i == 3:
                    gy_tok.append(act(gy, gy, ACTF.Gelu_apprx_tanh, d))

        bu(0)
        st_tk, q_tk, z_tk = {}, {}, {}
        for n in range(16):
            if n + 1 < 16:
                bu(n + 1)
            b, m = bu_t[n]
            cs = tab_s[:, :].rearrange("p (a n t) -> p a n t", a=2, n=16)[:, :, n, :]
            csb = cs.unsqueeze(1).broadcast_to([128, 2, 2, 256])
            bv = banks[b][:, :].rearrange("p (a t) -> p a t", a=2)
            d = tt(DVE, prod[0], bv.unsqueeze(2).broadcast_to([128, 2, 2, 256]), csb, ALU.mult, m, a_tab, bt_tok)
            free[b] = [d]
            w0 = tt(DVE_ON, w_in[:, 0, :], prod[0][:, 0, 0, :], prod[0][:, 1, 1, :], ALU.add, d)
            w1 = tt(DVE_ON, w_in[:, 1, :], prod[0][:, 1, 0, :], prod[0][:, 0, 1, :], ALU.subtract, d)
            rb_ = rr[:, n:n + 1].broadcast_to([128, 256])
            for j in range(2):
                d = DVE_ON(lambda e, j=j, rb_=rb_: e.tensor_tensor_scan(z[:, j, :], rb_, w_in[:, j, :], 0.0, ALU.mult, ALU.add),
                           (w0, w1)[j], q_tk.get(n - 1))
            q_tk[n] = tt(POOL, prod[1], z.unsqueeze(2).broadcast_to([128, 2, 2, 256]), csb, ALU.mult, d, bt_tok)
            xs_ = states[n % 2]
            tt(POOL, xs_[:, 0, :], prod[1][:, 0, 0, :], prod[1][:, 1, 1, :], ALU.subtract, ym.get(n - 2))
            st_tk[n] = tt(POOL_ON, xs_[:, 1, :], prod[1][:, 0, 1, :], prod[1][:, 1, 0, :], ALU.add, q_tk[n], ym.get(n - 2))
            if n:
                ssm_out(n - 1)
            next(fill, None)
        ssm_out(15)
        d = st_tk[15]
        st["lo"] = ["pool"]
        att2 = tab_s[:, 0:3072]
        kk_s, ki_s = tab_s[:, 3072:3584], tab_s[:, 3584:3840]
        cosA = con(K_CA, 64).rearrange("p (t f) -> p t f", t=2)
        sinA = con(K_SA, 64).rearrange("p (t f) -> p t f", t=2)
        cosI = con(K_CI, 32).rearrange("p (t f) -> p t f", t=2)
        sinI = con(K_SI, 32).rearrange("p (t f) -> p t f", t=2)
        rQ = rope(DVE, proj[:, :, 0:640].rearrange("p t (u d) -> p t u d", d=64), 32, cosA, sinA, [tab_s[:, 0:2560]], pr_tok, d)
        rI = rope(POOL, proj[:, :, 768:1056].rearrange("p t (u d) -> p t u d", d=32), 16, cosI, sinI,
                  [tab_s[:, 3840:4992]], pr_tok, d)
        kk2 = kk_s.rearrange("p (t h r d) -> p t h r d", t=2, h=2, r=2)
        ki4 = ki_s.rearrange("p (t r d) -> p t r d", t=2, r=4)
        dup = []
        for t in range(2):
            dup.append(DVE(lambda e, t=t: e.tensor_copy(
                ki4[:, t], proj[:, t, 1024:1056].unsqueeze(1).broadcast_to([128, 4, 32])), rI))
        for t in range(2):
            kv = proj[:, t, 512:640].rearrange("p (h d) -> p h d", h=2)
            for r in range(2):
                dup.append(DVE(lambda e, t=t, r=r, kv=kv: e.tensor_copy(kk2[:, t, :, r, :], kv), rQ))
        srcs = [proj[:, :, 128 * j:128 * j + 128] for j in range(4)]
        srcs += [kk_s.rearrange("p (t c) -> p t c", t=2)[:, :, 128 * j:128 * j + 128] for j in range(2)]
        srcs += [proj[:, :, 768 + 128 * j:896 + 128 * j] for j in range(2)]
        srcs += [ki_s.rearrange("p (t c) -> p t c", t=2)]
        q_tok = []
        for _ in range(4):
            next(fill)
        for j in (8, 6, 0, 2, 4):
            b = bank(high)
            ns = min(2, 9 - j)
            for s in range(ns):
                for t in range(2):
                    w = tr(banks[b][:, s * 256 + t * 128:s * 256 + t * 128 + 128], srcs[j + s][:, t, :],
                           rQ, rI, dup, free[b])
            e = act(qT2[:, j:j + ns, :], banks[b][:, 0:256 * ns].rearrange("p (s t) -> p s t", s=ns), ACTF.Copy, w)
            free[b] = [e]
            q_tok.append(e)
        rel = [tab_s[:, 4992 + 256 * j:5248 + 256 * j] for j in range(4)]
        sc = [tab_s[:, 6016 + 256 * t:6272 + 256 * t] for t in range(2)]
        mask2 = [tab_s[:, 6528 + 256 * t:6784 + 256 * t] for t in range(2)]
        m8 = stat(8)
        rel_free = [[] for _ in range(4)]
        sel_tok = []

        def chosen(t):
            nk = t + 1
            d = None
            s_ = sc[t][:, 0:128 * nk]
            for h in range(8):
                b = bank(high)
                o = 32 * (h % 4)
                m = mm(banks[b][:, 0:128 * nk],
                       [(qT2[o:o + 32, 6 + h // 4, tcols(t)], qT2[o:o + 32, 8, 0:128 * nk])], q_tok, free[b])
                r = rel[h % 4][:, 0:128 * nk]
                a = act(r, banks[b][:, 0:128 * nk], ACTF.Relu, m, rel_free[h % 4])
                free[b] = [a]
                wcol = proj[:, t, 1056 + h:1057 + h]
                if h == 0:
                    d = ts(DVE, s_, r, wcol, None, ALU.mult, None, a, pr_tok)
                else:
                    d = stt(s_, r, wcol, s_, ALU.mult, ALU.add, a, d)
                rel_free[h % 4] = [d]
            d = stt(s_, s_, 0.0625, maskC[:, t, 0:128 * nk], ALU.mult, ALU.add, d)
            for r in range(8):
                d = DVE(lambda e, s_=s_: e.max(m8, s_), d)
                d = DVE(lambda e, s_=s_: e.match_replace(s_, m8, s_, TAKEN), d)
            m_ = mask2[t][:, 0:128 * nk]
            d = ts(DVE, m_, s_, -2e38, NEG, ALU.is_gt, ALU.mult, d)
            d = tt(DVE, m_, m_, maskC[:, t, 0:128 * nk], ALU.add, d)
            sel_tok.append(d)

        chosen(0)
        run(fill)
        st["lo"] = ["pool"]
        gyl = []
        for i in range(4):
            gyl.append(halves(hTh[:, i, :], hTl[:, i, :], gy[:, i, :], gy_tok, g_tok))
        ys_tok = []

        def glu(c, ps, m):
            a = act(ps, ps, ACTF.Sigmoid, m)
            tmp = gt2[:, 256 * (c % 2):256 * (c % 2) + 256]
            d = tt(DVE, tmp, gy[:, c, :], ps, ALU.mult, a, ys_tok[-2:])
            ys_tok.append(halves(hTh[:, 4 + c, :], hTl[:, 4 + c, :], tmp, d))
            return d

        run(by_features(2, 4, hT, glu, [], gyl))
        chosen(1)
        me_tok = []

        def gated(which):
            def evac(n, t, ps, m):
                sl = gates[:, t, which * 1024 + n * 512:which * 1024 + (n + 1) * 512]
                d = tt(DVE, sl, ps, sl, ALU.mult, m, g_tok)
                if which:
                    s0 = gates[:, t, n * 512:(n + 1) * 512]
                    d2 = tt(DVE, s0, s0, sl, ALU.add, d)
                    me_tok.append(d2)
                return d
            return evac

        run(by_tokens(2, 512, 2, 2, lambda k, c: hT(4 + k, c), gated(0), [], ys_tok))
        ya = tab_s[:, 7040:8064].rearrange("p (t n) -> p t n", t=2)
        maps = []
        for t in range(2):
            nk = t + 1
            for h in range(8):
                o = 64 * (h % 2)
                maps.append((nk, qT2[o:o + 64, h // 2, tcols(t)], qT2[o:o + 64, 4 + h // 4, 0:128 * nk],
                             lambda k, h=h: proj[:, k, 640 + 64 * (h // 4):704 + 64 * (h // 4)],
                             mask2[t][:, 0:128 * nk], 0.125, (4 + t, 64 * h), [q_tok, sel_tok[t], pr_tok]))
        ya_tok = []
        for i, pv, ex in attend(att2, maps, q_tok, sel_tok):
            if i in (7, 15):
                t = i // 8
                r = rden[:, 8 * t:8 * t + 8]
                d = DVE(lambda e, r=r, t=t: e.reciprocal(r, den[:, 8 * t:8 * t + 8]), ex)
                d = tt(DVE, ya[:, t, :].rearrange("p (h d) -> p h d", h=8), banks[4 + t][:, :].rearrange("p (h d) -> p h d", h=8),
                       r.unsqueeze(2).broadcast_to([128, 8, 64]), ALU.mult, d, pv)
                free[4 + t] = [d]
                ya_tok.append(d)
        ya_h = transposed(ya, 4, halves_evac(), ya_tok)
        run(by_tokens(2, 512, 2, 2, hT, gated(1), [], ya_h))
        mT = transposed(gates, 8, halves_evac(), [me_tok, me_tok])
        norm = add_and_norm(gates[:, :, 1024:2048], mT)
        h_tok = norm.turned(0, 1)
        spill = q.dma("act", spill_d, xs[:, :], s_spill, [h_tok])
        sc_2.close()
        early.close()
        sc_p = ExitStack()
        H_s = scoped(sc_p, "H", 32768)
        ach = [scoped(sc_p, f"ach{j}", 256, F32R)[:, :] for j in range(2)]
        acl = [scoped(sc_p, f"acl{j}", 256, F32R)[:, :] for j in range(2)]
        H = H_s[:, :].rearrange("p (j t) -> p j t", j=128)
        R_AT = 16800
        assert R_AT >= K_W - 128 + S_W + 8192 + 6144
        at = [R_AT]

        def RT(n):
            at[0] += n
            assert at[0] <= 32768
            return H_s[:, at[0] - n:at[0]]

        pqT = RT(4096).rearrange("p (n t) -> p n t", n=16)
        pq_tok = []
        run(by_features(16, 8, hT, lambda c, ps, m: copy(c, pqT[:, c, :], ps, m), pq_tok, h_tok))
        us = [Unit(8), Unit(8)]
        S = RT(4096).rearrange("p (t n c) -> p t n c", t=2, n=16)
        s_tok = []
        for t in range(2):
            for n in range(0, 16, 4):
                b = bank()
                for j in range(4):
                    m = mm(banks[b][:, j * 128:(j + 1) * 128],
                           [(pqT[:, n + j, tcols(t)], us[n // 8].h.rearrange("p (n c) -> p n c", n=8)[:, (n + j) % 8, :])], pq_tok, us[n // 8].tok, free[b])
                e = copy(n // 4, S[:, t, n:n + 4, :], banks[b][:, :].rearrange("p (n c) -> p n c", n=4), m)
                free[b] = [e]
                s_tok.append(e)
        st["lo"] = ["pool", "dve", "pool"]
        for u in us:
            u.used(m)
        v16 = RT(256).rearrange("p (n k) -> p n k", n=16)
        i16 = RT(256).bitcast(U32).rearrange("p (n k) -> p n k", n=16)
        if16 = RT(256).rearrange("p (n k) -> p n k", n=16)
        tops = RT(128).rearrange("p (h k) -> p h k", h=8)
        pos = RT(128).bitcast(U32).rearrange("p (h k) -> p h k", h=8)
        pa, pb = RT(128), RT(128)
        pau, pbu = RT(128).bitcast(U32), RT(128).bitcast(U32)
        gt = RT(128).rearrange("p (h k) -> p h k", h=8)
        zs = RT(8)
        sel = RT(256).rearrange("p (a n) -> p a n", a=2)
        cand = RT(2048).rearrange("p (h c) -> p h c", h=8)
        oh = RT(2048).rearrange("p (h k j) -> p h k j", h=8, k=16)
        selG = xs[:, 0:384].bitcast(BF16).rearrange("p (s t) -> p s t", s=3)
        sel1, sel2 = [xs[:, 384 + 128 * j:512 + 128 * j].bitcast(BF16) for j in range(2)]
        sT_tok = []

        def routing(t, prev, done):
            d = None
            for n in range(16):
                sv = S[:, t, n, :]
                d = DVE(lambda e, n=n, sv=sv: e.max(v16[:, n, 0:8], sv), s_tok, prev)
                d = DVE(lambda e, n=n, sv=sv: e.max_index(i16[:, n, 0:8], v16[:, n, 0:8], sv), d)
                d = DVE(lambda e, n=n, sv=sv: e.match_replace(sv, v16[:, n, 0:8], sv, TAKEN), d)
                d = DVE(lambda e, n=n, sv=sv: e.max(v16[:, n, 8:16], sv), d)
                d = DVE(lambda e, n=n, sv=sv: e.max_index(i16[:, n, 8:16], v16[:, n, 8:16], sv), d)
                yield
            vv = v16.rearrange("p (h c) k -> p h c k", c=2)
            d = tt(DVE, cand.rearrange("p h (i j) -> p h i j", i=16),
                   vv[:, :, 0, :].unsqueeze(3).broadcast_to([128, 8, 16, 16]),
                   vv[:, :, 1, :].unsqueeze(2).broadcast_to([128, 8, 16, 16]), ALU.add, d)
            for h in range(8):
                cv_ = cand[:, h, :]
                d = DVE(lambda e, h=h, cv_=cv_: e.max(tops[:, h, 0:8], cv_), d)
                d = DVE(lambda e, h=h, cv_=cv_: e.max_index(pos[:, h, 0:8], tops[:, h, 0:8], cv_), d)
                d = DVE(lambda e, h=h, cv_=cv_: e.match_replace(cv_, tops[:, h, 0:8], cv_, TAKEN), d)
                d = DVE(lambda e, h=h, cv_=cv_: e.max(tops[:, h, 8:16], cv_), d)
                d = DVE(lambda e, h=h, cv_=cv_: e.max_index(pos[:, h, 8:16], tops[:, h, 8:16], cv_), d)
                yield
            d = tt(DVE, gt, tops, tops[:, :, 0:1].broadcast_to([128, 8, 16]), ALU.subtract, d)
            a = act(gt, gt, ACTF.Exp, d)
            posf_ = pos.rearrange("p h k -> p (h k)")
            d = ts(DVE, pau, posf_, 4, None, ALU.logical_shift_right, None, d)
            d = ts(DVE, pbu, posf_, 15, None, ALU.bitwise_and, None, d)
            d = DVE(lambda e: e.tensor_copy(pa, pau), d)
            d = DVE(lambda e: e.tensor_copy(pb, pbu), d)
            d = DVE(lambda e: e.tensor_copy(if16, i16), d)
            yield
            ifv = if16.rearrange("p (h c) k -> p h c k", c=2)
            for c, pp in ((0, pa), (1, pb)):
                d = tt(DVE, oh, pp.rearrange("p (h k) -> p h k", h=8).unsqueeze(3).broadcast_to([128, 8, 16, 16]),
                       iot.unsqueeze(1).unsqueeze(1).broadcast_to([128, 8, 16, 16]), ALU.is_equal, d)
                yield
                d = tt(DVE, oh, oh, ifv[:, :, c, :].unsqueeze(2).broadcast_to([128, 8, 16, 16]), ALU.mult, d)
                d = DVE(lambda e, c=c: e.tensor_reduce(sel[:, c, :].rearrange("p (h k) -> p h k", h=8), oh, AX, ALU.add), d)
                yield
            d = DVE(lambda e: e.tensor_reduce(zs, gt, AX, ALU.add), a, d)
            d = DVE(lambda e: e.reciprocal(zs, zs), d)
            done.append(tt(DVE, gt, gt, zs.unsqueeze(2).broadcast_to([128, 8, 16]), ALU.mult, d))

        def sel_turned(t, d):
            b = 2 + t
            for j, src in enumerate((gt.rearrange("p h k -> p (h k)"), sel[:, 0, :], sel[:, 1, :])):
                w = tr(banks[b][:, j * 128:(j + 1) * 128], src, d, free[b])
            e = DVE(lambda e, t=t, b=b: e.tensor_copy(sel1[:, tcols(t)], banks[b][:, 128:256]), w, spill)
            e = DVE(lambda e, t=t, b=b: e.tensor_copy(sel2[:, tcols(t)], banks[b][:, 256:384]), e)
            rest = banks[b][:, 0:128]
            for j in range(3):
                part = selG[:, j, tcols(t)]
                e = DVE(lambda e, part=part, rest=rest: e.tensor_copy(part, rest), e)
                if j < 2:
                    e = tt(DVE, rest, rest, part, ALU.subtract, e)
            free[b] = [e]
            sT_tok.append(e)
            return e

        h_tk = {}

        def hidden(j):
            u = Unit(8)
            b = j % 2
            m = mm3(banks[b][:, 0:256], [u.pair(k, slice(0, 128)) for k in range(8)],
                    [hT(k, ALLC) for k in range(8)], True, True, u.tok, h_tok, free[b])
            u.used(m)
            h_tk[j] = act(H[:, j, :], banks[b][:, 0:256], ACTF.Gelu_apprx_tanh, m, sT_tok if j * 256 + 256 > R_AT else None,
                          s_tok)
            free[b] = [h_tk[j]]

        ohA = [xs[:, 640 + 256 * j:896 + 256 * j].bitcast(BF16).rearrange("p (t n) -> p t n", t=4) for j in range(2)]
        ohB = xs[:, 1152:1280].bitcast(BF16).rearrange("p (t n) -> p t n", t=4)
        ohG = [xs[:, 1280 + 384 * j:1664 + 384 * j].bitcast(BF16).rearrange("p (s t n) -> p s t n", s=3, t=4) for j in range(2)]
        g_mm = []
        oh_tk = {}
        G_tok = {0: [], 1: []}

        def one_hot(i):
            half, g = i // 64, i % 64
            ts4 = slice(4 * g, 4 * g + 4)
            prev = g_mm[i - 2] if i >= 2 else None
            dA = tt(DVE_ON, ohA[i % 2], iob.unsqueeze(1).broadcast_to([128, 4, 128]),
                    sel1[:, ts4].unsqueeze(2).broadcast_to([128, 4, 128]), ALU.is_equal, sT_tok, prev)
            dB = tt(DVE_ON, ohB, iob[:, 64 * half:64 * half + 64].unsqueeze(1).broadcast_to([128, 4, 64]),
                    sel2[:, ts4].unsqueeze(2).broadcast_to([128, 4, 64]), ALU.is_equal, sT_tok, oh_tk.get(i - 1))
            dB = tt(POOL, ohG[i % 2], ohB.unsqueeze(1).broadcast_to([128, 3, 4, 64]),
                    selG[:, :, ts4].unsqueeze(3).broadcast_to([128, 3, 4, 64]), ALU.mult, dB, prev)
            oh_tk[i] = [dA, dB]

        def gates_of(half, g):
            i = 64 * half + g
            if i == 0:
                one_hot(0)
                one_hot(1)
            b = 2 + i % 2
            for j in range(4):
                m = mm(banks[b][:, j * 64:(j + 1) * 64], [(ohA[i % 2][:, j, :], ohG[i % 2][:, s_, j, :]) for s_ in range(3)],
                       oh_tk[i], free[b])
            g_mm.append(m)
            hv = H[:, 64 * half:64 * half + 64, 4 * g:4 * g + 4]
            e = tt(DVE_ON, hv, hv, banks[b][:, 0:256].rearrange("p (t j) -> p j t", t=4), ALU.mult, m, h_tk[64 * half + 63])
            free[b] = [e]
            G_tok[half] = [e]
            if i < 126:
                one_hot(i + 2)

        def split_gated(j):
            a = act(ach[j % 2], H[:, j, :], ACTF.Copy, G_tok[j // 64], v_mm.get(j - 2))
            ac_tk[j] = tt(DVE_ON, acl[j % 2], H[:, j, :], ach[j % 2].bitcast(F32), ALU.subtract, a)

        v_mm, ac_tk = {}, {}

        def down(js):
            us = [Unit(1) for _ in js]
            for t in range(2):
                for i, j in enumerate(js):
                    for n in range(2):
                        b = 4 + 2 * t + n
                        v_mm[j] = v_end[t] = mm3(banks[b][:, :], [(ach[j % 2][:, tcols(t)], acl[j % 2][:, tcols(t)])],
                                                 [us[i].pair(0, slice(n * 512, (n + 1) * 512))], j == 0, j == 127,
                                                 ac_tk[j], us[i].tok, free[b] if j == 0 else None)
                    if t:
                        us[i].used(v_mm[j])

        v_end = {}
        picked = [[], []]
        steps = routing(0, h_tok, picked[0])
        for j in range(128):
            if j == 31:
                run(steps)
                steps = routing(1, sel_turned(0, picked[0]), picked[1])
            if j == 63:
                st["lo"] = ["dve", "pool"]
                run(steps)
                sel_turned(1, picked[1])
            next(steps, None)
            hidden(j)
            if j >= 65:
                gates_of(0, j - 65)
        gates_of(0, 63)
        split_gated(0)
        for j in range(128):
            if j < 64:
                gates_of(1, j)
            if j + 1 < 128:
                split_gated(j + 1)
            if j < 126:
                down([j])
        down([126, 127])
        back = q.dma("act", xs[:, :], spill_d, s_back, [spill, G_tok[1]])
        u = Unit(1)
        done = []
        for t in range(2):
            for n in range(2):
                xv = x[:, t, n * 512:(n + 1) * 512]
                e = tt(DVE, xv, xv, banks[4 + 2 * t + n][:, :], ALU.add, v_end[t], back)
            p = rms_rstd(x[:, t, :], H_s[:, 1024 * t:1024 * t + 1024], t, 1.0 / 1024, e)
            d = stt(x[:, t, :], x[:, t, :], rstd[:, t:t + 1], u.h, ALU.mult, ALU.mult, p, u.tok)
            done.append(q.dma("sp", out_d[tcols(t), :], x[:, t, :], s_out, [d]))
        fin_tok = done[-1]
        sc_p.close()

        q.number(sems)
        block = ctx.enter_context(nc.Block())

        @block.sync
        def _(eng):
            q.emit("sp", eng)
            eng.wait_ge(s_out, fin_tok.val)

        @block.scalar
        def _(eng):
            q.emit("act", eng)

        @block.vector
        def _(eng):
            q.emit("dve", eng)

        @block.tensor
        def _(eng):
            q.emit("pe", eng)

        @block.gpsimd
        def _(eng):
            q.emit("pool", eng)


def constants():
    c = np.zeros((128, K_W), np.float32)
    c[:, K_ID:K_ID + 128] = np.eye(128, dtype=np.float32)
    c[:, K_IOTA:K_IOTA + 128] = np.arange(128)
    p = np.arange(128)
    k = np.arange(256)
    for t in range(2):
        qp = (t * 128 + p)[:, None]
        causal = k[None, :] <= qp
        c[:, K_MC + 256 * t:K_MC + 256 * t + 256] = np.where(causal, 0.0, NEG)
        dist = qp - k[None, :]
        count = (causal & (dist <= 128)) * 1 + (causal & (dist % 4 == 0)) * 1 + (causal & (dist % 16 == 0)) * 1
        c[:, K_MD + 256 * t:K_MD + 256 * t + 256] = np.where(count > 0, 8.0 * np.log(np.maximum(count, 1)), NEG)
        for dim, kc, ks in ((64, K_CA, K_SA), (32, K_CI, K_SI)):
            inv = np.float32(10000.0) ** (-np.arange(0, dim, 2, dtype=np.float32) / np.float32(dim))
            a = (np.float32(1.0) * qp.astype(np.float32)) * inv.astype(np.float32)[None, :]
            n = dim // 2
            c[:, kc + n * t:kc + n * t + n] = np.cos(a.astype(np.float64))
            c[:, ks + n * t:ks + n * t + n] = np.sin(a.astype(np.float64))
    for rot, o in ((8, 0), (16, 4)):
        h = rot // 2
        c[:, K_INV + o:K_INV + o + h] = np.power(np.float32(500000.0), -np.arange(h, dtype=np.float32) * 2.0 / rot)
    c[:, K_T:K_T + 256] = k
    return c


def slabs(w, width):
    d, n = w.shape
    return w.reshape(d // 128, 128, n // width, width).transpose(2, 1, 0, 3).reshape(n // width, 128, -1)


def feat(v):
    return v.reshape(-1, 128).T


def layout(i):
    a = {}
    x = np.asarray(i["x"])
    a["x"] = x[0].reshape(2, 128, 1024).transpose(1, 0, 2)
    a["pos"] = np.asarray(i["positions"])[0].reshape(2, 128).T
    a["consts"] = constants()
    s = np.zeros((128, S_W), np.float32)
    for l in range(DEPTH):
        cv = np.stack([feat(np.asarray(i["conv_w"][l][j])) for j in range(3)] + [feat(np.asarray(i["conv_b"][l]))], axis=2)
        s[:, S_CONV + 176 * l:S_CONV + 176 * l + 176] = cv.reshape(128, 176)
        for j, n in enumerate(("lambda_q1", "lambda_k1", "lambda_q2", "lambda_k2")):
            s[:, S_LAM + 128 * l + 32 * j:S_LAM + 128 * l + 32 * j + 32] = np.asarray(i[n])[l]
        s[:, S_GD + 64 * l:S_GD + 64 * l + 64] = np.asarray(i["g_diff"])[l]
    s[:, S_DSK:S_DSK + 4] = feat(np.asarray(i["d_skip_2"])[0])
    s[:, S_LDT:S_LDT + 16] = np.repeat(np.asarray(i["log_dt_2"])[0].reshape(16, 2), 64, axis=1).T
    s[:, S_ARE:S_ARE + 16] = np.asarray(i["a_re_2"])[0].reshape(16, 128).T
    s[:, S_AIM:S_AIM + 16] = np.asarray(i["a_im_2"])[0].reshape(16, 128).T
    a["smalls"] = s
    w_in = np.asarray(i["w_in"])
    a["win"] = np.stack([slabs(w_in[l], 512) for l in range(DEPTH)])
    a["wout"] = np.stack([slabs(np.asarray(i["w_out"])[l], 512) for l in range(DEPTH)])
    up = np.asarray(i["w_up"]).reshape(DEPTH, 8, 128, 2, NTILE, 128)
    a["wup"] = up.transpose(0, 4, 3, 2, 1, 5).reshape(DEPTH, 2 * NTILE, 128, 1024)
    a["wdown"] = np.asarray(i["w_down"]).reshape(DEPTH, NTILE, 128, 1024)
    a["rows"] = np.stack([np.broadcast_to(np.asarray(g), (128, 1024)) for g in (
        i["g_mix"][0], i["g_mix"][1], i["g_ffn"][0], i["g_ffn"][1], i["g_final"], i["norm1_g_2"][0], i["norm2_g_2"][0], i["norm_f_g_2"])])
    w2 = np.asarray(i["w_in_2"])[0]
    a["wu"] = slabs(w2[:, 0:512], 128)
    a["wqkv"] = slabs(w2[:, 512:1536], 512)
    a["wga"] = slabs(w2[:, 1576:3624], 512)
    a["wqk"] = slabs(w2[:, 1536:1576], 40)[0]
    sw = np.zeros((4, 16, 2, 64, 2, 16), np.float32)
    for j, n in enumerate(("b_re_2", "b_im_2")):
        b = np.asarray(i[n])[0].reshape(16, 2, 64, 16)
        for g in range(2):
            sw[j, :, g, :, g, :] = b[:, g]
    for j, n in enumerate(("c_re_2", "c_im_2")):
        c = np.asarray(i[n])[0].reshape(16, 2, 16, 64).transpose(0, 1, 3, 2)
        for g in range(2):
            sw[2 + j, :, g, :, g, :] = c[:, g]
    a["wsm"] = sw.reshape(4, 16, 128, 32).transpose(2, 0, 1, 3).reshape(128, 2048)
    a["wglu"] = slabs(np.asarray(i["w_glu_2"])[0], 256)
    a["wsu"] = slabs(np.asarray(i["w_ssm_up_2"])[0], 512)
    a["wau"] = slabs(np.asarray(i["w_attn_up_2"])[0], 512)
    a["wout2"] = slabs(np.asarray(i["w_out_2"])[0], 512)
    a["wpq"] = slabs(np.asarray(i["peer_wq_2"])[0], 128)
    keys = np.stack([np.asarray(i["peer_k1_2"])[0], np.asarray(i["peer_k2_2"])[0]], axis=1)
    a["keys"] = keys.reshape(16, 128, 128).transpose(2, 0, 1).reshape(128, 2048)
    u = np.asarray(i["peer_u_2"])[0].reshape(128, 128, 8, 128)
    a["ut"] = u.transpose(1, 3, 2, 0).reshape(128, 128, 1024)
    v = np.asarray(i["peer_v_2"])[0].reshape(128, 128, 1024)
    a["vt"] = v.transpose(1, 0, 2)
    return a


_ORDER = ["x", "pos", "consts", "smalls", "win", "wout", "wup", "wdown", "rows", "wu", "wqkv", "wqk", "wga", "wsm", "wglu", "wsu",
          "wau", "wout2", "wpq", "keys", "ut", "vt"]


def kernel(**inputs):
    import concourse.bacc as _bacc
    from concourse.bass_utils import run_bass_kernel_spmd as _run

    nc = _bacc.Bacc("TRN2", target_bir_lowering=False, num_devices=1)
    made = layout(inputs)
    arrays, args = {}, []
    for name in _ORDER:
        a = np.ascontiguousarray(made[name])
        arrays[f"in_{name}_dram"] = a
        args.append(nc.dram_tensor(f"in_{name}_dram", a.shape, mybir.dt.from_np(a.dtype), kind="ExternalInput").ap())
    out = nc.dram_tensor("out_0_dram", (256, 1024), F32, kind="ExternalOutput").ap()
    spill = nc.dram_tensor("spill_dram", (128, 2048), F32, kind="Internal").ap()
    program(nc, *args, out, spill)
    r = _run(nc, [arrays], core_ids=[0])
    return r.results[0]["out_0_dram"].reshape(1, 256, 1024)
```
